# Optimizing a Trainium2 kernel written in Bass

```python
import jax
import jax.numpy as jnp
from jax import lax
import numpy as np
import math
import jax, jax.numpy as jnp

D_MODEL = 1024
BATCH = 1
SEQ = 512
DEPTH = 1

GRID_W = 64
MEM_LEN = 256
N_BRANCHES = 3
RET_HEADS = 4
RET_QK_DIM = 128
RET_V_DIM = 256
RET_CHUNK = 128
ROPE_BASE = 10000.0
NA_HEADS = 8
NA_HEAD_DIM = 64
NA_ROWS = 8
NA_COLS = 16
XA_HEADS = 4
XA_HEAD_DIM = 128
MOE_GROUPS = 4
MOE_EXPERTS_PER_GROUP = 4
MOE_TOP_K = 2
MOE_D_FF = 512
RMS_EPS = 1e-6
GN_EPS = 1e-5

RET_QK_WIDTH = RET_HEADS * RET_QK_DIM
RET_V_WIDTH = RET_HEADS * RET_V_DIM
NA_WIDTH = NA_HEADS * NA_HEAD_DIM
XA_WIDTH = XA_HEADS * XA_HEAD_DIM
IN_SPLITS = (RET_QK_WIDTH, RET_QK_WIDTH, RET_V_WIDTH, RET_V_WIDTH, NA_WIDTH, NA_WIDTH, NA_WIDTH, XA_WIDTH, N_BRANCHES * D_MODEL)
IN_WIDTH = 2 * RET_QK_WIDTH + 2 * RET_V_WIDTH + 3 * NA_WIDTH + XA_WIDTH + N_BRANCHES * D_MODEL


def _rmsnorm(x, g):
    xf = x.astype(jnp.float32)
    y = xf * lax.rsqrt(jnp.mean(xf * xf, axis=-1, keepdims=True) + RMS_EPS)
    return (y * g.astype(jnp.float32)).astype(x.dtype)

def _rope(a):
    seq, dh = a.shape[1], a.shape[-1]
    half = dh // 2
    inv_freq = ROPE_BASE ** (-jnp.arange(half, dtype=jnp.float32) / half)
    ang = jnp.arange(seq, dtype=jnp.float32)[:, None] * inv_freq[None, :]
    cos = jnp.cos(ang)[None, :, None, :]
    sin = jnp.sin(ang)[None, :, None, :]
    a1, a2 = a[..., :half], a[..., half:]
    return jnp.concatenate([a1 * cos - a2 * sin, a1 * sin + a2 * cos], axis=-1)

def _retention_one_direction(q, k, v, log_gamma, strict):
    b, h, s, dk = q.shape
    dv = v.shape[-1]
    c = RET_CHUNK
    n = s // c
    qc = q.reshape(b, h, n, c, dk)
    kc = k.reshape(b, h, n, c, dk)
    vc = v.reshape(b, h, n, c, dv)
    pos = jnp.arange(c, dtype=jnp.float32)
    diff = pos[:, None] - pos[None, :]
    mask = (diff > 0) if strict else (diff >= 0)
    decay = jnp.where(mask[None], jnp.exp(jnp.where(mask, diff, 0.0)[None] * log_gamma[:, None, None]), 0.0)
    scores = jnp.einsum('bhnid,bhnjd->bhnij', qc, kc) * decay[None, :, None]
    y_inner = jnp.einsum('bhnij,bhnje->bhnie', scores, vc)
    k_decay = jnp.exp((c - 1 - pos)[None, :] * log_gamma[:, None])
    q_decay = jnp.exp((pos + 1)[None, :] * log_gamma[:, None])
    chunk_decay = jnp.exp(c * log_gamma)[None, :, None, None]
    kv = jnp.einsum('bhnjd,hj,bhnje->bhnde', kc, k_decay, vc)

    def step(state, kv_chunk):
        return state * chunk_decay + kv_chunk, state

    _, prev = lax.scan(step, jnp.zeros((b, h, dk, dv), jnp.float32), jnp.moveaxis(kv, 2, 0))
    prev = jnp.moveaxis(prev, 0, 2)
    y_cross = jnp.einsum('bhnid,hi,bhnde->bhnie', qc, q_decay, prev)
    return (y_inner + y_cross).reshape(b, h, s, dv)

def _retention_branch(rq, rk, rv, rg, dec_f, dec_b, gn_gain, w_o):
    b, s, _ = rq.shape
    q = _rope(rq.reshape(b, s, RET_HEADS, RET_QK_DIM).astype(jnp.float32)) * (RET_QK_DIM ** -0.5)
    k = _rope(rk.reshape(b, s, RET_HEADS, RET_QK_DIM).astype(jnp.float32))
    v = rv.reshape(b, s, RET_HEADS, RET_V_DIM).astype(jnp.float32)
    q, k, v = q.transpose(0, 2, 1, 3), k.transpose(0, 2, 1, 3), v.transpose(0, 2, 1, 3)
    lg_f = jax.nn.log_sigmoid(dec_f.astype(jnp.float32))
    lg_b = jax.nn.log_sigmoid(dec_b.astype(jnp.float32))
    y_fwd = _retention_one_direction(q, k, v, lg_f, False)
    y_bwd = jnp.flip(_retention_one_direction(jnp.flip(q, 2), jnp.flip(k, 2), jnp.flip(v, 2), lg_b, True), 2)
    y = y_fwd + y_bwd
    mu = jnp.mean(y, axis=-1, keepdims=True)
    var = jnp.mean(jnp.square(y - mu), axis=-1, keepdims=True)
    y = (y - mu) * lax.rsqrt(var + GN_EPS)
    y = y.transpose(0, 2, 1, 3).reshape(b, s, RET_V_WIDTH) * gn_gain.astype(jnp.float32)
    return (jax.nn.silu(rg) * y.astype(rg.dtype)) @ w_o

def _neighbourhood_attention(nq, nk, nv, rpb):
    b, s, _ = nq.shape
    rows_n = s // GRID_W
    w = GRID_W
    kr = min(NA_ROWS, rows_n)
    kc = NA_COLS

    def to_grid(a):
        return a.reshape(b, rows_n, w, NA_HEADS, NA_HEAD_DIM).transpose(0, 3, 1, 2, 4)

    qg, kg, vg = to_grid(nq), to_grid(nk), to_grid(nv)
    rows = jnp.arange(rows_n)
    row_start = jnp.clip(rows - kr // 2, 0, rows_n - kr)
    row_idx = row_start[:, None] + jnp.arange(kr)[None, :]
    cols = jnp.arange(w)
    col_start = jnp.clip(cols - kc // 2, 0, w - kc)
    col_off = cols[None, :] - col_start[:, None]
    col_mask = (col_off >= 0) & (col_off < kc)
    k_rows = jnp.take(kg, row_idx, axis=2)
    v_rows = jnp.take(vg, row_idx, axis=2)
    sc = jnp.einsum('bhrqd,bhrwkd->bhrqwk', qg, k_rows).astype(jnp.float32) * (NA_HEAD_DIM ** -0.5)
    rel_r = row_idx - rows[:, None] + (NA_ROWS - 1)
    rel_c = jnp.clip(cols[None, :] - cols[:, None], -(kc - 1), kc - 1) + (kc - 1)
    bias = rpb[:, rel_r[:, None, :, None], rel_c[None, :, None, :]].astype(jnp.float32)
    sc = jnp.where(col_mask[:, None, :], sc + bias, -jnp.inf)
    p = jax.nn.softmax(sc, axis=(-2, -1)).astype(vg.dtype)
    o = jnp.einsum('bhrqwk,bhrwkd->bhrqd', p, v_rows)
    return o.transpose(0, 2, 3, 1, 4).reshape(b, s, NA_WIDTH)

def _memory_cross_attention(xq, mem_n, w_kv):
    b, s, _ = xq.shape
    m = mem_n.shape[1]
    mk, mv = jnp.split(mem_n @ w_kv, 2, axis=-1)
    q = xq.reshape(b, s, XA_HEADS, XA_HEAD_DIM)
    k = mk.reshape(b, m, XA_HEADS, XA_HEAD_DIM)
    v = mv.reshape(b, m, XA_HEADS, XA_HEAD_DIM)
    sc = jnp.einsum('bshd,bmhd->bhsm', q, k).astype(jnp.float32) * (XA_HEAD_DIM ** -0.5)
    p = jax.nn.softmax(sc, axis=-1).astype(v.dtype)
    return jnp.einsum('bhsm,bmhd->bshd', p, v).reshape(b, s, XA_WIDTH)

def _hierarchical_moe(h, w_rg, b_rg, w_re, b_re, w_gate, w_up, w_down):
    b, s, d = h.shape
    t = h.reshape(b * s, d)
    g_n, e_n = MOE_GROUPS, MOE_EXPERTS_PER_GROUP
    grp_p = jax.nn.softmax((t @ w_rg + b_rg).astype(jnp.float32), axis=-1)
    grp_w, grp_idx = lax.top_k(grp_p, 1)
    exp_logits = (t @ w_re + b_re).astype(jnp.float32).reshape(-1, g_n, e_n)
    in_grp = jnp.take_along_axis(exp_logits, grp_idx[:, :, None], axis=1)[:, 0]
    top_w, top_idx = lax.top_k(jax.nn.softmax(in_grp, axis=-1), MOE_TOP_K)
    top_w = top_w / jnp.sum(top_w, axis=-1, keepdims=True) * grp_w
    exp_w = jnp.sum(jax.nn.one_hot(top_idx, e_n, dtype=jnp.float32) * top_w[..., None], axis=1)
    combine = (jax.nn.one_hot(grp_idx[:, 0], g_n, dtype=jnp.float32)[:, :, None] * exp_w[:, None, :]).astype(t.dtype)
    out = jnp.zeros_like(t)
    for g in range(g_n):
        a = jnp.einsum('td,edf->tef', t, w_gate[g])
        u = jnp.einsum('td,edf->tef', t, w_up[g])
        hid = jax.nn.silu(a) * u * combine[:, g, :, None]
        out = out + jnp.einsum('tef,efd->td', hid, w_down[g])
    return out.reshape(b, s, d)

def first_inputs(seed: int = 0) -> dict:
    key = jax.random.key(seed)
    ks = jax.random.split(key, 24)
    f32 = jnp.float32
    d = D_MODEL
    n_l = DEPTH
    g_n, e_n, f_n = MOE_GROUPS, MOE_EXPERTS_PER_GROUP, MOE_D_FF

    def nrm(k, shape, fan_in):
        return jax.random.normal(k, shape, f32) * (fan_in ** -0.5)

    def gain(k, shape):
        return 1.0 + 0.02 * jax.random.normal(k, shape, f32)

    base_gamma = 1.0 - 2.0 ** (-5.0 - jnp.arange(RET_HEADS, dtype=f32))
    base_logit = jnp.log(base_gamma) - jnp.log1p(-base_gamma)
    return {
        'x': jax.random.normal(ks[0], (BATCH, SEQ, d), f32),
        'mem': jax.random.normal(ks[1], (BATCH, MEM_LEN, d), f32),
        'g_mix': gain(ks[2], (n_l, d)),
        'w_in': nrm(ks[3], (n_l, d, IN_WIDTH), d),
        'ret_decay_fwd': base_logit[None] + 0.05 * jax.random.normal(ks[4], (n_l, RET_HEADS), f32),
        'ret_decay_bwd': base_logit[None] + 0.05 * jax.random.normal(ks[5], (n_l, RET_HEADS), f32),
        'ret_norm_gain': gain(ks[6], (n_l, RET_V_WIDTH)),
        'w_ret_o': nrm(ks[7], (n_l, RET_V_WIDTH, d), RET_V_WIDTH),
        'na_rpb': 0.1 * jax.random.normal(ks[8], (n_l, NA_HEADS, 2 * NA_ROWS - 1, 2 * NA_COLS - 1), f32),
        'w_na_o': nrm(ks[9], (n_l, NA_WIDTH, d), NA_WIDTH),
        'g_mem': gain(ks[10], (n_l, d)),
        'w_mem_kv': nrm(ks[11], (n_l, d, 2 * XA_WIDTH), d),
        'w_xa_o': nrm(ks[12], (n_l, XA_WIDTH, d), XA_WIDTH),
        'w_out': nrm(ks[13], (n_l, d, d), d),
        'g_ffn': gain(ks[14], (n_l, d)),
        'w_router_group': nrm(ks[15], (n_l, d, g_n), d),
        'b_router_group': 0.01 * jax.random.normal(ks[16], (n_l, g_n), f32),
        'w_router_expert': nrm(ks[17], (n_l, d, g_n * e_n), d),
        'b_router_expert': 0.01 * jax.random.normal(ks[18], (n_l, g_n * e_n), f32),
        'w_exp_gate': nrm(ks[19], (n_l, g_n, e_n, d, f_n), d),
        'w_exp_up': nrm(ks[20], (n_l, g_n, e_n, d, f_n), d),
        'w_exp_down': nrm(ks[21], (n_l, g_n, e_n, f_n, d), f_n),
        'g_final': gain(ks[22], (d,)),
    }

def first_block(x, mem, g_mix, w_in, ret_decay_fwd, ret_decay_bwd, ret_norm_gain, w_ret_o, na_rpb, w_na_o, g_mem, w_mem_kv, w_xa_o, w_out, g_ffn, w_router_group, b_router_group, w_router_expert, b_router_expert, w_exp_gate, w_exp_up, w_exp_down, g_final):
    split_points = [int(p) for p in np.cumsum(np.array(IN_SPLITS))[:-1]]
    for l in range(DEPTH):
        h = _rmsnorm(x, g_mix[l])
        rq, rk, rv, rg, nq, nk, nv, xq, gate_logits = jnp.split(h @ w_in[l], split_points, axis=-1)
        y_ret = _retention_branch(rq, rk, rv, rg, ret_decay_fwd[l], ret_decay_bwd[l], ret_norm_gain[l], w_ret_o[l])
        y_na = _neighbourhood_attention(nq, nk, nv, na_rpb[l]) @ w_na_o[l]
        y_xa = _memory_cross_attention(xq, _rmsnorm(mem, g_mem[l]), w_mem_kv[l]) @ w_xa_o[l]
        g_ret, g_na, g_xa = jnp.split(jax.nn.sigmoid(gate_logits), N_BRANCHES, axis=-1)
        x = x + (g_ret * y_ret + g_na * y_na + g_xa * y_xa) @ w_out[l]
        x = x + _hierarchical_moe(_rmsnorm(x, g_ffn[l]), w_router_group[l], b_router_group[l], w_router_expert[l], b_router_expert[l], w_exp_gate[l], w_exp_up[l], w_exp_down[l])
    return _rmsnorm(x, g_final)


DEPTH_2 = 2

CTX_LEN = 256
ROPE_THETA = 10000.0
EPS = 1e-6
Q_BLOCK = 128

MLA_HEADS = 4
MLA_Q_RANK = 256
MLA_KV_RANK = 128
MLA_NOPE = 64
MLA_ROPE = 32
MLA_V = 64
DIFF_HEADS = 4
DIFF_QK = 32
DIFF_V = 2 * DIFF_QK
GQA_HEADS = 8
GQA_KV_HEADS = 2
GQA_DIM = 64
GQA_GROUP = GQA_HEADS // GQA_KV_HEADS

MIX_WIDTH = MLA_HEADS * MLA_V + DIFF_HEADS * DIFF_V + GQA_HEADS * GQA_DIM
FFN_HIDDEN = -(-8 * D_MODEL // (3 * 256)) * 256

IN_SIZES = (
    MLA_Q_RANK,
    MLA_KV_RANK + MLA_ROPE,
    DIFF_HEADS * 2 * DIFF_QK,
    DIFF_HEADS * 2 * DIFF_QK,
    DIFF_HEADS * DIFF_V,
    GQA_HEADS * GQA_DIM,
    GQA_KV_HEADS * GQA_DIM,
    GQA_KV_HEADS * GQA_DIM,
)
IN_WIDTH_2 = sum(IN_SIZES)

MLA_SCALE = 1.0 / math.sqrt(MLA_NOPE + MLA_ROPE)
DIFF_SCALE = 1.0 / math.sqrt(DIFF_QK)
GQA_SCALE = 1.0 / math.sqrt(GQA_DIM)


def _rms(x, g):
    xf = x.astype(jnp.float32)
    y = xf * lax.rsqrt(jnp.mean(xf * xf, axis=-1, keepdims=True) + EPS)
    return (y * g.astype(jnp.float32)).astype(x.dtype)

def _axial_rope_tables(row, col, rot_dim):
    quarter = rot_dim // 4
    inv = ROPE_THETA ** (-jnp.arange(quarter, dtype=jnp.float32) / quarter)
    ang = jnp.concatenate([row.astype(jnp.float32)[:, None] * inv,
                           col.astype(jnp.float32)[:, None] * inv], axis=-1)
    return jnp.cos(ang), jnp.sin(ang)

def _rope_2(x, tables):
    if tables is None:
        return x
    cos, sin = tables
    half = x.shape[-1] // 2
    xf = x.astype(jnp.float32)
    x1, x2 = xf[..., :half], xf[..., half:]
    c = cos[None, :, None, :]
    s = sin[None, :, None, :]
    return jnp.concatenate([x1 * c - x2 * s, x2 * c + x1 * s], axis=-1).astype(x.dtype)

def _hf(t):
    return t.transpose(0, 2, 1, 3)

def _sdpa(q, k, v, scale):
    s = jnp.einsum('bhgqd,bhkd->bhgqk', q, k).astype(jnp.float32) * scale
    p = jax.nn.softmax(s, axis=-1).astype(v.dtype)
    return jnp.einsum('bhgqk,bhkd->bhgqd', p, v)

def _latent_attention(q, k, v, scale):
    B, Hk, G, S, d = q.shape
    nb = S // Q_BLOCK
    qb = q.reshape(B, Hk, G, nb, Q_BLOCK, d).transpose(3, 0, 1, 2, 4, 5)
    ob = lax.map(lambda qi: _sdpa(qi, k, v, scale), qb)
    return ob.transpose(1, 2, 3, 0, 4, 5).reshape(B, Hk, G, S, ob.shape[-1])

def _project(h, w_in, g_mla_q, w_mla_qb, g_mla_kv, w_mla_kvb, g_gqa_q, g_gqa_k,
             rope_small, rope_large):
    B, T, _ = h.shape
    p = h @ w_in
    idx = np.cumsum(IN_SIZES)[:-1].tolist()
    q_a, kv_a, dq, dk, dv, gq, gk, gv = jnp.split(p, idx, axis=-1)

    q = (_rms(q_a, g_mla_q) @ w_mla_qb).reshape(B, T, MLA_HEADS, MLA_NOPE + MLA_ROPE)
    q_nope, q_pe = q[..., :MLA_NOPE], _rope_2(q[..., MLA_NOPE:], rope_small)
    c_kv = kv_a[..., :MLA_KV_RANK]
    k_pe = _rope_2(kv_a[..., MLA_KV_RANK:][:, :, None, :], rope_small)
    kv = (_rms(c_kv, g_mla_kv) @ w_mla_kvb).reshape(B, T, MLA_HEADS, MLA_NOPE + MLA_V)
    k_nope, v_mla = kv[..., :MLA_NOPE], kv[..., MLA_NOPE:]
    q_mla = jnp.concatenate([q_nope, q_pe], axis=-1)
    k_mla = jnp.concatenate([k_nope, jnp.broadcast_to(k_pe, (B, T, MLA_HEADS, MLA_ROPE))], axis=-1)
    mla = (_hf(q_mla)[:, :, None], _hf(k_mla), _hf(v_mla))

    q_d = _rope_2(dq.reshape(B, T, DIFF_HEADS * 2, DIFF_QK), rope_small)
    k_d = _rope_2(dk.reshape(B, T, DIFF_HEADS * 2, DIFF_QK), rope_small)
    v_d = jnp.repeat(dv.reshape(B, T, DIFF_HEADS, DIFF_V), 2, axis=2)
    diff = (_hf(q_d)[:, :, None], _hf(k_d), _hf(v_d))

    q_g = _rope_2(_rms(gq.reshape(B, T, GQA_HEADS, GQA_DIM), g_gqa_q), rope_large)
    k_g = _rope_2(_rms(gk.reshape(B, T, GQA_KV_HEADS, GQA_DIM), g_gqa_k), rope_large)
    v_g = gv.reshape(B, T, GQA_KV_HEADS, GQA_DIM)
    q_g = q_g.reshape(B, T, GQA_KV_HEADS, GQA_GROUP, GQA_DIM).transpose(0, 2, 3, 1, 4)
    gqa = (q_g, _hf(k_g), _hf(v_g))
    return (mla, diff, gqa)

def _merge(o_mla, o_diff, o_gqa, lam, lam_init, g_diff_sub):
    B, _, _, T, _ = o_mla.shape
    y_mla = o_mla[:, :, 0].transpose(0, 2, 1, 3).reshape(B, T, MLA_HEADS * MLA_V)
    od = o_diff[:, :, 0].reshape(B, DIFF_HEADS, 2, T, DIFF_V)
    d = od[:, :, 0] - lam.astype(od.dtype) * od[:, :, 1]
    d = _rms(d, g_diff_sub) * (1.0 - lam_init)
    y_diff = d.transpose(0, 2, 1, 3).reshape(B, T, DIFF_HEADS * DIFF_V)
    y_gqa = o_gqa.transpose(0, 3, 1, 2, 4).reshape(B, T, GQA_HEADS * GQA_DIM)
    return jnp.concatenate([y_mla, y_diff, y_gqa], axis=-1)

def _swiglu(h, w_gate, w_up, w_down):
    return (jax.nn.silu(h @ w_gate) * (h @ w_up)) @ w_down

def second_inputs(seed: int = 0) -> dict:
    key = jax.random.key(seed)
    ks = iter(jax.random.split(key, 32))

    def nrm(shape, scale):
        return jax.random.normal(next(ks), shape, jnp.float32) * scale

    def gain(shape):
        return 1.0 + 0.05 * jax.random.normal(next(ks), shape, jnp.float32)

    D = D_MODEL
    return {
        "x": nrm((BATCH, SEQ, D), 1.0),
        "c": nrm((BATCH, D), 1.0),
        "ctx": nrm((BATCH, CTX_LEN, D), 1.0),
        "c_ctx": nrm((D,), 1.0),
        "w_ada": nrm((DEPTH_2, D, 6 * D), 0.5 * D ** -0.5),
        "b_ada": nrm((DEPTH_2, 6 * D), 0.01),
        "g_attn_pre": gain((DEPTH_2, D)),
        "g_attn_post": gain((DEPTH_2, D)),
        "w_in": nrm((DEPTH_2, D, IN_WIDTH_2), D ** -0.5),
        "g_mla_q": gain((DEPTH_2, MLA_Q_RANK)),
        "w_mla_qb": nrm((DEPTH_2, MLA_Q_RANK, MLA_HEADS * (MLA_NOPE + MLA_ROPE)), MLA_Q_RANK ** -0.5),
        "g_mla_kv": gain((DEPTH_2, MLA_KV_RANK)),
        "w_mla_kvb": nrm((DEPTH_2, MLA_KV_RANK, MLA_HEADS * (MLA_NOPE + MLA_V)), MLA_KV_RANK ** -0.5),
        "lambda_q1": nrm((DEPTH_2, DIFF_QK), 0.1),
        "lambda_k1": nrm((DEPTH_2, DIFF_QK), 0.1),
        "lambda_q2": nrm((DEPTH_2, DIFF_QK), 0.1),
        "lambda_k2": nrm((DEPTH_2, DIFF_QK), 0.1),
        "g_diff_sub": gain((DEPTH_2, DIFF_V)),
        "g_gqa_q": gain((DEPTH_2, GQA_DIM)),
        "g_gqa_k": gain((DEPTH_2, GQA_DIM)),
        "w_out": nrm((DEPTH_2, MIX_WIDTH, D), MIX_WIDTH ** -0.5),
        "g_ffn_pre": gain((DEPTH_2, D)),
        "g_ffn_post": gain((DEPTH_2, D)),
        "w_ffn_gate": nrm((DEPTH_2, D, FFN_HIDDEN), D ** -0.5),
        "w_ffn_up": nrm((DEPTH_2, D, FFN_HIDDEN), D ** -0.5),
        "w_ffn_down": nrm((DEPTH_2, FFN_HIDDEN, D), FFN_HIDDEN ** -0.5),
    }

def second_block(x, c, ctx, c_ctx, w_ada, b_ada, g_attn_pre, g_attn_post, w_in, g_mla_q, w_mla_qb,
              g_mla_kv, w_mla_kvb, lambda_q1, lambda_k1, lambda_q2, lambda_k2, g_diff_sub,
              g_gqa_q, g_gqa_k, w_out, g_ffn_pre, g_ffn_post, w_ffn_gate, w_ffn_up, w_ffn_down):
    n_tok = x.shape[1]
    rows = n_tok // GRID_W
    row = jnp.repeat(jnp.arange(rows, dtype=jnp.int32), GRID_W)
    col = jnp.tile(jnp.arange(GRID_W, dtype=jnp.int32), rows)
    rope_small = _axial_rope_tables(row, col, MLA_ROPE)
    rope_large = _axial_rope_tables(row, col, GQA_DIM)

    silu_c = jax.nn.silu(c)
    silu_cc = jax.nn.silu(c_ctx)
    xc = ctx
    scales = (MLA_SCALE, DIFF_SCALE, GQA_SCALE)

    for l in range(DEPTH_2):
        last = l == DEPTH_2 - 1
        mod = (silu_c @ w_ada[l] + b_ada[l])[:, None, :]
        mod_c = (silu_cc @ w_ada[l] + b_ada[l])[None, None, :]
        sh_a, sc_a, gt_a, sh_f, sc_f, gt_f = jnp.split(mod, 6, axis=-1)
        csh_a, csc_a, cgt_a, csh_f, csc_f, cgt_f = jnp.split(mod_c, 6, axis=-1)

        lam_init = 0.8 - 0.6 * math.exp(-0.3 * l)
        lam = (jnp.exp(jnp.sum(lambda_q1[l].astype(jnp.float32) * lambda_k1[l].astype(jnp.float32)))
               - jnp.exp(jnp.sum(lambda_q2[l].astype(jnp.float32) * lambda_k2[l].astype(jnp.float32)))
               + lam_init)

        h = _rms(x, g_attn_pre[l]) * (1.0 + sc_a) + sh_a
        hc = _rms(xc, g_attn_pre[l]) * (1.0 + csc_a) + csh_a
        proj_args = (w_in[l], g_mla_q[l], w_mla_qb[l], g_mla_kv[l], w_mla_kvb[l], g_gqa_q[l], g_gqa_k[l])
        lat = _project(h, *proj_args, rope_small, rope_large)
        cxt = _project(hc, *proj_args, None, None)

        o_lat = []
        for (q, k, v), (qc, kc, vc), s in zip(lat, cxt, scales):
            k_all = jnp.concatenate([k, kc], axis=2)
            v_all = jnp.concatenate([v, vc], axis=2)
            o_lat.append(_latent_attention(q, k_all, v_all, s))
        y = _merge(o_lat[0], o_lat[1], o_lat[2], lam, lam_init, g_diff_sub[l]) @ w_out[l]
        x = x + gt_a * _rms(y, g_attn_post[l])

        if not last:
            o_ctx = [_sdpa(qc, kc, vc, s) for (qc, kc, vc), s in zip(cxt, scales)]
            yc = _merge(o_ctx[0], o_ctx[1], o_ctx[2], lam, lam_init, g_diff_sub[l]) @ w_out[l]
            xc = xc + cgt_a * _rms(yc, g_attn_post[l])

        hf = _rms(x, g_ffn_pre[l]) * (1.0 + sc_f) + sh_f
        x = x + gt_f * _rms(_swiglu(hf, w_ffn_gate[l], w_ffn_up[l], w_ffn_down[l]), g_ffn_post[l])
        if not last:
            hfc = _rms(xc, g_ffn_pre[l]) * (1.0 + csc_f) + csh_f
            xc = xc + cgt_f * _rms(_swiglu(hfc, w_ffn_gate[l], w_ffn_up[l], w_ffn_down[l]), g_ffn_post[l])

    return x


def setup_inputs(seed=0):
    out = dict(first_inputs(seed))
    for name, value in second_inputs(seed + 1).items():
        if name != "x":
            out[name + "_2"] = value
    return out


def reference(
    x, mem, g_mix, w_in, ret_decay_fwd, ret_decay_bwd, ret_norm_gain, w_ret_o, na_rpb, w_na_o,
    g_mem, w_mem_kv, w_xa_o, w_out, g_ffn, w_router_group, b_router_group, w_router_expert,
    b_router_expert, w_exp_gate, w_exp_up, w_exp_down, g_final, c_2, ctx_2, c_ctx_2, w_ada_2,
    b_ada_2, g_attn_pre_2, g_attn_post_2, w_in_2, g_mla_q_2, w_mla_qb_2, g_mla_kv_2,
    w_mla_kvb_2, lambda_q1_2, lambda_k1_2, lambda_q2_2, lambda_k2_2, g_diff_sub_2, g_gqa_q_2,
    g_gqa_k_2, w_out_2, g_ffn_pre_2, g_ffn_post_2, w_ffn_gate_2, w_ffn_up_2, w_ffn_down_2,
):
    x = first_block(
        x, mem, g_mix, w_in, ret_decay_fwd, ret_decay_bwd, ret_norm_gain, w_ret_o, na_rpb,
        w_na_o, g_mem, w_mem_kv, w_xa_o, w_out, g_ffn, w_router_group, b_router_group,
        w_router_expert, b_router_expert, w_exp_gate, w_exp_up, w_exp_down, g_final,
    )
    return second_block(
        x, c_2, ctx_2, c_ctx_2, w_ada_2, b_ada_2, g_attn_pre_2, g_attn_post_2, w_in_2,
        g_mla_q_2, w_mla_qb_2, g_mla_kv_2, w_mla_kvb_2, lambda_q1_2, lambda_k1_2, lambda_q2_2,
        lambda_k2_2, g_diff_sub_2, g_gqa_q_2, g_gqa_k_2, w_out_2, g_ffn_pre_2, g_ffn_post_2,
        w_ffn_gate_2, w_ffn_up_2, w_ffn_down_2,
    )


_drawn_inputs = setup_inputs


def setup_inputs(seed=0):
    import zlib

    import numpy as np

    out = dict(_drawn_inputs(seed))
    spreads = {}
    factors = {'ret_norm_gain': 14.223,
     'na_rpb': 12.648,
     'g_mem': 8.0,
     'b_router_group': 26.715,
     'b_router_expert': 22.706,
     'g_final': 2.79,
     'g_attn_pre_2': 3.048,
     'g_mla_q_2': 8.0,
     'g_mla_kv_2': 6.485,
     'lambda_q2_2': 4.429,
     'lambda_k2_2': 7.562,
     'g_diff_sub_2': 24.024,
     'g_gqa_q_2': 8.0,
     'g_gqa_k_2': 8.0,
     'g_ffn_post_2': 2.897,
     'g_ffn': 5.349,
     'g_attn_post_2': 4.95,
     'lambda_q1_2': 8.0,
     'lambda_k1_2': 8.0}
    for name, (base, spread) in spreads.items():
        noise = np.random.default_rng([zlib.crc32(name.encode()), seed]).standard_normal(out[name].shape)
        drawn = base * np.exp(spread * noise) if base else spread * noise
        out[name] = jnp.asarray(drawn.astype(out[name].dtype))
    for name, factor in factors.items():
        out[name] = (out[name] * factor).astype(out[name].dtype)
    return out
```

```python
import math
from contextlib import ExitStack, contextmanager

import numpy as np

import concourse.bass as bass
from concourse import mybir

P = 128
D = 1024
KT = D // P
SEQ = 512
CTX = 256
ALL = SEQ + CTX
F32 = mybir.dt.float32
ACT = mybir.ActivationFunctionType
ALU = mybir.AluOpType
AX = mybir.AxisListType.X

BLOCKS = 16
CHUNK = BLOCKS * P
RING = 3

RET_HEADS, NA_HEADS, XA_HEADS = 4, 8, 4
GRID_W, GRID_H, WIN = 64, 8, 32
EXPERTS, D_FF = 16, 512
HIDDEN = 2816
HT = HIDDEN // P
LAYERS = 2
MLA_H, DIFF_H, GQA_H = 4, 4, 8
LAM_INIT = [0.8 - 0.6 * math.exp(-0.3 * l) for l in range(LAYERS)]
RPB_RUN = 7 * 31 + WIN + 16
DIFFS = SEQ + 3 * P
BIG = 1e30
ARENA = 25184

MOE_FIRST = 48
ADA_TILES = LAYERS * 48
ADA_PER_EXPERT = ADA_TILES // EXPERTS
MOE_CHUNKS = 6 + ADA_PER_EXPERT * KT // BLOCKS


def param_layout():
    at, out = 0, {}
    items = [("g_mix", 8), ("ret_gain", 8), ("g_mem", 8), ("g_ffn", 8), ("g_final", 8), ("decay", 8),
             ("router_bias", 80), ("c", 16), ("b_ada", 2 * ADA_TILES)]
    for l in range(LAYERS):
        items += [(f"{n}{l}", w) for n, w in (
            ("attn_pre", 8), ("attn_post", 8), ("mla_q", 2), ("mla_kv", 1), ("diff_sub", 1), ("gqa_q", 1),
            ("gqa_k", 1), ("ffn_pre", 8), ("ffn_post", 8), ("lambda", 4))]
    for n, w in items:
        out[n] = (at, w)
        at += w
    return out, at


def const_layout():
    at, out = 0, {}
    for n, w in (("ident", P), ("ones", P), ("ones64", P), ("rot128", P), ("rot64", P), ("rot32", P),
                 ("mask", 3 * 256), ("rank", 16)):
        out[n] = (at, w)
        at += w
    return out, at


class Signal:

    def __init__(self, nc, ctx, name, known):
        self.name, self.sem = name, ctx.enter_context(nc.semaphore(name))
        self.n, self.points, self.new, self.known = 0, {}, [], known.get(name)

    def on(self, *key, also=None):
        self.n += 1
        for k in (key, also):
            if k is not None:
                assert k not in self.points, k
                self.points[k] = (self.n, 0, 1)
                self.new.append(k)
        return self.sem, 1

    def at(self, *key, i=None):
        if self.known is None:
            return self.sem, 1
        first, step, trips = self.known[key]
        if i is None:
            return self.sem, first + step * (trips - 1)
        return self.sem, i * step + first


@contextmanager
def repeated(engine, trips, signals):
    start = [s.n for s in signals]
    for s in signals:
        s.new = []
    with engine.Fori(0, trips) as i:
        yield i
    for s, n0 in zip(signals, start):
        step = s.n - n0
        for k in s.new:
            s.points[k] = (s.points[k][0], step, trips)
        s.n = n0 + step * trips


class Chunks:

    def __init__(self):
        self.block = 0


def program(nc, ins, out, known):
    PAR, n_par = param_layout()
    CON, n_con = const_layout()
    stream = ins["stream"]
    n_chunks = stream.shape[0]
    with ExitStack() as ctx:
        def sb(name, *shape):
            return ctx.enter_context(nc.sbuf_tensor(name, [P, *shape], F32))

        def sem(name):
            return ctx.enter_context(nc.semaphore(name))

        ring = sb("ring", RING, CHUNK)
        x = sb("x", KT, ALL)
        h = sb("h", KT, ALL)
        work = sb("work", 12, SEQ)
        tmp, std, rstd = work[:, 0:8], work[:, 8:10], work[:, 10:12]
        par = sb("par", n_par)
        con = sb("con", n_con)
        w_router = sb("w_router", KT, 20)
        mods = sb("mods", ADA_TILES, 2)
        silu_c = sb("silu_c", KT, 2)
        cols = sb("cols", 64)
        stat = sb("stat", 8, 4)
        route = sb("route", 640)
        arena = sb("arena", ARENA)
        ps = ctx.enter_context(nc.psum_tensor("ps", [P, 8, 512], F32))

        def pc(name, j=0, w=1):
            a = PAR[name][0] + j
            return par[:, a:a + w]

        def cc(name):
            a, w = CON[name]
            return con[:, a:a + w]

        def area(offset, *dims):
            n = int(np.prod(dims))
            assert offset + n <= ARENA, (offset, dims)
            v = arena[:, offset:offset + n]
            if len(dims) == 2:
                v = v.rearrange("p (a b) -> p a b", a=dims[0])
            if len(dims) == 3:
                v = v.rearrange("p (a b c) -> p a b c", a=dims[0], b=dims[1])
            return v

        def spread(ap, *dims):
            return bass.AP(tensor=ap.tensor, offset=ap.offset, ap=[list(ap.ap[0])] + [list(d) for d in dims])

        ident, ones, ones64 = cc("ident"), cc("ones"), cc("ones64")
        mixed_sum = area(0, 8, SEQ)
        ret_q, ret_k = area(4096, 4, SEQ), area(6144, 4, SEQ)
        ret_v = area(8192, 4, 1024)
        ret_y = area(12288, 8, SEQ)
        ret_s = area(16384, 4, SEQ)
        dist = area(18432, 2, DIFFS)
        ret_e = area(20224, 2, DIFFS)
        ret_t = work[:, 0:2, :].rearrange("p a b -> p (a b)")[:, 0:DIFFS]
        trig128 = area(22016, 2, SEQ)
        rpb = area(23040, NA_HEADS, RPB_RUN)
        na_q, na_k, na_v = area(4096, 4, SEQ), area(6144, 4, SEQ), area(8192, 4, SEQ)
        na_win = area(10240, 8, SEQ)
        na_o = area(14336, 4, SEQ)
        b1_p = area(16384, 3, 256)
        b1_pt = area(17152, 2, 2, SEQ)
        xa_q, xa_k, xa_v, xa_o = area(4096, 4, SEQ), area(6144, 4, CTX), area(7168, 2, SEQ), area(8192, 4, SEQ)
        comb = area(4096, EXPERTS, SEQ)
        hid = area(12288, 4, SEQ)
        mla_q, mla_k = area(0, 4, ALL), area(3072, 4, ALL)
        diff_q, diff_k = area(6144, 2, ALL), area(7680, 2, ALL)
        gqa_q, gqa_k = area(9216, 4, ALL), area(12288, ALL)
        val = area(13056, 6, 640)
        prob = work[:, :, :].rearrange("p a b -> p (a b)")[:, 3072:3072 + 3 * ALL].rearrange("p (a b) -> p a b", a=3)
        prob_t = area(16896, 2, 6, SEQ)
        q_low, kv_low, k_pe = area(16896, 2, ALL), area(18432, ALL), area(19200, ALL)
        w_small = area(19968, 2 * 384 + 512)
        trig = area(23040, 4, SEQ)
        out_1 = tmp[:, 0:3, :].rearrange("p a b -> p (a b)").rearrange("p (a b) -> p a b", a=2)
        out_2 = tmp[:, 3:6, :].rearrange("p a b -> p (a b)").rearrange("p (a b) -> p a b", a=2)
        attn_y = area(0, KT, ALL)
        ffn_hid = area(0, HT, ALL)
        ffn_y = area(16896, KT, ALL)

        R, at = {"rank": cc("rank").rearrange("p (t n) -> p t n", t=4)}, 64
        for name, w in (("lg", 20), ("gd", 4), ("eq", 4), ("cand", 4), ("g1", 4), ("ge", 4), ("ig", 4), ("ed", 4),
                        ("ee", 4), ("e2", 4), ("o1", 4), ("o2", 4)):
            R[name] = route[:, at:at + 4 * w].rearrange("p (t n) -> p t n", t=4)
            at += 4 * w
        for name in ("gm", "best", "gw", "em"):
            R[name] = route[:, at:at + 4]
            at += 4
        R["sel"] = route[:, at:at + 64].rearrange("p (t g e) -> p t g e", t=4, g=4)

        signals = {}

        def signal(engine, name):
            s = Signal(nc, ctx, name, known)
            signals.setdefault(engine, []).append(s)
            return s

        loaded = [sem(f"chunk_loaded{r}") for r in range(RING)]
        inputs_loaded = sem("inputs_loaded")
        context_loaded = sem("context_loaded")
        late_loaded = sem("late_loaded")
        stored = sem("stored")
        streamed, summed, scored = signal("pe", "streamed"), signal("pe", "summed"), signal("pe", "scored")
        turned, attended, multiplied = signal("pe", "turned"), signal("pe", "attended"), signal("pe", "multiplied")
        squared, rooted, exped = signal("act", "squared"), signal("act", "rooted"), signal("act", "exped")
        act_moved, gated = signal("act", "act_moved"), signal("act", "gated")
        normed, inverted, maxed = signal("dve", "normed"), signal("dve", "inverted"), signal("dve", "maxed")
        dve_moved, fused, scaled = signal("dve", "dve_moved"), signal("dve", "fused"), signal("dve", "scaled")
        small, roped = signal("dve", "small"), signal("dve", "roped")
        ends = {}
        known_ends = known.get("ends")
        seen = {}

        def stage(name, e):
            before = seen.setdefault(name, [0, {}])
            n = before[0]
            before[0] += 1
            if True:
                ends[(name, n)] = [s.n for s in signals[name]]
            if known_ends is None:
                return
            for other in ("pe", "act", "dve"):
                for s, value in zip(signals[other], known_ends[(other, n)]):
                    if value > before[1].get(s.name, 0):
                        e.wait_ge(s.sem, value)
                        before[1][s.name] = value

        late_order = []

        block = ctx.enter_context(nc.Block())

        @block.sync
        def _(sp):
            for dst, src in ((x[:, :, 0:SEQ], ins["xT"]), (x[:, :, SEQ:ALL], ins["memT"]), (par[:], ins["par"]),
                             (con[:], ins["con"]), (trig128, ins["trig128"]), (dist, ins["dist"]),
                             (rpb, ins["rpb"]), (w_router[:], ins["w_router"])):
                sp.dma_start(dst, src).then_inc(inputs_loaded, 16)

            def load(n, source, i=None):
                sp.dma_start(ring[:, n % RING], source).then_inc(loaded[n % RING], 16)

            moe_first, n = MOE_FIRST, 0
            while n < n_chunks:
                if n == moe_first + MOE_CHUNKS:
                    with sp.Fori(1, EXPERTS) as i:
                        for j in range(MOE_CHUNKS):
                            c = moe_first + j
                            if j >= RING:
                                sp.wait_ge(*streamed.at("chunk", c - RING, i=i))
                            else:
                                sp.wait_ge(*streamed.at("chunk", c + MOE_CHUNKS - RING, i=i - 1))
                            sp.dma_start(ring[:, c % RING], stream[i * MOE_CHUNKS + c]).then_inc(loaded[c % RING], 16)
                    n = moe_first + MOE_CHUNKS * EXPERTS
                    continue
                if n >= RING:
                    c = n - RING
                    last = moe_first + MOE_CHUNKS * EXPERTS
                    if last - RING <= c < last:
                        c = moe_first + (c - moe_first) % MOE_CHUNKS
                        sp.wait_ge(*streamed.at("chunk", c))
                    elif moe_first <= c < last:
                        sp.wait_ge(*streamed.at("chunk", c, i=0))
                    else:
                        sp.wait_ge(*streamed.at("chunk", c))
                load(n, stream[n])
                n += 1
            sp.wait_ge(*normed.at("final"))
            sp.dma_start(out, x[:, :, 0:SEQ]).then_inc(stored, 16)
            sp.wait_ge(stored, 16)

        @block.gpsimd
        def _(pool):
            pool.wait_ge(*normed.at("norm_mem done"))
            nc.gpsimd.dma_start(x[:, :, SEQ:ALL], ins["ctxT"]).then_inc(context_loaded, 16)
            pool.wait_ge(*dve_moved.at("moe done"))
            nc.gpsimd.dma_start(trig, ins["trig"]).then_inc(late_loaded, 16)
            nc.gpsimd.dma_start(w_small, ins["w_small"][0]).then_inc(late_loaded, 16)
            pool.wait_ge(*normed.at(("ffn_post", 0), 1, "end"))
            nc.gpsimd.dma_start(w_small, ins["w_small"][1]).then_inc(late_loaded, 16)

        SEQ_ONLY = [(0, SEQ)]
        BOTH = [(0, SEQ), (SEQ, CTX)]

        def norm_jobs(src, nk, pieces, mean_of, n, write, parts=P):
            return [dict(src=[src(k, c0, cn) for k in range(nk)], ones=mean_of, inv=1.0 / n, write=write,
                         piece=(c0, cn), parts=parts) for c0, cn in pieces]

        def slots(jobs):
            at, user, out_ = 0, {}, []
            for j, job in enumerate(jobs):
                own = []
                for k in range(len(job["src"])):
                    s = job.get("slots", range(8))[at % len(job.get("slots", range(8)))]
                    own.append((s, user.get(s)))
                    user[s] = j
                    at += 1
                out_.append(own)
            return out_

        def norm_pe(pe, tag, jobs, square_at=None):
            for j, job in enumerate(jobs):
                cn, parts = job["piece"][1], job["parts"]
                if j >= 2:
                    pe.wait_ge(*rooted.at(tag, j - 2))
                for k, (s, _) in enumerate(slots(jobs)[j]):
                    pe.wait_ge(*squared.at(tag, j, k))
                    mm = pe.matmul(ps[0:parts, j % 2, 0:cn], job["ones"][0:parts, 0:parts],
                                   tmp[0:parts, s, 0:cn], start=(k == 0), stop=(k == len(job["src"]) - 1))
                mm.then_inc(*summed.on(tag, j))

        def norm_act(act, tag, jobs):
            for j in range(len(jobs) + 1):
                if j < len(jobs):
                    job = jobs[j]
                    cn, parts = job["piece"][1], job["parts"]
                    for k, (s, user) in enumerate(slots(jobs)[j]):
                        if user is not None:
                            act.wait_ge(*summed.at(tag, user))
                        nc.scalar.activation(tmp[0:parts, s, 0:cn], job["src"][k], ACT.Square)\
                            .then_inc(*squared.on(tag, j, k))
                if j >= 1:
                    job = jobs[j - 1]
                    cn, parts = job["piece"][1], job["parts"]
                    act.wait_ge(*summed.at(tag, j - 1))
                    if j >= 3:
                        act.wait_ge(*inverted.at(tag, j - 3))
                    nc.scalar.activation(std[0:parts, (j - 1) % 2, 0:cn], ps[0:parts, (j - 1) % 2, 0:cn], ACT.Sqrt,
                                         bias=cols[0:parts, job.get("eps", 0):job.get("eps", 0) + 1],
                                         scale=job["inv"]).then_inc(*rooted.on(tag, j - 1))

        def norm_dve(dve, tag, jobs):
            for j, job in enumerate(jobs):
                cn, parts = job["piece"][1], job["parts"]
                dve.wait_ge(*rooted.at(tag, j))
                if j >= 2:
                    dve.wait_ge(*normed.at(tag, j - 2, "end"))
                r = rstd[0:parts, j % 2, 0:cn]
                nc.vector.reciprocal(r, std[0:parts, j % 2, 0:cn]).then_inc(*inverted.on(tag, j))
                dve.wait_ge(*inverted.at(tag, j))
                job["write"](dve, tag, j, job["piece"], r)

        def write_scaled(dst, gain, shift=None, final=None):
            def write(dve, tag, j, piece, r):
                c0, cn = piece
                job = job_of[tag][j]
                nk = len(job["src"])
                for k in range(nk):
                    key = (tag, j, "end") if k == nk - 1 and not shift else (tag, j, k)
                    nc.vector.scalar_tensor_tensor(out=dst(k, c0, cn), in0=job["src"][k], scalar=gain(k, c0), in1=r,
                                                   op0=ALU.mult, op1=ALU.mult)\
                        .then_inc(*normed.on(*key, also=(final,) if final and k == nk - 1 else None))
                if shift:
                    for k in range(nk):
                        dve.wait_ge(*normed.at(tag, j, k))
                        nc.vector.tensor_scalar(dst(k, c0, cn), dst(k, c0, cn), shift(k, c0), None, ALU.add)\
                            .then_inc(*normed.on(tag, j, "end" if k == nk - 1 else f"shifted{k}"))
            return write

        def write_residual(gain):
            def write(dve, tag, j, piece, r):
                c0, cn = piece
                job = job_of[tag][j]
                for k in range(KT):
                    nc.vector.scalar_tensor_tensor(out=job["src"][k], in0=job["src"][k], scalar=gain(k, c0), in1=r,
                                                   op0=ALU.mult, op1=ALU.mult).then_inc(*normed.on(tag, j, k))
                for k in range(KT):
                    dve.wait_ge(*normed.at(tag, j, k))
                    nc.vector.tensor_tensor(x[:, k, c0:c0 + cn], x[:, k, c0:c0 + cn], job["src"][k], ALU.add)\
                        .then_inc(*normed.on(tag, j, "end" if k == KT - 1 else f"added{k}"))
            return write

        job_of = {}

        def xs(k, c0, cn):
            return x[:, k, c0:c0 + cn]

        def hs(k, c0, cn):
            return h[:, k, c0:c0 + cn]

        job_of["norm_x"] = norm_jobs(xs, KT, SEQ_ONLY, ones, D, write_scaled(hs, lambda k, c0: pc("g_mix", k)))
        job_of["norm_mem"] = norm_jobs(xs, KT, [(SEQ, CTX)], ones, D,
                                       write_scaled(hs, lambda k, c0: pc("g_mem", k), final="norm_mem done"))
        job_of["norm_moe"] = norm_jobs(xs, KT, SEQ_ONLY, ones, D, write_scaled(hs, lambda k, c0: pc("g_ffn", k)))
        job_of["norm_first"] = norm_jobs(xs, KT, SEQ_ONLY, ones, D, write_scaled(xs, lambda k, c0: pc("g_final", k)))
        job_of["ret_norm"] = [dict(src=[ret_y[:, 2 * hd + e, :] for e in range(2)], ones=ones, inv=1.0 / 256, eps=1,
                                   piece=(0, SEQ), parts=P,
                                   write=write_scaled(lambda k, c0, cn, hd=hd: ret_y[:, 2 * hd + k, :],
                                                      lambda k, c0, hd=hd: pc("ret_gain", 2 * hd + k)))
                              for hd in range(RET_HEADS)]

        def scal(kind, k, c0):
            a = 8 + (kind * 2 + (1 if c0 >= SEQ else 0)) * 8 + k
            return cols[:, a:a + 1]

        def mod(l, which, k, c0):
            return mods[:, l * 48 + which * 8 + k, (1 if c0 >= SEQ else 0):(2 if c0 >= SEQ else 1)]

        for l in range(LAYERS):
            own = BOTH if l < LAYERS - 1 else SEQ_ONLY
            job_of["attn_pre", l] = norm_jobs(xs, KT, BOTH, ones, D, write_scaled(
                hs, lambda k, c0: scal(0, k, c0), lambda k, c0, l=l: mod(l, 0, k, c0)))
            job_of["attn_post", l] = norm_jobs(lambda k, c0, cn: attn_y[:, k, c0:c0 + cn], KT, own, ones, D,
                                               write_residual(lambda k, c0: scal(1, k, c0)))
            job_of["ffn_pre", l] = norm_jobs(xs, KT, own, ones, D, write_scaled(
                hs, lambda k, c0: scal(0, k, c0), lambda k, c0, l=l: mod(l, 3, k, c0)))
            job_of["ffn_post", l] = norm_jobs(lambda k, c0, cn: ffn_y[:, k, c0:c0 + cn], KT, own, ones, D,
                                              write_residual(lambda k, c0: scal(1, k, c0)))

            def low(k, c0, cn):
                return q_low[:, k, c0:c0 + cn]

            def kv(k, c0, cn):
                return kv_low[:, c0:c0 + cn]
            jobs = norm_jobs(kv, 1, BOTH, ones, 128, write_scaled(kv, lambda k, c0, l=l: pc(f"mla_kv{l}")))
            jobs += norm_jobs(low, 2, own, ones, 256, write_scaled(low, lambda k, c0, l=l: pc(f"mla_q{l}", k)))
            for t in range(4):
                def gq(k, c0, cn, t=t):
                    return gqa_q[:, t, c0:c0 + cn]
                jobs += norm_jobs(gq, 1, own, ones64, 64, write_scaled(gq, lambda k, c0, l=l: pc(f"gqa_q{l}")))

            def gk(k, c0, cn):
                return gqa_k[:, c0:c0 + cn]
            jobs += norm_jobs(gk, 1, BOTH, ones64, 64, write_scaled(gk, lambda k, c0, l=l: pc(f"gqa_k{l}")))
            job_of["low", l] = jobs
            jobs = []
            for t in range(2):
                def dd(k, c0, cn, t=t):
                    return out_1[:, t, c0:c0 + cn]
                jobs += norm_jobs(dd, 1, own, ones64, 64, write_scaled(
                    lambda k, c0, cn, t=t: h[:, 2 + t, c0:c0 + cn], lambda k, c0: cols[:, 6:7]))
            for job in jobs:
                job["slots"] = (6, 7)
            job_of["diff", l] = jobs

        chunks = Chunks()

        def take(pe, i=None, first=0, count=1):
            b = chunks.block
            n, o = b // BLOCKS, b % BLOCKS
            if o == 0:
                if i is None:
                    pe.wait_ge(loaded[n % RING], 16 * (n // RING + 1))
                else:
                    pe.wait_ge(loaded[n % RING], i * (16 * MOE_CHUNKS // RING) + 16 * (n // RING + 1))
            chunks.block += count
            return ring[:, n % RING, o * P:(o + count) * P]

        def chunk_end():
            return ("chunk", chunks.block // BLOCKS - 1) if chunks.block % BLOCKS == 0 else None

        def group(pe, key, banks, rhs, K, pieces, out_cols=None, i=None):
            for k in range(K):
                w = take(pe, i)
                for pi, (c0, cn) in enumerate(pieces):
                    mm = pe.matmul(ps[:, banks[pi], 0:cn], w, rhs(k, c0, cn), start=(k == 0), stop=(k == K - 1))
                    last = pi == len(pieces) - 1
                    also = chunk_end() if last else None
                    if k == K - 1:
                        mm.then_inc(*streamed.on(*key, pi, also=also))
                    elif also:
                        mm.then_inc(*streamed.on(*also))

        def tiles(ms, pieces_of):
            g = 0
            for m in range(ms):
                for pi, (c0, cn) in enumerate(pieces_of(m)):
                    yield g, m, pi, c0, cn
                    g += 1

        def moved_at(tag, g):
            return (act_moved if g % 2 == 0 else dve_moved).at(tag, g)

        def project_pe(pe, tag, ms, K, rhs, pieces_of):
            g = 0
            for m in range(ms):
                pieces = pieces_of(m)
                for pi in range(len(pieces)):
                    if g + pi >= 8:
                        pe.wait_ge(*moved_at(tag, g + pi - 8))
                group(pe, (tag, m), [(g + pi) % 8 for pi in range(len(pieces))], rhs, K, pieces)
                g += len(pieces)

        def project_move(engine, which, tag, ms, pieces_of, dst):
            for g, m, pi, c0, cn in tiles(ms, pieces_of):
                if g % 2 != which:
                    continue
                engine.wait_ge(*streamed.at(tag, m, pi))
                d, s = dst(m, c0, cn, ps[:, g % 8, 0:cn])
                if which == 0:
                    nc.scalar.activation(d, s, ACT.Copy).then_inc(*act_moved.on(tag, g))
                else:
                    nc.vector.tensor_copy(d, s).then_inc(*dve_moved.on(tag, g))

        def values_pe(pe, tag, token_tiles, lhs, nb, g0=0):
            start = chunks.block
            taken = [take(pe, count=nb) for _ in range(KT)]
            for t in range(token_tiles):
                if g0 + t >= 8:
                    pe.wait_ge(*moved_at(tag, g0 + t - 8))
                for k in range(KT):
                    mm = pe.matmul(ps[:, (g0 + t) % 8, 0:nb * P], lhs(k, t), taken[k],
                                   start=(k == 0), stop=(k == KT - 1))
                    used = start + (k + 1) * nb
                    if t == token_tiles - 1 and k < KT - 1 and used % BLOCKS == 0:
                        mm.then_inc(*streamed.on("chunk", used // BLOCKS - 1))
                mm.then_inc(*streamed.on(tag, g0 + t, also=chunk_end() if t == token_tiles - 1 else None))

        def values_move(engine, which, tag, token_tiles, dst, width, g0=0):
            for t in range(token_tiles):
                if (g0 + t) % 2 != which:
                    continue
                engine.wait_ge(*streamed.at(tag, g0 + t))
                s = ps[:, (g0 + t) % 8, 0:width]
                if which == 0:
                    nc.scalar.activation(dst(t), s, ACT.Copy).then_inc(*act_moved.on(tag, g0 + t))
                else:
                    nc.vector.tensor_copy(dst(t), s).then_inc(*dve_moved.on(tag, g0 + t))

        def branch_pe(pe, tag, K, rhs):
            for m in range(KT):
                for b, (what, kk, r) in enumerate((("gate", KT, hs), ("y", K, rhs))):
                    if m >= 4:
                        pe.wait_ge(*(gated.at(tag, m - 4) if b == 0 else fused.at(tag, m - 4, "y")))
                    group(pe, (tag, what, m), [(2 * m + b) % 8], r, kk, SEQ_ONLY)

        def branch_act(act, tag):
            for m in range(KT):
                act.wait_ge(*streamed.at(tag, "gate", m, 0))
                if m >= 2:
                    act.wait_ge(*fused.at(tag, m - 2, "y"))
                nc.scalar.activation(tmp[:, m % 2, :], ps[:, (2 * m) % 8, :], ACT.Sigmoid).then_inc(*gated.on(tag, m))

        def branch_dve(dve, tag, first):
            for m in range(KT):
                dve.wait_ge(*gated.at(tag, m))
                dve.wait_ge(*streamed.at(tag, "y", m, 0))
                y = ps[:, (2 * m + 1) % 8, :]
                if first:
                    nc.vector.tensor_tensor(mixed_sum[:, m, :], tmp[:, m % 2, :], y, ALU.mult)\
                        .then_inc(*fused.on(tag, m, "y"))
                    continue
                if m >= 2:
                    dve.wait_ge(*fused.at(tag, m - 2, "sum"))
                nc.vector.tensor_tensor(tmp[:, 2 + m % 2, :], tmp[:, m % 2, :], y, ALU.mult)\
                    .then_inc(*fused.on(tag, m, "y"))
                dve.wait_ge(*fused.at(tag, m, "y"))
                nc.vector.tensor_tensor(mixed_sum[:, m, :], mixed_sum[:, m, :], tmp[:, 2 + m % 2, :], ALU.add)\
                    .then_inc(*fused.on(tag, m, "sum"))

        class Attention:
            def __init__(self, tag, heads, per_head, keys, scale, score, mix, dest, p, pt, bias=None):
                self.tag, self.heads, self.per_head, self.keys, self.scale = tag, heads, per_head, keys, scale
                self.score, self.mix, self.dest, self.p, self.pt, self.bias = score, mix, dest, p, pt, bias
                self.units, self.kt = heads * per_head, keys // P

            def s(self, u):
                return ps[:, 2 * (u % 2):2 * (u % 2) + 2, :].rearrange("p a b -> p (a b)")[:, 0:self.keys]

            def copies(self, u):
                return [act_moved.at(self.tag, "pt", u)] + ([dve_moved.at(self.tag, "pt", u)] if self.kt > 4 else [])

        def attend_pe(pe, a):
            tag = a.tag
            for step in range(a.units + 3):
                u = step
                if u < a.units:
                    if u >= 2:
                        pe.wait_ge(*(fused.at(tag, "biased", u - 2) if a.bias else exped.at(tag, u - 2)))
                    for k0 in range(0, a.keys, 512):
                        kn = min(512, a.keys - k0)
                        lhs, rhs = a.score(u, k0, kn)
                        mm = pe.matmul(ps[:, 2 * (u % 2) + k0 // 512, 0:kn], lhs, rhs, start=True, stop=True)
                    mm.then_inc(*scored.on(tag, u))
                u = step - 2
                if 0 <= u < a.units:
                    pe.wait_ge(*scaled.at(tag, u))
                    if u >= 1:
                        for w in a.copies(u - 1):
                            pe.wait_ge(*w)
                    for t in range(a.kt):
                        mm = pe.transpose(ps[:, 4 + t // 4, (t % 4) * P:(t % 4 + 1) * P],
                                          a.p[:, u % 3, t * P:(t + 1) * P], ident)
                        if t == min(3, a.kt - 1):
                            mm.then_inc(*turned.on(tag, u, 0))
                        elif t == a.kt - 1:
                            mm.then_inc(*turned.on(tag, u, 1))
                u = step - 3
                if u >= 0 and u % a.per_head == a.per_head - 1:
                    hd = u // a.per_head
                    for w in a.copies(u):
                        pe.wait_ge(*w)
                    if hd >= 2:
                        pe.wait_ge(*dve_moved.at(tag, "out", hd - 2))
                    products = a.mix(hd)
                    for o, lhs, rhs, start, stop in products:
                        mm = pe.matmul(o, lhs, rhs, start=start, stop=stop)
                    mm.then_inc(*attended.on(tag, hd))

        def attend_act(act, a):
            tag = a.tag
            for step in range(a.units + 2):
                u = step
                if u < a.units:
                    act.wait_ge(*maxed.at(tag, "negated", u))
                    if u >= 3:
                        act.wait_ge(*turned.at(tag, u - 3, 1 if a.kt > 4 else 0))
                    nc.scalar.activation(a.p[:, u % 3, 0:a.keys], a.p[:, u % 3, 0:a.keys] if a.bias else a.s(u),
                                         ACT.Exp, bias=stat[:, u % 8, 1:2], scale=1.0 if a.bias else a.scale,
                                         accum_out=stat[:, u % 8, 2:3]).then_inc(*exped.on(tag, u))
                u = step - 2
                if u >= 0:
                    act.wait_ge(*turned.at(tag, u, 0))
                    hd, q = u // a.per_head, u % a.per_head
                    if hd >= 2 and q == 0:
                        act.wait_ge(*attended.at(tag, hd - 2))
                    n = min(4, a.kt)
                    nc.scalar.activation(a.pt[:, hd % 2, 0:n, q * P:(q + 1) * P],
                                         ps[:, 4, 0:n * P].rearrange("p (t q) -> p t q", t=n), ACT.Copy)\
                        .then_inc(*act_moved.on(tag, "pt", u))

        def attend_dve(dve, a):
            tag = a.tag
            for step in range(a.units + 3):
                u = step
                if u < a.units:
                    s, st = a.s(u), stat[:, u % 8]
                    dve.wait_ge(*scored.at(tag, u))
                    if a.bias:
                        if u >= 3:
                            dve.wait_ge(*turned.at(tag, u - 3, 0))
                        near, mask = a.bias(u)
                        buf = a.p[:, u % 3, 0:a.keys]
                        nc.vector.scalar_tensor_tensor(out=buf.rearrange("p (w r) -> p w r", w=WIN),
                                                       in0=s.rearrange("p (w r) -> p w r", w=WIN), scalar=a.scale,
                                                       in1=near, op0=ALU.mult, op1=ALU.add)\
                            .then_inc(*fused.on(tag, "biased", u))
                        dve.wait_ge(*fused.at(tag, "biased", u))
                        nc.vector.tensor_tensor(buf, buf, mask, ALU.add).then_inc(*fused.on(tag, "masked", u))
                        dve.wait_ge(*fused.at(tag, "masked", u))
                        s = buf
                    if u >= 8:
                        dve.wait_ge(*scaled.at(tag, u - 8))
                    nc.vector.reduce_max(st[:, 0:1], s, AX).then_inc(*maxed.on(tag, "max", u))
                    dve.wait_ge(*maxed.at(tag, "max", u))
                    nc.vector.tensor_scalar(st[:, 1:2], st[:, 0:1], -1.0 if a.bias else -a.scale, None, ALU.mult)\
                        .then_inc(*maxed.on(tag, "negated", u))
                u = step - 1
                if 0 <= u < a.units:
                    st = stat[:, u % 8]
                    dve.wait_ge(*exped.at(tag, u))
                    nc.vector.reciprocal(st[:, 3:4], st[:, 2:3]).then_inc(*inverted.on(tag, u))
                    dve.wait_ge(*inverted.at(tag, u))
                    nc.vector.tensor_scalar(a.p[:, u % 3, 0:a.keys], a.p[:, u % 3, 0:a.keys], st[:, 3:4], None,
                                            ALU.mult).then_inc(*scaled.on(tag, u))
                u = step - 2
                if 0 <= u < a.units and a.kt > 4:
                    dve.wait_ge(*turned.at(tag, u, 1))
                    hd, q = u // a.per_head, u % a.per_head
                    if hd >= 2 and q == 0:
                        dve.wait_ge(*attended.at(tag, hd - 2))
                    nc.vector.tensor_copy(a.pt[:, hd % 2, 4:6, q * P:(q + 1) * P],
                                          ps[:, 5, 0:2 * P].rearrange("p (t q) -> p t q", t=2))\
                        .then_inc(*dve_moved.on(tag, "pt", u))
                u = step - 3
                if u >= 0 and u % a.per_head == a.per_head - 1:
                    hd = u // a.per_head
                    dve.wait_ge(*attended.at(tag, hd))
                    d, s = a.dest(hd)
                    nc.vector.tensor_copy(d, s).then_inc(*dve_moved.on(tag, "out", hd))

        WIN_AT = [min(max(16 * t - 8, 0), GRID_W - WIN) for t in range(4)]

        def na_score(u, k0, kn):
            hd, t = u // 4, u % 4
            q0 = (hd % 2) * 64
            k0 = WIN_AT[t] * GRID_H
            return na_q[q0:q0 + 64, hd // 2, t * P:(t + 1) * P], na_k[q0:q0 + 64, hd // 2, k0:k0 + 256]

        def na_bias(u):
            hd, t = u // 4, u % 4
            shift = WIN_AT[t] - 16 * t + 15 + 1
            run = rpb[:, hd, shift:shift + 1]
            near = spread(run, (1, WIN), (31, GRID_H))
            kind = {0: 0, 1: 1, 2: 1, 3: 2}[t]
            return near, cc("mask")[:, kind * 256:(kind + 1) * 256]

        def na_mix(hd):
            q0 = (hd % 2) * 64
            return [(ps[q0:q0 + 64, 6 + hd % 2, t * P:(t + 1) * P], na_win[:, 2 * t + kt, hd * 64:(hd + 1) * 64],
                     b1_pt[:, hd % 2, kt, t * P:(t + 1) * P], kt == 0, kt == 1) for t in range(4) for kt in range(2)]

        def na_dest(hd):
            q0 = (hd % 2) * 64
            return (na_o[q0:q0 + 64, hd // 2, :].rearrange("p (r w) -> p r w", w=GRID_W),
                    ps[q0:q0 + 64, 6 + hd % 2, :].rearrange("p (w r) -> p r w", r=GRID_H))

        near_attention = Attention("na", NA_HEADS, 4, 256, 64 ** -0.5, na_score, na_mix, na_dest, b1_p, b1_pt, na_bias)
        memory_attention = Attention(
            "xa", XA_HEADS, 4, 256, 128 ** -0.5,
            lambda u, k0, kn: (xa_q[:, u // 4, (u % 4) * P:(u % 4 + 1) * P], xa_k[:, u // 4, :]),
            lambda hd: [(ps[:, 6 + hd % 2, :], xa_v[:, kt, hd * P:(hd + 1) * P], b1_pt[:, hd % 2, kt, :], kt == 0, kt == 1)
                        for kt in range(2)],
            lambda hd: (xa_o[:, hd, :], ps[:, 6 + hd % 2, :]), b1_p, b1_pt)

        def head_parts(kind, hd):
            if kind == "mla":
                return mla_q[0:96, hd, :], mla_k[0:96, hd, :], hd * 64, (h, hd // 2, hd % 2)
            if kind == "diff":
                a = (hd % 4) * 32
                return (diff_q[a:a + 32, hd // 4, :], diff_k[a:a + 32, hd // 4, :], 256 + (hd // 2) * 64,
                        ((out_1, out_2)[hd % 2], hd // 4, (hd // 2) % 2))
            a = (hd // 4) * 64
            return gqa_q[a:a + 64, hd % 4, :], gqa_k[a:a + 64, :], 512 + (hd // 4) * 64, (h, 4 + hd // 2, hd % 2)

        def block2_attention(l, kind, heads, scale, on_context):
            q0, per_head = (SEQ, 2) if on_context else (0, 4)
            key0, keys = (SEQ, CTX) if on_context else (0, ALL)
            width = per_head * P

            def score(u, k0, kn):
                q, k, _, _ = head_parts(kind, u // per_head)
                a = q0 + (u % per_head) * P
                return q[:, a:a + P], k[:, key0 + k0:key0 + k0 + kn]

            def mix(hd):
                _, _, v0, (_, _, half) = head_parts(kind, hd)
                o = ps[half * 64:half * 64 + 64, 6 + hd % 2, 0:width]
                n = keys // P
                return [(o, val[:, key0 // P + t, v0:v0 + 64], prob_t[:, hd % 2, t, 0:width], t == 0, t == n - 1)
                        for t in range(n)]

            def dest(hd):
                _, _, _, (buf, tile, half) = head_parts(kind, hd)
                a = half * 64
                return buf[a:a + 64, tile, q0:q0 + width], ps[a:a + 64, 6 + hd % 2, 0:width]
            return Attention((kind, l, on_context), heads, per_head, keys, scale, score, mix, dest, prob, prob_t)

        attentions = {l: [block2_attention(l, kind, n, s, c) for c in ([False, True] if l < LAYERS - 1 else [False])
                          for kind, n, s in (("mla", MLA_H, 96 ** -0.5), ("diff", 2 * DIFF_H, 32 ** -0.5),
                                             ("gqa", GQA_H, 64 ** -0.5))] for l in range(LAYERS)}

        rope1 = [(ret_q[:, t, :], 0, P, "rot128", trig128[:, 0, :], trig128[:, 1, :]) for t in range(4)]
        rope1 += [(ret_k[:, t, :], 0, P, "rot128", trig128[:, 0, :], trig128[:, 1, :]) for t in range(4)]

        def full(kind, buf):
            return buf, 0, P, "rot64" if kind == "large" else "rot32", *(trig[:, (0 if kind == "large" else 2) + j, :]
                                                                         for j in range(2))

        rope2 = [full("large", gqa_q[:, t, 0:SEQ]) for t in range(4)] + [full("large", gqa_k[:, 0:SEQ])]
        rope2 += [full("small", b[:, t, 0:SEQ]) for b in (diff_q, diff_k) for t in range(2)]
        rope2 += [(b, 64, 32, "rot32", trig[:, 2, :], trig[:, 3, :])
                  for b in [k_pe[:, 0:SEQ]] + [mla_q[:, t, 0:SEQ] for t in range(4)]]

        def rope_pe(pe, tag, jobs):
            for j, (a, p0, n, m, c, s) in enumerate(jobs):
                if j >= 8:
                    pe.wait_ge(*roped.at(tag, "sine", j - 8))
                pe.matmul(ps[p0:p0 + n, j % 8, :], cc(m)[p0:p0 + n, p0:p0 + n], a[p0:p0 + n], start=True, stop=True)\
                    .then_inc(*multiplied.on(tag, j))

        def rope_dve(dve, tag, jobs):
            for j, (a, p0, n, m, c, s) in enumerate(jobs):
                a = a[p0:p0 + n]
                t = tmp[p0:p0 + n, j % 4, :]
                dve.wait_ge(*multiplied.at(tag, j))
                if j >= 4:
                    dve.wait_ge(*roped.at(tag, "sum", j - 4))
                nc.vector.tensor_tensor(t, ps[p0:p0 + n, j % 8, :], s[p0:p0 + n], ALU.mult).then_inc(*roped.on(tag, "sine", j))
                nc.vector.tensor_tensor(a, a, c[p0:p0 + n], ALU.mult).then_inc(*roped.on(tag, "cosine", j))
                dve.wait_ge(*roped.at(tag, "cosine", j))
                nc.vector.tensor_tensor(a, a, t, ALU.add).then_inc(*roped.on(tag, "sum", j))

        def to_tiles(*bufs):
            flat = [b[:, t, :] for b in bufs for t in range(b.shape[1])]
            return lambda m, c0, cn, s: (flat[m][:, c0:c0 + cn], s)

        def na_store(m, c0, cn, s):
            d = (na_q, na_k, na_v)[m // 4][:, m % 4, :]
            return d.rearrange("p (w r) -> p r w", r=GRID_H), s.rearrange("p (r w) -> p r w", w=GRID_W)

        def in2_store(m, c0, cn, s):
            flat = [q_low[:, 0], q_low[:, 1], diff_q[:, 0], diff_q[:, 1]] + [gqa_q[:, t] for t in range(4)] + \
                   [kv_low, k_pe, diff_k[:, 0], diff_k[:, 1], gqa_k]
            return flat[m][:, c0:c0 + cn], s

        def seq_only(m):
            return SEQ_ONLY

        def in2_pieces(l):
            return lambda m: SEQ_ONLY if m < 8 and l == LAYERS - 1 else BOTH

        plain = {
            "ret_qk": (8, KT, hs, seq_only, to_tiles(ret_q, ret_k)),
            "na_in": (12, KT, hs, seq_only, na_store),
            "xa_k": (4, KT, lambda k, c0, cn: h[:, k, SEQ:ALL], lambda m: [(0, CTX)], to_tiles(xa_k)),
            "xa_q": (4, KT, hs, seq_only, to_tiles(xa_q)),
        }
        for l in range(LAYERS):
            own = (lambda m: BOTH) if l < LAYERS - 1 else seq_only
            plain["in2", l] = (13, KT, hs, in2_pieces(l), in2_store)
            plain["out2", l] = (KT, KT, hs, own, to_tiles(attn_y))
            plain["down", l] = (KT, HT, lambda k, c0, cn: ffn_hid[:, k, c0:c0 + cn], own, to_tiles(ffn_y))

        def run_plain(e, which, tag):
            ms, K, rhs, pieces_of, dst = plain[tag]
            if which == "pe":
                project_pe(e, tag, ms, K, rhs, pieces_of)
            else:
                project_move(e, which, tag, ms, pieces_of, dst)

        def h_tokens(c):
            return lambda k, t: h[:, k, c + t * P:c + (t + 1) * P]

        value_stages = {
            "ret_v0": (4, h_tokens(0), 4, lambda t: ret_v[:, t, 0:512]),
            "ret_v1": (4, h_tokens(0), 4, lambda t: ret_v[:, t, 512:1024]),
            "xa_v": (2, h_tokens(SEQ), 4, lambda t: xa_v[:, t, :]),
        }
        for l in range(LAYERS):
            value_stages["diff_v", l] = (6, h_tokens(0), 2, lambda t: val[:, t, 256:512])
            value_stages["gqa_v", l] = (6, h_tokens(0), 1, lambda t: val[:, t, 512:640])

        def run_values(e, which, tag):
            n, lhs, nb, dst = value_stages[tag]
            if which == "pe":
                values_pe(e, tag, n, lhs, nb)
            else:
                values_move(e, which, tag, n, dst, nb * P)

        qb = w_small[:, 0:768].rearrange("p (k n) -> p k n", k=2)
        kvb = w_small[:, 768:1280]

        def lifts(l):
            own = BOTH if l < LAYERS - 1 else SEQ_ONLY
            jobs = []
            for hd in range(MLA_H):
                for c0, cn in own:
                    jobs.append((96, cn, [(qb[:, k, hd * 96:hd * 96 + 96], q_low[:, k, c0:c0 + cn]) for k in range(2)],
                                 mla_q[0:96, hd, c0:c0 + cn]))
                for c0, cn in BOTH:
                    jobs.append((64, cn, [(kvb[:, hd * P:hd * P + 64], kv_low[:, c0:c0 + cn])], mla_k[0:64, hd, c0:c0 + cn]))
            v = kvb.rearrange("p (h n) -> p h n", h=MLA_H)[:, :, 64:128]
            for t in range(6):
                jobs.append((P, 256, [(kv_low[:, t * P:(t + 1) * P], v)], val[:, t, 0:256]))
            return jobs

        def lift_pe(pe, l):
            jobs = lifts(l)
            for g, (n, cn, products, _) in enumerate(jobs):
                if g >= 8:
                    pe.wait_ge(*moved_at(("lift", l), g - 8))
                for k, (lhs, rhs) in enumerate(products):
                    mm = pe.matmul(ps[0:n, g % 8, 0:cn], lhs, rhs, start=(k == 0), stop=(k == len(products) - 1))
                mm.then_inc(*multiplied.on("lift", l, g))

        def lift_move(e, which, l):
            jobs = lifts(l)
            for g, (n, cn, _, d) in enumerate(jobs):
                if g % 2 != which:
                    continue
                e.wait_ge(*multiplied.at("lift", l, g))
                also = ("lift done", l) if g >= len(jobs) - 2 else None
                s = ps[0:n, g % 8, 0:cn]
                if which == 0:
                    nc.scalar.activation(d, s, ACT.Copy).then_inc(*act_moved.on(("lift", l), g, also=also))
                else:
                    nc.vector.tensor_copy(d, s).then_inc(*dve_moved.on(("lift", l), g, also=also))

        FFN_LOOP = HT // RING

        @block.tensor
        def _(pe):
            def begin():
                stage("pe", pe)

            pe.wait_ge(inputs_loaded, 16 * 8)
            norm_pe(pe, "norm_x", job_of["norm_x"])
            begin()
            norm_pe(pe, "norm_mem", job_of["norm_mem"])
            begin()
            run_plain(pe, "pe", "ret_qk")
            begin()
            run_values(pe, "pe", "ret_v0")
            begin()
            run_values(pe, "pe", "ret_v1")
            begin()
            rope_pe(pe, "rope1", rope1)
            begin()
            for hd in range(RET_HEADS):
                for jt in range(4):
                    if hd:
                        pe.wait_ge(*fused.at("decayed", hd - 1, jt))
                    pe.matmul(ps[:, jt, :], ret_k[:, hd, jt * P:(jt + 1) * P], ret_q[:, hd, :], start=True, stop=True)\
                        .then_inc(*scored.on("ret", hd, jt))
                for e in range(2):
                    if hd:
                        pe.wait_ge(*act_moved.at("ret_y", hd - 1, e))
                    for jt in range(4):
                        pe.wait_ge(*fused.at("decayed", hd, jt))
                        mm = pe.matmul(ps[:, 4 + e, :], ret_v[:, jt, hd * 256 + e * P:hd * 256 + (e + 1) * P],
                                       ret_s[:, jt, :], start=(jt == 0), stop=(jt == 3))
                    mm.then_inc(*attended.on("ret", hd, e))
            begin()
            for hd in range(RET_HEADS):
                for e in range(2):
                    mm = pe.matmul(ps[:, hd, :], ones, ret_y[:, 2 * hd + e, :], start=(e == 0), stop=(e == 1))
                mm.then_inc(*summed.on("ret_mean", hd))
            begin()
            norm_pe(pe, "ret_norm", job_of["ret_norm"])
            begin()
            for m in range(8):
                group(pe, ("ret_gate", m), [m], hs, KT, SEQ_ONLY)
            begin()
            branch_pe(pe, "ret_out", 8, lambda k, c0, cn: ret_y[:, k, :])
            begin()
            run_plain(pe, "pe", "na_in")
            begin()
            for w in range(8):
                k0 = WIN_AT[w // 2] * GRID_H + (w % 2) * P
                for c in range(4):
                    mm = pe.transpose(ps[:, w, c * P:(c + 1) * P], na_v[:, c, k0:k0 + P], ident)
                mm.then_inc(*turned.on("windows", w))
            begin()
            attend_pe(pe, near_attention)
            begin()
            branch_pe(pe, "na_out", 4, lambda k, c0, cn: na_o[:, k, :])
            begin()
            run_plain(pe, "pe", "xa_k")
            begin()
            run_values(pe, "pe", "xa_v")
            begin()
            run_plain(pe, "pe", "xa_q")
            begin()
            attend_pe(pe, memory_attention)
            begin()
            branch_pe(pe, "xa_out", 4, lambda k, c0, cn: xa_o[:, k, :])
            begin()
            for m in range(KT):
                group(pe, ("mix_out", m), [m], lambda k, c0, cn: mixed_sum[:, k, :], KT, SEQ_ONLY)
            begin()
            norm_pe(pe, "norm_moe", job_of["norm_moe"])
            begin()
            for t in range(4):
                for k in range(KT):
                    mm = pe.matmul(ps[:, 0, t * 20:(t + 1) * 20], h[:, k, t * P:(t + 1) * P], w_router[:, k, :],
                                   start=(k == 0), stop=(k == KT - 1))
            mm.then_inc(*multiplied.on("logits"))
            for e in range(EXPERTS):
                pe.wait_ge(*small.at("diagonal", e, 3))
                if e >= 4:
                    pe.wait_ge(*act_moved.at("comb", e - 4))
                pe.matmul(ps[:, 1 + e % 4, :], ones, tmp[:, e % 4, :], start=True, stop=True)\
                    .then_inc(*multiplied.on("comb", e))
            begin()
            assert chunks.block == MOE_FIRST * BLOCKS
            with repeated(pe, EXPERTS, signals["pe"]) as i:
                before = chunks.block
                for f in range(4):
                    for b, what in enumerate(("gate", "up")):
                        bank = 2 * f + b
                        m = (bank - 1) % 8
                        pe.wait_ge(*dve_moved.at("moe", m, i=i - 1))
                        group(pe, ("moe", what, f), [bank], hs, KT, SEQ_ONLY, i=i)
                pe.wait_ge(*gated.at("moe", 0, i=i))
                for a in range(ADA_PER_EXPERT):
                    for k in range(KT):
                        w = take(pe, i)
                        mm = pe.matmul(ps[:, 0, 2 * a:2 * a + 2], w, silu_c[:, k, :], start=(k == 0), stop=(k == KT - 1))
                        also = chunk_end()
                        if a == ADA_PER_EXPERT - 1 and k == KT - 1:
                            mm.then_inc(*streamed.on("ada", also=also))
                        elif also:
                            mm.then_inc(*streamed.on(*also))
                for m in range(KT):
                    bank = (m + 1) % 8
                    if m == 0:
                        pe.wait_ge(*fused.at("moe", "hid", 3, i=i))
                    if m == KT - 1:
                        pe.wait_ge(*dve_moved.at("ada", i=i))
                    group(pe, ("moe", "down", m), [bank], lambda k, c0, cn: hid[:, k, :], 4, SEQ_ONLY, i=i)
                assert chunks.block - before == MOE_CHUNKS * BLOCKS
            chunks.block += MOE_CHUNKS * BLOCKS * (EXPERTS - 1)
            begin()
            norm_pe(pe, "norm_first", job_of["norm_first"])
            begin()
            for l in range(LAYERS):
                own = BOTH if l < LAYERS - 1 else SEQ_ONLY
                pe.wait_ge(*small.at("lambda products", l))
                pe.matmul(ps[:, 7, 0:2], ones[0:32, :], cols[0:32, 2:4], start=True, stop=True)\
                    .then_inc(*multiplied.on("lambda", l))
                norm_pe(pe, ("attn_pre", l), job_of["attn_pre", l])
                begin()
                run_plain(pe, "pe", ("in2", l))
                begin()
                run_values(pe, "pe", ("diff_v", l))
                begin()
                run_values(pe, "pe", ("gqa_v", l))
                begin()
                norm_pe(pe, ("low", l), job_of["low", l])
                begin()
                pe.wait_ge(late_loaded, 16 * (2 + l))
                lift_pe(pe, l)
                begin()
                rope_pe(pe, ("rope2", l), rope2)
                begin()
                for a in attentions[l]:
                    attend_pe(pe, a)
                    begin()
                begin()
                norm_pe(pe, ("diff", l), job_of["diff", l])
                begin()
                run_plain(pe, "pe", ("out2", l))
                begin()
                norm_pe(pe, ("attn_post", l), job_of["attn_post", l])
                begin()
                norm_pe(pe, ("ffn_pre", l), job_of["ffn_pre", l])
                begin()
                n = len(own)
                for m in range(HT):
                    for b, what in enumerate(("gate", "up")):
                        if m >= 2:
                            for pi in range(n):
                                pe.wait_ge(*(gated if b == 0 else fused).at("ffn", l, m - 2, pi))
                        group(pe, ("ffn", l, what, m), [4 * (m % 2) + 2 * b + pi for pi in range(n)], hs, KT, own)
                begin()
                run_plain(pe, "pe", ("down", l))
                begin()
                norm_pe(pe, ("ffn_post", l), job_of["ffn_post", l])
                begin()
            assert chunks.block == n_chunks * BLOCKS, (chunks.block, n_chunks)

        @block.scalar
        def _(act):
            def begin():
                stage("act", act)

            act.wait_ge(inputs_loaded, 16 * 8)
            act.wait_ge(*small.at("epsilons"))
            norm_act(act, "norm_x", job_of["norm_x"])
            begin()
            norm_act(act, "norm_mem", job_of["norm_mem"])
            begin()
            nc.scalar.activation(silu_c[:].rearrange("p a b -> p (a b)"), pc("c", 0, 16), ACT.Silu).then_inc(*act_moved.on("silu_c"))
            nc.scalar.activation(route[:, 0:8], pc("decay", 0, 8), ACT.Abs).then_inc(*act_moved.on("abs"))
            act.wait_ge(*act_moved.at("abs"))
            nc.scalar.activation(route[:, 8:16], route[:, 0:8], ACT.Exp, scale=-1.0).then_inc(*exped.on("decay"))
            act.wait_ge(*small.at("one plus"))
            nc.scalar.activation(route[:, 24:32], route[:, 16:24], ACT.Ln).then_inc(*exped.on("decay log"))
            run_plain(act, 0, "ret_qk")
            begin()
            run_values(act, 0, "ret_v0")
            begin()
            run_values(act, 0, "ret_v1")
            begin()
            begin()
            for hd in range(RET_HEADS):
                act.wait_ge(*fused.at("exponent", hd))
                if hd >= 2:
                    act.wait_ge(*fused.at("decayed", hd - 2, 3))
                nc.scalar.activation(ret_e[:, hd % 2, :], ret_t, ACT.Exp).then_inc(*exped.on("ret", hd))
                for e in range(2):
                    act.wait_ge(*attended.at("ret", hd, e))
                    nc.scalar.activation(ret_y[:, 2 * hd + e, :], ps[:, 4 + e, :], ACT.Copy).then_inc(*act_moved.on("ret_y", hd, e))
            begin()
            begin()
            norm_act(act, "ret_norm", job_of["ret_norm"])
            begin()
            for m in range(8):
                act.wait_ge(*streamed.at("ret_gate", m, 0))
                nc.scalar.activation(tmp[:, m, :], ps[:, m, :], ACT.Silu).then_inc(*gated.on("ret_gate", m))
            begin()
            branch_act(act, "ret_out")
            begin()
            run_plain(act, 0, "na_in")
            begin()
            for w in range(0, 8, 2):
                act.wait_ge(*turned.at("windows", w))
                nc.scalar.activation(na_win[:, w, :], ps[:, w, :], ACT.Copy).then_inc(*act_moved.on("windows", w))
            begin()
            attend_act(act, near_attention)
            begin()
            branch_act(act, "na_out")
            begin()
            run_plain(act, 0, "xa_k")
            begin()
            run_values(act, 0, "xa_v")
            begin()
            run_plain(act, 0, "xa_q")
            begin()
            attend_act(act, memory_attention)
            begin()
            branch_act(act, "xa_out")
            begin()
            begin()
            norm_act(act, "norm_moe", job_of["norm_moe"])
            begin()
            act.wait_ge(*small.at("group distance"))
            nc.scalar.activation(R["ge"], R["gd"], ACT.Exp).then_inc(*exped.on("groups"))
            act.wait_ge(*small.at("expert distance"))
            nc.scalar.activation(R["ee"], R["ed"], ACT.Exp).then_inc(*exped.on("experts"))
            for e in range(EXPERTS):
                act.wait_ge(*multiplied.at("comb", e))
                nc.scalar.activation(comb[:, e, :], ps[:, 1 + e % 4, :], ACT.Copy).then_inc(*act_moved.on("comb", e))
            begin()
            with repeated(act, EXPERTS, signals["act"]) as i:
                for f in range(4):
                    act.wait_ge(*streamed.at("moe", "gate", f, 0, i=i))
                    if f >= 2:
                        act.wait_ge(*fused.at("moe", "up", f - 2, i=i))
                    nc.scalar.activation(tmp[:, f % 2, :], ps[:, 2 * f, :], ACT.Silu).then_inc(*gated.on("moe", f))
            begin()
            norm_act(act, "norm_first", job_of["norm_first"])
            begin()
            for l in range(LAYERS):
                own = BOTH if l < LAYERS - 1 else SEQ_ONLY
                act.wait_ge(*multiplied.at("lambda", l))
                nc.scalar.activation(cols[:, 4:6], ps[:, 7, 0:2], ACT.Exp).then_inc(*exped.on("lambda", l))
                if l == 0:
                    act.wait_ge(context_loaded, 16)
                norm_act(act, ("attn_pre", l), job_of["attn_pre", l])
                begin()
                run_plain(act, 0, ("in2", l))
                begin()
                run_values(act, 0, ("diff_v", l))
                begin()
                run_values(act, 0, ("gqa_v", l))
                begin()
                norm_act(act, ("low", l), job_of["low", l])
                begin()
                lift_move(act, 0, l)
                begin()
                begin()
                for a in attentions[l]:
                    attend_act(act, a)
                    begin()
                begin()
                norm_act(act, ("diff", l), job_of["diff", l])
                begin()
                run_plain(act, 0, ("out2", l))
                begin()
                norm_act(act, ("attn_post", l), job_of["attn_post", l])
                begin()
                norm_act(act, ("ffn_pre", l), job_of["ffn_pre", l])
                begin()
                for m in range(HT):
                    for pi, (c0, cn) in enumerate(own):
                        act.wait_ge(*streamed.at("ffn", l, "gate", m, pi))
                        if m >= 2:
                            act.wait_ge(*fused.at("ffn", l, m - 2, pi))
                        nc.scalar.activation(tmp[:, 2 * (m % 2) + pi, 0:cn], ps[:, 4 * (m % 2) + pi, 0:cn], ACT.Silu)\
                            .then_inc(*gated.on("ffn", l, m, pi))
                begin()
                run_plain(act, 0, ("down", l))
                begin()
                norm_act(act, ("ffn_post", l), job_of["ffn_post", l])
                begin()

        @block.vector
        def _(dve):
            def begin():
                stage("dve", dve)

            def then(instruction, *key):
                instruction.then_inc(*small.on(*key))
                dve.wait_ge(*small.at(*key))

            nc.vector.memset(cols[:, 0:1], 1e-6).then_inc(*small.on("epsilon norm"))
            nc.vector.memset(cols[:, 1:2], 1e-5).then_inc(*small.on("epsilons"))
            dve.wait_ge(inputs_loaded, 16 * 8)
            norm_dve(dve, "norm_x", job_of["norm_x"])
            begin()
            norm_dve(dve, "norm_mem", job_of["norm_mem"])
            begin()
            e_, one_e, ln_e, d_, eq_, t_ = (route[:, a:a + 8] for a in (8, 16, 24, 32, 40, 48))
            dve.wait_ge(*exped.at("decay"))
            nc.vector.tensor_scalar(one_e, e_, 1.0, None, ALU.add).then_inc(*small.on("one plus"))
            dve.wait_ge(*small.at("one plus"))
            then(nc.vector.tensor_scalar(d_, one_e, -1.0, None, ALU.add), "lg", 0)
            then(nc.vector.tensor_scalar(eq_, d_, 0.0, None, ALU.is_equal), "lg", 1)
            then(nc.vector.tensor_tensor(d_, d_, eq_, ALU.add), "lg", 2)
            then(nc.vector.reciprocal(d_, d_), "lg", 3)
            dve.wait_ge(*exped.at("decay log"))
            then(nc.vector.tensor_tensor(ln_e, ln_e, eq_, ALU.add), "lg", 4)
            then(nc.vector.tensor_tensor(d_, d_, e_, ALU.mult), "lg", 5)
            then(nc.vector.tensor_tensor(d_, d_, ln_e, ALU.mult), "lg", 6)
            then(nc.vector.tensor_scalar(t_, pc("decay", 0, 8), 0.0, None, ALU.min), "lg", 7)
            then(nc.vector.tensor_tensor(route[:, 56:64], t_, d_, ALU.subtract), "lg", 8)
            lg = route[:, 56:64]
            run_plain(dve, 1, "ret_qk")
            begin()
            run_values(dve, 1, "ret_v0")
            begin()
            run_values(dve, 1, "ret_v1")
            begin()
            rope_dve(dve, "rope1", rope1)
            begin()
            for hd in range(RET_HEADS):
                if hd:
                    dve.wait_ge(*exped.at("ret", hd - 1))
                nc.vector.tensor_scalar(ret_t, dist[:, 1, :], lg[:, 4 + hd:5 + hd], None, ALU.mult)\
                    .then_inc(*fused.on("backward", hd))
                dve.wait_ge(*fused.at("backward", hd))
                nc.vector.scalar_tensor_tensor(out=ret_t, in0=dist[:, 0, :], scalar=lg[:, hd:hd + 1], in1=ret_t,
                                               op0=ALU.mult, op1=ALU.add).then_inc(*fused.on("exponent", hd))
                dve.wait_ge(*exped.at("ret", hd))
                for jt in range(4):
                    dve.wait_ge(*scored.at("ret", hd, jt))
                    if hd:
                        dve.wait_ge(*attended.at("ret", hd - 1, 1))
                    a = 3 * P - jt * P
                    nc.vector.scalar_tensor_tensor(out=ret_s[:, jt, :], in0=ps[:, jt, :], scalar=128 ** -0.5,
                                                   in1=ret_e[:, hd % 2, a:a + SEQ], op0=ALU.mult, op1=ALU.mult)\
                        .then_inc(*fused.on("decayed", hd, jt))
            begin()
            for hd in range(RET_HEADS):
                dve.wait_ge(*summed.at("ret_mean", hd))
                for e in range(2):
                    nc.vector.scalar_tensor_tensor(out=ret_y[:, 2 * hd + e, :], in0=ps[:, hd, :], scalar=-1.0 / 256,
                                                   in1=ret_y[:, 2 * hd + e, :], op0=ALU.mult, op1=ALU.add)\
                        .then_inc(*fused.on("centred", hd, e))
            begin()
            norm_dve(dve, "ret_norm", job_of["ret_norm"])
            begin()
            for m in range(8):
                dve.wait_ge(*gated.at("ret_gate", m))
                nc.vector.tensor_tensor(ret_y[:, m, :], ret_y[:, m, :], tmp[:, m, :], ALU.mult).then_inc(*fused.on("ret_gated", m))
            begin()
            branch_dve(dve, "ret_out", True)
            begin()
            run_plain(dve, 1, "na_in")
            begin()
            for w in range(1, 8, 2):
                dve.wait_ge(*turned.at("windows", w))
                nc.vector.tensor_copy(na_win[:, w, :], ps[:, w, :]).then_inc(*dve_moved.on("windows", w))
            begin()
            attend_dve(dve, near_attention)
            begin()
            branch_dve(dve, "na_out", False)
            begin()
            run_plain(dve, 1, "xa_k")
            begin()
            run_values(dve, 1, "xa_v")
            begin()
            run_plain(dve, 1, "xa_q")
            begin()
            attend_dve(dve, memory_attention)
            begin()
            branch_dve(dve, "xa_out", False)
            begin()
            for m in range(KT):
                dve.wait_ge(*streamed.at("mix_out", m, 0))
                nc.vector.tensor_tensor(x[:, m, 0:SEQ], x[:, m, 0:SEQ], ps[:, m, :], ALU.add).then_inc(*dve_moved.on("mix_out", m))
            begin()
            norm_dve(dve, "norm_moe", job_of["norm_moe"])
            begin()
            def wide(ap):
                return spread(ap, (1, 4), (0, 4))

            def first_best(hit, out_, *key):
                then(nc.vector.tensor_tensor(R["cand"], hit, R["rank"], ALU.mult), *key, "rank")
                then(nc.vector.reduce_max(R["best"], R["cand"], AX), *key, "best")
                then(nc.vector.tensor_tensor(out_, R["cand"], wide(R["best"]), ALU.is_equal), *key, "hit")

            dve.wait_ge(*multiplied.at("logits"))
            then(nc.vector.tensor_tensor(R["lg"], ps[:, 0, 0:80].rearrange("p (t n) -> p t n", t=4),
                                         pc("router_bias", 0, 80).rearrange("p (t n) -> p t n", t=4), ALU.add), "logits")
            gl, el = R["lg"][:, :, 0:4], R["lg"][:, :, 4:20]
            then(nc.vector.reduce_max(R["gm"], gl, AX), "group max")
            then(nc.vector.tensor_tensor(R["gd"], gl, wide(R["gm"]), ALU.subtract), "group distance")
            then(nc.vector.tensor_scalar(R["eq"], R["gd"], 0.0, None, ALU.is_ge), "group hits")
            first_best(R["eq"], R["g1"], "group")
            dve.wait_ge(*exped.at("groups"))
            then(nc.vector.reduce_sum(R["gw"], R["ge"], axis=AX), "group sum")
            then(nc.vector.reciprocal(R["gw"], R["gw"]), "group weight")
            g1_wide = spread(R["g1"], (4, 4), (1, 4), (0, 4))
            then(nc.vector.tensor_tensor(R["sel"], el.rearrange("p t (g e) -> p t g e", g=4), g1_wide, ALU.mult), "chosen")
            sel_a = R["sel"]
            then(nc.vector.reduce_sum(R["ig"], sel_a.rearrange("p t g e -> p t e g"), axis=AX), "in group")
            then(nc.vector.reduce_max(R["em"], R["ig"], AX), "expert max")
            then(nc.vector.tensor_tensor(R["ed"], R["ig"], wide(R["em"]), ALU.subtract), "expert distance")
            then(nc.vector.tensor_scalar(R["eq"], R["ed"], 0.0, None, ALU.is_ge), "expert hits")
            first_best(R["eq"], R["o1"], "first")
            then(nc.vector.scalar_tensor_tensor(out=R["e2"], in0=R["o1"], scalar=-BIG, in1=R["ed"], op0=ALU.mult,
                                                op1=ALU.add), "without the first")
            then(nc.vector.reduce_max(R["em"], R["e2"], AX), "second max")
            then(nc.vector.tensor_tensor(R["eq"], R["e2"], wide(R["em"]), ALU.is_equal), "second hits")
            first_best(R["eq"], R["o2"], "second")
            then(nc.vector.tensor_tensor(R["o1"], R["o1"], R["o2"], ALU.add), "both")
            dve.wait_ge(*exped.at("experts"))
            then(nc.vector.tensor_tensor(R["ee"], R["ee"], R["o1"], ALU.mult), "two weights")
            then(nc.vector.reduce_sum(R["em"], R["ee"], axis=AX), "their sum")
            then(nc.vector.reciprocal(R["em"], R["em"]), "its reciprocal")
            then(nc.vector.tensor_tensor(R["em"], R["em"], R["gw"], ALU.mult), "with the group's weight")
            then(nc.vector.tensor_tensor(R["ee"], R["ee"], wide(R["em"]), ALU.mult), "expert weights")
            ew = spread(R["ee"], (4, 4), (0, 4), (1, 4))
            then(nc.vector.tensor_tensor(R["sel"], g1_wide, ew, ALU.mult), "combine")
            for e in range(EXPERTS):
                if e >= 4:
                    dve.wait_ge(*multiplied.at("comb", e - 4))
                for t in range(4):
                    a = R["sel"][:, t, e // 4, e % 4:e % 4 + 1]
                    nc.vector.tensor_scalar(tmp[:, e % 4, t * P:(t + 1) * P], ident, a, None, ALU.mult)\
                        .then_inc(*small.on("diagonal", e, t))
            begin()
            with repeated(dve, EXPERTS, signals["dve"]) as i:
                for f in range(4):
                    dve.wait_ge(*gated.at("moe", f, i=i))
                    dve.wait_ge(*streamed.at("moe", "up", f, 0, i=i))
                    nc.vector.tensor_tensor(hid[:, f, :], tmp[:, f % 2, :], ps[:, 2 * f + 1, :], ALU.mult)\
                        .then_inc(*fused.on("moe", "up", f))
                    dve.wait_ge(*fused.at("moe", "up", f, i=i))
                    nc.vector.tensor_tensor(hid[:, f, :], hid[:, f, :], area(4096, EXPERTS * SEQ)[:, bass.ds(i * SEQ, SEQ)],
                                            ALU.mult).then_inc(*fused.on("moe", "hid", f))
                dve.wait_ge(*streamed.at("ada", i=i))
                n = 2 * ADA_PER_EXPERT
                nc.vector.tensor_tensor(mods[:].rearrange("p a b -> p (a b)")[:, bass.ds(i * n, n)], ps[:, 0, 0:n],
                                        par[:, bass.ds(i * n + PAR["b_ada"][0], n)], ALU.add)\
                    .then_inc(*dve_moved.on("ada"))
                for m in range(KT):
                    dve.wait_ge(*streamed.at("moe", "down", m, 0, i=i))
                    nc.vector.tensor_tensor(x[:, m, 0:SEQ], x[:, m, 0:SEQ], ps[:, (m + 1) % 8, :], ALU.add)\
                        .then_inc(*dve_moved.on("moe", m, also=("moe done",) if m == KT - 1 else None))
            begin()
            norm_dve(dve, "norm_first", job_of["norm_first"])
            begin()
            for l in range(LAYERS):
                own = BOTH if l < LAYERS - 1 else SEQ_ONLY
                lam = pc(f"lambda{l}", 0, 4)
                nc.vector.tensor_tensor(cols[:, 2:4], spread(lam, (2, 2)), spread(lam[:, 1:2], (2, 2)), ALU.mult)\
                    .then_inc(*small.on("lambda products", l))

                def gains(kind, name, which, plus, *key):
                    for s in range(2):
                        a = 8 + (kind * 2 + s) * 8
                        m = spread(mods[:, l * 48 + which * 8, s:s + 1], (2, 8))
                        then(nc.vector.scalar_tensor_tensor(out=cols[:, a:a + 8], in0=m, scalar=plus, in1=pc(name, 0, 8),
                                                            op0=ALU.add, op1=ALU.mult), *key, s)
                gains(0, f"attn_pre{l}", 1, 1.0, "attn_pre", l)
                gains(1, f"attn_post{l}", 2, 0.0, "attn_post", l)
                if l == 0:
                    dve.wait_ge(context_loaded, 16)
                dve.wait_ge(*exped.at("lambda", l))
                then(nc.vector.tensor_tensor(cols[:, 7:8], cols[:, 5:6], cols[:, 4:5], ALU.subtract), "lambda", l, 0)
                then(nc.vector.tensor_scalar(cols[:, 7:8], cols[:, 7:8], -LAM_INIT[l], None, ALU.add), "lambda", l, 1)
                then(nc.vector.tensor_scalar(cols[:, 6:7], pc(f"diff_sub{l}"), 1.0 - LAM_INIT[l], None, ALU.mult),
                     "lambda", l, 2)
                norm_dve(dve, ("attn_pre", l), job_of["attn_pre", l])
                begin()
                run_plain(dve, 1, ("in2", l))
                begin()
                run_values(dve, 1, ("diff_v", l))
                begin()
                run_values(dve, 1, ("gqa_v", l))
                begin()
                norm_dve(dve, ("low", l), job_of["low", l])
                begin()
                lift_move(dve, 1, l)
                begin()
                rope_dve(dve, ("rope2", l), rope2)
                dve.wait_ge(*roped.at(("rope2", l), "sum", 9))
                for hd in range(MLA_H):
                    nc.vector.tensor_copy(mla_k[64:96, hd, :], k_pe[64:96, :]).then_inc(*dve_moved.on("k_pe", l, hd))
                begin()
                for a in attentions[l]:
                    attend_dve(dve, a)
                    begin()
                for t in range(2):
                    w = ALL if l < LAYERS - 1 else SEQ
                    nc.vector.scalar_tensor_tensor(out=out_1[:, t, 0:w], in0=out_2[:, t, 0:w], scalar=cols[:, 7:8],
                                                   in1=out_1[:, t, 0:w], op0=ALU.mult, op1=ALU.add)\
                        .then_inc(*fused.on("difference", l, t))
                begin()
                norm_dve(dve, ("diff", l), job_of["diff", l])
                begin()
                run_plain(dve, 1, ("out2", l))
                begin()
                norm_dve(dve, ("attn_post", l), job_of["attn_post", l])
                begin()
                gains(0, f"ffn_pre{l}", 4, 1.0, "ffn_pre", l)
                gains(1, f"ffn_post{l}", 5, 0.0, "ffn_post", l)
                norm_dve(dve, ("ffn_pre", l), job_of["ffn_pre", l])
                begin()
                for m in range(HT):
                    for pi, (c0, cn) in enumerate(own):
                        dve.wait_ge(*gated.at("ffn", l, m, pi))
                        dve.wait_ge(*streamed.at("ffn", l, "up", m, pi))
                        nc.vector.tensor_tensor(ffn_hid[:, m, c0:c0 + cn], tmp[:, 2 * (m % 2) + pi, 0:cn],
                                                ps[:, 4 * (m % 2) + 2 + pi, 0:cn], ALU.mult)\
                            .then_inc(*fused.on("ffn", l, m, pi))
                begin()
                run_plain(dve, 1, ("down", l))
                begin()
                norm_dve(dve, ("ffn_post", l), job_of["ffn_post", l])
                begin()
            normed.points[("final",)] = (normed.n, 0, 1)
    return {**{s.name: s.points for v in signals.values() for s in v}, "ends": ends}


def _blocks(w):
    k, m = w.shape
    return w.reshape(k // P, P, m // P, P).transpose(2, 0, 1, 3).reshape(-1, P, P)


def _side_by_side(w):
    k, m = w.shape
    return w.reshape(k // P, P, m // P, P).transpose(0, 2, 1, 3).reshape(-1, P, P)


def _interleaved(*ws):
    tiles = [_blocks(w).reshape(w.shape[1] // P, w.shape[0] // P, P, P) for w in ws]
    return np.concatenate([t[m] for m in range(tiles[0].shape[0]) for t in tiles])


def _stream(a):
    w, kvw = a["w_in"][0], a["w_mem_kv"][0]
    gates = [w[:, 5120 + b * D:5120 + (b + 1) * D] for b in range(3)]
    out = [_blocks(w[:, 0:1024]), _side_by_side(w[:, 1024:1536]), _side_by_side(w[:, 1536:2048]),
           _blocks(w[:, 2048:3072]), _interleaved(gates[0], a["w_ret_o"][0]), _blocks(w[:, 3072:4608]),
           _interleaved(gates[1], a["w_na_o"][0]), _blocks(kvw[:, 0:512]), _side_by_side(kvw[:, 512:1024]),
           _blocks(w[:, 4608:5120]), _interleaved(gates[2], a["w_xa_o"][0]), _blocks(a["w_out"][0])]
    ada = np.concatenate([a["w_ada_2"][l] for l in range(LAYERS)], axis=1)
    n = ADA_PER_EXPERT * P
    for e in range(EXPERTS):
        g, j = e // 4, e % 4
        out += [_interleaved(a["w_exp_gate"][0, g, j], a["w_exp_up"][0, g, j]), _blocks(ada[:, e * n:(e + 1) * n]),
                _blocks(a["w_exp_down"][0, g, j])]
    for l in range(LAYERS):
        v = a["w_in_2"][l]
        k_pe = np.zeros((D, P), v.dtype)
        k_pe[:, 64:96] = v[:, 384:416]
        gq = v[:, 1184:1696].reshape(D, 2, 4, 64).transpose(0, 2, 1, 3).reshape(D, 512)
        out += [_blocks(np.concatenate([v[:, 0:256], v[:, 416:672], gq, v[:, 256:384], k_pe, v[:, 672:928],
                                        v[:, 1696:1824]], axis=1)),
                _side_by_side(v[:, 928:1184]), _side_by_side(v[:, 1824:1952]), _blocks(a["w_out_2"][l]),
                _interleaved(a["w_ffn_gate_2"][l], a["w_ffn_up_2"][l]), _blocks(a["w_ffn_down_2"][l])]
    out = np.concatenate(out)
    n = out.shape[0] // BLOCKS
    return np.ascontiguousarray(out.reshape(n, BLOCKS, P, P).transpose(0, 2, 1, 3).reshape(n, P, CHUNK))


def _columns(v):
    return v.reshape(-1, P).T


def _params(a):
    lay, n = param_layout()
    out = np.zeros((P, n), np.float32)

    def put(name, v):
        first, w = lay[name]
        out[:v.shape[0], first:first + w] = v

    put("g_mix", _columns(a["g_mix"][0]))
    put("ret_gain", _columns(a["ret_norm_gain"][0]))
    put("g_mem", _columns(a["g_mem"][0]))
    put("g_ffn", _columns(a["g_ffn"][0]))
    put("g_final", _columns(a["g_final"]))
    put("decay", np.broadcast_to(np.concatenate([a["ret_decay_fwd"][0], a["ret_decay_bwd"][0]]), (P, 8)))
    put("router_bias", np.broadcast_to(np.tile(np.concatenate([a["b_router_group"][0], a["b_router_expert"][0]]), 4),
                                       (P, 80)))
    put("c", np.stack([_columns(a["c_2"][0]), _columns(a["c_ctx_2"])], axis=2).reshape(P, 16))
    put("b_ada", np.repeat(_columns(a["b_ada_2"].reshape(-1)), 2, axis=1))
    for l in range(LAYERS):
        for name, source in (("attn_pre", "g_attn_pre_2"), ("attn_post", "g_attn_post_2"), ("mla_q", "g_mla_q_2"),
                             ("mla_kv", "g_mla_kv_2"), ("ffn_pre", "g_ffn_pre_2"), ("ffn_post", "g_ffn_post_2")):
            put(f"{name}{l}", _columns(a[source][l]))
        for name, source in (("diff_sub", "g_diff_sub_2"), ("gqa_q", "g_gqa_q_2"), ("gqa_k", "g_gqa_k_2")):
            put(f"{name}{l}", _columns(np.tile(a[source][l], 2)))
        put(f"lambda{l}", np.stack([a[f"lambda_{n}_2"][l] for n in ("q1", "k1", "q2", "k2")], axis=1))
    return out


def _rotation(half):
    out = np.zeros((P, P), np.float32)
    for m in range(P):
        first = m % (2 * half) < half
        out[m + half if first else m - half, m] = -1.0 if first else 1.0
    return out


def _constants():
    f = np.float32
    lay, n = const_layout()
    con = np.zeros((P, n), f)

    def put(name, v):
        first, w = lay[name]
        con[:, first:first + w] = v

    put("ident", np.eye(P))
    put("ones", 1.0)
    put("ones64", np.kron(np.eye(2), np.ones((64, 64))))
    for half in (64, 32, 16):
        put(f"rot{2 * half}", _rotation(half))
    mask = np.zeros((P, 3, 256), f)
    for kind, (t, start) in enumerate(((0, 0), (1, 8), (3, 32))):
        q = 16 * t + np.arange(P) // 8
        off = (start + np.arange(256) // GRID_H)[None, :] - np.clip(q - 8, 0, 48)[:, None]
        mask[:, kind] = np.where((off >= 0) & (off < 16), 0.0, -BIG)
    put("mask", mask.reshape(P, -1))
    put("rank", np.tile([4.0, 3.0, 2.0, 1.0], 4))
    delta = np.arange(DIFFS)[None, :] - 3 * P - np.arange(P)[:, None]
    dist = np.stack([np.maximum(delta, 0), np.maximum(-delta, 0)], axis=1).astype(f)

    def trig(ang):
        return [np.cos(ang).T.astype(f), np.sin(ang).T.astype(f)]

    s = np.arange(SEQ, dtype=f)
    inv = (f(10000.0) ** (-np.arange(64, dtype=f) / f(64))).astype(f)
    trig128 = np.stack(trig((s[:, None] * inv[None, :])[:, np.arange(P) % 64]), axis=1)
    both = []
    for quarter in (16, 8):
        inv = (f(10000.0) ** (-np.arange(quarter, dtype=f) / f(quarter))).astype(f)
        row, col = np.floor(s / GRID_W).astype(f), (s % GRID_W).astype(f)
        ang = np.concatenate([row[:, None] * inv, col[:, None] * inv], axis=1)
        both += trig(ang[:, np.arange(P) % (2 * quarter)])
    return {"con": con, "dist": dist, "trig128": trig128, "trig": np.stack(both, axis=1)}


def _near_bias(rpb):
    flat = np.pad(rpb.reshape(-1), (16, 32))
    q = np.arange(P)
    first = 16 + (7 - q % 8) * 31 - q // 8 - 1
    at = first[:, None, None] + 465 * np.arange(NA_HEADS)[None, :, None] + np.arange(RPB_RUN)[None, None, :]
    return flat[at]


def _feature_major(v):
    return np.ascontiguousarray(v.reshape(-1, KT, P).transpose(2, 1, 0))


def kernel(**inputs):
    import concourse.bacc as bacc
    from concourse.bass_utils import run_bass_kernel_spmd

    a = {k: np.asarray(v) for k, v in inputs.items()}
    small = [np.concatenate([a["w_mla_qb_2"][l].reshape(2, P, 384).transpose(1, 0, 2).reshape(P, 768),
                             a["w_mla_kvb_2"][l]], axis=1) for l in range(LAYERS)]
    arrays = {"stream": _stream(a), "xT": _feature_major(a["x"][0]), "memT": _feature_major(a["mem"][0]),
              "ctxT": _feature_major(a["ctx_2"][0]), "par": _params(a), "rpb": _near_bias(a["na_rpb"][0]),
              "w_router": np.concatenate([a["w_router_group"][0], a["w_router_expert"][0]], axis=1)
              .reshape(KT, P, 20).transpose(1, 0, 2), "w_small": np.stack(small), **_constants()}
    arrays = {k: np.ascontiguousarray(v) for k, v in arrays.items()}

    def build(known):
        nc = bacc.Bacc("TRN2", target_bir_lowering=False, num_devices=1)
        ins = {n: nc.dram_tensor(f"in_{n}", v.shape, mybir.dt.from_np(v.dtype), kind="ExternalInput").ap()
               for n, v in arrays.items()}
        out = nc.dram_tensor("out_0", (P, KT, SEQ), F32, kind="ExternalOutput").ap()
        return nc, program(nc, ins, out, known)

    _, counted = build({})
    nc, again = build(counted)
    assert again == counted or all(again[k] == counted[k] for k in counted if k != "ends")
    r = run_bass_kernel_spmd(nc, [{f"in_{n}": v for n, v in arrays.items()}], core_ids=[0])
    y = r.results[0]["out_0"]
    return np.ascontiguousarray(y.transpose(2, 1, 0)).reshape(1, SEQ, D)
```

```python
import math
from contextlib import ExitStack, contextmanager

import numpy as np

import concourse.bass as bass
from concourse import mybir

P = 128
D = 1024
KT = D // P
SEQ = 512
CTX = 256
ALL = SEQ + CTX
F32 = mybir.dt.float32
ACT = mybir.ActivationFunctionType
ALU = mybir.AluOpType
AX = mybir.AxisListType.X

BLOCKS = 16
CHUNK = BLOCKS * P
RING = 3

RET_HEADS, NA_HEADS, XA_HEADS = 4, 8, 4
GRID_W, GRID_H, WIN = 64, 8, 32
EXPERTS, D_FF = 16, 512
HIDDEN = 2816
HT = HIDDEN // P
LAYERS = 2
MLA_H, DIFF_H, GQA_H = 4, 4, 8
LAM_INIT = [0.8 - 0.6 * math.exp(-0.3 * l) for l in range(LAYERS)]
RPB_RUN = 7 * 31 + WIN + 16
DIFFS = SEQ + 3 * P
BIG = 1e30
ARENA = 25184

ADA_TILES = LAYERS * 48
ADA_STEP = ADA_TILES // (3 * KT)
MOE_FIRST = 96
GROUPS, IN_GROUP = 4, EXPERTS // 4
EXPERT_CHUNKS = 3 * D * D_FF // (P * CHUNK)
UNIT_CHUNKS = IN_GROUP * EXPERT_CHUNKS
UNITS = SEQ // P + GROUPS - 1
SLOTS = (UNITS + 1) * P


def param_layout():
    at, out = 0, {}
    items = [("g_mix", 8), ("ret_gain", 8), ("g_mem", 8), ("g_ffn", 8), ("g_final", 8), ("decay", 8),
             ("router_bias", 80), ("c", 16), ("b_ada", 2 * ADA_TILES)]
    for l in range(LAYERS):
        items += [(f"{n}{l}", w) for n, w in (
            ("attn_pre", 8), ("attn_post", 8), ("mla_q", 2), ("mla_kv", 1), ("diff_sub", 1), ("gqa_q", 1),
            ("gqa_k", 1), ("ffn_pre", 8), ("ffn_post", 8), ("lambda", 4))]
    for n, w in items:
        out[n] = (at, w)
        at += w
    return out, at


def const_layout():
    at, out = 0, {}
    for n, w in (("ident", P), ("ones", P), ("ones64", P), ("rot128", P), ("rot64", P), ("rot32", P),
                 ("mask", 3 * 256), ("rank", 16), ("before", P), ("steps", 16), ("unit_no", 4 * UNITS),
                 ("slot_no", UNITS)):
        out[n] = (at, w)
        at += w
    return out, at


class Signal:

    def __init__(self, nc, ctx, name, known):
        self.name, self.sem = name, ctx.enter_context(nc.semaphore(name))
        self.n, self.points, self.new, self.known = 0, {}, [], known.get(name)

    def on(self, *key, also=None):
        self.n += 1
        for k in (key, also):
            if k is not None:
                assert k not in self.points, k
                self.points[k] = (self.n, 0, 1)
                self.new.append(k)
        return self.sem, 1

    def at(self, *key, i=None):
        if self.known is None:
            return self.sem, 1
        first, step, trips = self.known[key]
        if i is None:
            return self.sem, first + step * (trips - 1)
        return self.sem, i * step + first


@contextmanager
def repeated(engine, trips, signals):
    start = [s.n for s in signals]
    for s in signals:
        s.new = []
    with engine.Fori(0, trips) as i:
        yield i
    for s, n0 in zip(signals, start):
        step = s.n - n0
        for k in s.new:
            s.points[k] = (s.points[k][0], step, trips)
        s.n = n0 + step * trips


class Chunks:

    def __init__(self):
        self.block = 0


def program(nc, ins, out, known):
    PAR, n_par = param_layout()
    CON, n_con = const_layout()
    stream = ins["stream"]
    n_chunks = stream.shape[0]
    with ExitStack() as ctx:
        def sb(name, *shape):
            return ctx.enter_context(nc.sbuf_tensor(name, [P, *shape], F32))

        def sem(name):
            return ctx.enter_context(nc.semaphore(name))

        ring = sb("ring", RING, CHUNK)
        x = sb("x", KT, ALL)
        h = sb("h", KT, ALL)
        work = sb("work", 12, SEQ)
        tmp, std, rstd = work[:, 0:8], work[:, 8:10], work[:, 10:12]
        par = sb("par", n_par)
        con = sb("con", n_con)
        w_router = sb("w_router", KT, 20)
        mods = sb("mods", ADA_TILES, 2)
        silu_c = sb("silu_c", KT, 2)
        cols = sb("cols", 64)
        stat = sb("stat", 8, 4)
        route = sb("route", 640)
        unit_group = ctx.enter_context(nc.sbuf_tensor("unit_group", [P, 8], mybir.dt.int32))
        arena = sb("arena", ARENA)
        ps = ctx.enter_context(nc.psum_tensor("ps", [P, 8, 512], F32))

        def pc(name, j=0, w=1):
            a = PAR[name][0] + j
            return par[:, a:a + w]

        def cc(name):
            a, w = CON[name]
            return con[:, a:a + w]

        def area(offset, *dims):
            n = int(np.prod(dims))
            assert offset + n <= ARENA, (offset, dims)
            v = arena[:, offset:offset + n]
            if len(dims) == 2:
                v = v.rearrange("p (a b) -> p a b", a=dims[0])
            if len(dims) == 3:
                v = v.rearrange("p (a b c) -> p a b c", a=dims[0], b=dims[1])
            return v

        def spread(ap, *dims):
            return bass.AP(tensor=ap.tensor, offset=ap.offset, ap=[list(ap.ap[0])] + [list(d) for d in dims])

        ident, ones, ones64 = cc("ident"), cc("ones"), cc("ones64")
        mixed_sum = area(0, 8, SEQ)
        ret_q, ret_k = area(4096, 4, SEQ), area(6144, 4, SEQ)
        ret_v = area(8192, 4, 1024)
        ret_y = area(12288, 8, SEQ)
        ret_s = area(16384, 4, SEQ)
        dist = area(18432, 2, DIFFS)
        ret_e = area(20224, 2, DIFFS)
        ret_t = work[:, 0:2, :].rearrange("p a b -> p (a b)")[:, 0:DIFFS]
        trig128 = area(22016, 2, SEQ)
        rpb = area(23040, NA_HEADS, RPB_RUN)
        na_q, na_k, na_v = area(4096, 4, SEQ), area(6144, 4, SEQ), area(8192, 4, SEQ)
        na_win = area(10240, 8, SEQ)
        na_o = area(14336, 4, SEQ)
        b1_p = area(16384, 3, 256)
        b1_pt = area(17152, 2, 2, SEQ)
        xa_q, xa_k, xa_v, xa_o = area(4096, 4, SEQ), area(6144, 4, CTX), area(7168, 2, SEQ), area(8192, 4, SEQ)
        h_tok = area(0, 4, D)
        pick = area(4096, 4, SLOTS)
        unit_y = area(8192, UNITS * D)
        unit_h = area(15360, KT, P)
        hid = area(16384, 2, D_FF)
        hid_t = area(17408, 2, 4, P)
        put = area(18432, UNITS, SEQ)
        slot_row = area(22528, SLOTS)
        mla_q, mla_k = area(0, 4, ALL), area(3072, 4, ALL)
        diff_q, diff_k = area(6144, 2, ALL), area(7680, 2, ALL)
        gqa_q, gqa_k = area(9216, 4, ALL), area(12288, ALL)
        val = area(13056, 6, 640)
        prob = work[:, :, :].rearrange("p a b -> p (a b)")[:, 3072:3072 + 3 * ALL].rearrange("p (a b) -> p a b", a=3)
        prob_t = area(16896, 2, 6, SEQ)
        q_low, kv_low, k_pe = area(16896, 2, ALL), area(18432, ALL), area(19200, ALL)
        w_small = area(19968, 2 * 384 + 512)
        trig = area(23040, 4, SEQ)
        out_1 = tmp[:, 0:3, :].rearrange("p a b -> p (a b)").rearrange("p (a b) -> p a b", a=2)
        out_2 = tmp[:, 3:6, :].rearrange("p a b -> p (a b)").rearrange("p (a b) -> p a b", a=2)
        attn_y = area(0, KT, ALL)
        ffn_hid = area(0, HT, ALL)
        ffn_y = area(16896, KT, ALL)

        R, at = {"rank": cc("rank").rearrange("p (t n) -> p t n", t=4)}, 64
        for name, w in (("lg", 20), ("gd", 4), ("eq", 4), ("cand", 4), ("g1", 4), ("ge", 4), ("ig", 4), ("ed", 4),
                        ("ee", 4), ("e2", 4), ("o1", 4), ("o2", 4), ("rk", 4), ("cmp", 4)):
            R[name] = route[:, at:at + 4 * w].rearrange("p (t n) -> p t n", t=4)
            at += 4 * w
        for name, w in (("gm", 4), ("best", 4), ("gw", 4), ("em", 4), ("n", 4), ("units", 4), ("slot", 4), ("from", 8),
                        ("over", 4 * UNITS), ("ug", UNITS), ("w", 4 * UNITS)):
            R[name] = route[:, at:at + w]
            at += w
        R["sel"] = route[:, at:at + 64].rearrange("p (t g e) -> p t g e", t=4, g=4)

        signals = {}

        def signal(engine, name):
            s = Signal(nc, ctx, name, known)
            signals.setdefault(engine, []).append(s)
            return s

        loaded = [sem(f"chunk_loaded{r}") for r in range(RING)]
        inputs_loaded = sem("inputs_loaded")
        context_loaded = sem("context_loaded")
        slots_loaded = sem("slots_loaded")
        late_loaded = sem("late_loaded")
        stored = sem("stored")
        streamed, summed, scored = signal("pe", "streamed"), signal("pe", "summed"), signal("pe", "scored")
        turned, attended, multiplied = signal("pe", "turned"), signal("pe", "attended"), signal("pe", "multiplied")
        squared, rooted, exped = signal("act", "squared"), signal("act", "rooted"), signal("act", "exped")
        act_moved, gated = signal("act", "act_moved"), signal("act", "gated")
        normed, inverted, maxed = signal("dve", "normed"), signal("dve", "inverted"), signal("dve", "maxed")
        dve_moved, fused, scaled = signal("dve", "dve_moved"), signal("dve", "fused"), signal("dve", "scaled")
        small, roped = signal("dve", "small"), signal("dve", "roped")
        ends = {}
        known_ends = known.get("ends")
        seen = {}

        def stage(name, e, wait=True):
            before = seen.setdefault(name, [0, {}])
            n = before[0]
            before[0] += 1
            ends[(name, n)] = [s.n for s in signals[name]]
            if known_ends is None or not wait:
                return
            for other in ("pe", "act", "dve"):
                for s, value in zip(signals[other], known_ends[(other, n)]):
                    if value > before[1].get(s.name, 0):
                        e.wait_ge(s.sem, value)
                        before[1][s.name] = value

        block = ctx.enter_context(nc.Block())

        @block.sync
        def _(sp):
            for dst, src in ((x[:, :, 0:SEQ], ins["xT"]), (x[:, :, SEQ:ALL], ins["memT"]), (par[:], ins["par"]),
                             (con[:], ins["con"]), (trig128, ins["trig128"]), (dist, ins["dist"]),
                             (rpb, ins["rpb"]), (w_router[:], ins["w_router"])):
                sp.dma_start(dst, src).then_inc(inputs_loaded, 16)

            def load(n, source, i=None):
                sp.dma_start(ring[:, n % RING], source).then_inc(loaded[n % RING], 16)

            for n in range(MOE_FIRST):
                if n >= RING:
                    sp.wait_ge(*streamed.at("chunk", n - RING))
                load(n, stream[n])

            def unit_chunk(group, j):
                return stream[group * UNIT_CHUNKS + (MOE_FIRST + j)]

            sp.wait_ge(*small.at("unit groups"))
            group = sp.value_load(unit_group[0:1, 0:1], min_val=0, max_val=GROUPS - 1)
            for j in range(UNIT_CHUNKS):
                n = MOE_FIRST + j
                sp.wait_ge(*(streamed.at("chunk", n - RING, i=0) if j >= RING else streamed.at("chunk", n - RING)))
                load(n, unit_chunk(group, j))
            with sp.Fori(1, UNITS) as i:
                group = sp.value_load(unit_group[0:1, bass.ds(i, 1)], min_val=0, max_val=GROUPS - 1)
                for j in range(UNIT_CHUNKS):
                    n = MOE_FIRST + j
                    if j >= RING:
                        sp.wait_ge(*streamed.at("chunk", n - RING, i=i))
                    else:
                        sp.wait_ge(*streamed.at("chunk", n + UNIT_CHUNKS - RING, i=i - 1))
                    load(n, unit_chunk(group, j))
            after = MOE_FIRST + UNITS * UNIT_CHUNKS
            for n in range(after, n_chunks + (UNITS - GROUPS) * UNIT_CHUNKS):
                if n - RING < after:
                    sp.wait_ge(*streamed.at("chunk", n - RING - (UNITS - 1) * UNIT_CHUNKS))
                else:
                    sp.wait_ge(*streamed.at("chunk", n - RING))
                load(n, stream[n - (UNITS - GROUPS) * UNIT_CHUNKS])
            sp.wait_ge(*normed.at("final"))
            sp.dma_start(out, x[:, :, 0:SEQ]).then_inc(stored, 16)
            sp.wait_ge(stored, 16)

        @block.gpsimd
        def _(pool):
            pool.wait_ge(*normed.at("norm_mem done"))
            nc.gpsimd.dma_start(x[:, :, SEQ:ALL], ins["ctxT"]).then_inc(context_loaded, 16)
            pool.wait_ge(*normed.at("norm_moe", 0, "end"))
            nc.gpsimd.dma_start(slot_row, ins["slot_row"]).then_inc(slots_loaded, 16)
            pool.wait_ge(*dve_moved.at("moe done"))
            nc.gpsimd.dma_start(trig, ins["trig"]).then_inc(late_loaded, 16)
            nc.gpsimd.dma_start(w_small, ins["w_small"][0]).then_inc(late_loaded, 16)
            pool.wait_ge(*normed.at(("ffn_post", 0), 1, "end"))
            nc.gpsimd.dma_start(w_small, ins["w_small"][1]).then_inc(late_loaded, 16)

        SEQ_ONLY = [(0, SEQ)]
        BOTH = [(0, SEQ), (SEQ, CTX)]

        def norm_jobs(src, nk, pieces, mean_of, n, write, parts=P):
            return [dict(src=[src(k, c0, cn) for k in range(nk)], ones=mean_of, inv=1.0 / n, write=write,
                         piece=(c0, cn), parts=parts) for c0, cn in pieces]

        def slots(jobs):
            at, user, out_ = 0, {}, []
            for j, job in enumerate(jobs):
                own = []
                for k in range(len(job["src"])):
                    s = job.get("slots", range(8))[at % len(job.get("slots", range(8)))]
                    own.append((s, user.get(s)))
                    user[s] = j
                    at += 1
                out_.append(own)
            return out_

        def norm_pe(pe, tag, jobs, square_at=None):
            for j, job in enumerate(jobs):
                cn, parts = job["piece"][1], job["parts"]
                if j >= 2:
                    pe.wait_ge(*rooted.at(tag, j - 2))
                for k, (s, _) in enumerate(slots(jobs)[j]):
                    pe.wait_ge(*squared.at(tag, j, k))
                    mm = pe.matmul(ps[0:parts, j % 2, 0:cn], job["ones"][0:parts, 0:parts],
                                   tmp[0:parts, s, 0:cn], start=(k == 0), stop=(k == len(job["src"]) - 1))
                mm.then_inc(*summed.on(tag, j))

        def x_ready(tag):
            return lambda j, k: normed.at(tag, j, "end" if k == KT - 1 else f"added{k}") if j < len(job_of[tag]) else None

        def moved_ready(tag, pieces):
            return lambda j, k: moved_at(tag, k * pieces + j)

        def norm_act(act, tag, jobs, ready=None):
            for j in range(len(jobs) + 1):
                if j < len(jobs):
                    job = jobs[j]
                    cn, parts = job["piece"][1], job["parts"]
                    for k, (s, user) in enumerate(slots(jobs)[j]):
                        if user is not None:
                            act.wait_ge(*summed.at(tag, user))
                        if ready and ready(j, k):
                            act.wait_ge(*ready(j, k))
                        nc.scalar.activation(tmp[0:parts, s, 0:cn], job["src"][k], ACT.Square)\
                            .then_inc(*squared.on(tag, j, k))
                if j >= 1:
                    job = jobs[j - 1]
                    cn, parts = job["piece"][1], job["parts"]
                    act.wait_ge(*summed.at(tag, j - 1))
                    if j >= 3:
                        act.wait_ge(*inverted.at(tag, j - 3))
                    nc.scalar.activation(std[0:parts, (j - 1) % 2, 0:cn], ps[0:parts, (j - 1) % 2, 0:cn], ACT.Sqrt,
                                         bias=cols[0:parts, job.get("eps", 0):job.get("eps", 0) + 1],
                                         scale=job["inv"]).then_inc(*rooted.on(tag, j - 1))

        def norm_dve(dve, tag, jobs):
            for j, job in enumerate(jobs):
                cn, parts = job["piece"][1], job["parts"]
                dve.wait_ge(*rooted.at(tag, j))
                if j >= 2:
                    dve.wait_ge(*normed.at(tag, j - 2, "end"))
                r = rstd[0:parts, j % 2, 0:cn]
                nc.vector.reciprocal(r, std[0:parts, j % 2, 0:cn]).then_inc(*inverted.on(tag, j))
                dve.wait_ge(*inverted.at(tag, j))
                job["write"](dve, tag, j, job["piece"], r)

        def write_scaled(dst, gain, shift=None, final=None):
            def write(dve, tag, j, piece, r):
                c0, cn = piece
                job = job_of[tag][j]
                nk = len(job["src"])
                for k in range(nk):
                    key = (tag, j, "end") if k == nk - 1 and not shift else (tag, j, k)
                    nc.vector.scalar_tensor_tensor(out=dst(k, c0, cn), in0=job["src"][k], scalar=gain(k, c0), in1=r,
                                                   op0=ALU.mult, op1=ALU.mult)\
                        .then_inc(*normed.on(*key, also=(final,) if final and k == nk - 1 else None))
                if shift:
                    for k in range(nk):
                        dve.wait_ge(*normed.at(tag, j, k))
                        nc.vector.tensor_scalar(dst(k, c0, cn), dst(k, c0, cn), shift(k, c0), None, ALU.add)\
                            .then_inc(*normed.on(tag, j, "end" if k == nk - 1 else f"shifted{k}"))
            return write

        def write_residual(gain):
            def write(dve, tag, j, piece, r):
                c0, cn = piece
                job = job_of[tag][j]
                for k in range(KT):
                    nc.vector.scalar_tensor_tensor(out=job["src"][k], in0=job["src"][k], scalar=gain(k, c0), in1=r,
                                                   op0=ALU.mult, op1=ALU.mult).then_inc(*normed.on(tag, j, k))
                for k in range(KT):
                    dve.wait_ge(*normed.at(tag, j, k))
                    nc.vector.tensor_tensor(x[:, k, c0:c0 + cn], x[:, k, c0:c0 + cn], job["src"][k], ALU.add)\
                        .then_inc(*normed.on(tag, j, "end" if k == KT - 1 else f"added{k}"))
            return write

        job_of = {}

        def xs(k, c0, cn):
            return x[:, k, c0:c0 + cn]

        def hs(k, c0, cn):
            return h[:, k, c0:c0 + cn]

        job_of["norm_x"] = norm_jobs(xs, KT, SEQ_ONLY, ones, D, write_scaled(hs, lambda k, c0: pc("g_mix", k)))
        job_of["norm_x"] += norm_jobs(xs, KT, [(SEQ, CTX)], ones, D,
                                      write_scaled(hs, lambda k, c0: pc("g_mem", k), final="norm_mem done"))
        job_of["norm_moe"] = norm_jobs(xs, KT, SEQ_ONLY, ones, D, write_scaled(hs, lambda k, c0: pc("g_ffn", k)))
        job_of["norm_first"] = norm_jobs(xs, KT, SEQ_ONLY, ones, D, write_scaled(xs, lambda k, c0: pc("g_final", k)))
        job_of["ret_norm"] = [dict(src=[ret_y[:, 2 * hd + e, :] for e in range(2)], ones=ones, inv=1.0 / 256, eps=1,
                                   piece=(0, SEQ), parts=P,
                                   write=write_scaled(lambda k, c0, cn, hd=hd: ret_y[:, 2 * hd + k, :],
                                                      lambda k, c0, hd=hd: pc("ret_gain", 2 * hd + k)))
                              for hd in range(RET_HEADS)]

        def scal(kind, k, c0):
            a = 8 + (kind * 2 + (1 if c0 >= SEQ else 0)) * 8 + k
            return cols[:, a:a + 1]

        def mod(l, which, k, c0):
            return mods[:, l * 48 + which * 8 + k, (1 if c0 >= SEQ else 0):(2 if c0 >= SEQ else 1)]

        for l in range(LAYERS):
            own = BOTH if l < LAYERS - 1 else SEQ_ONLY
            job_of["attn_pre", l] = norm_jobs(xs, KT, BOTH, ones, D, write_scaled(
                hs, lambda k, c0: scal(0, k, c0), lambda k, c0, l=l: mod(l, 0, k, c0)))
            job_of["attn_post", l] = norm_jobs(lambda k, c0, cn: attn_y[:, k, c0:c0 + cn], KT, own, ones, D,
                                               write_residual(lambda k, c0: scal(1, k, c0)))
            job_of["ffn_pre", l] = norm_jobs(xs, KT, own, ones, D, write_scaled(
                hs, lambda k, c0: scal(0, k, c0), lambda k, c0, l=l: mod(l, 3, k, c0)))
            job_of["ffn_post", l] = norm_jobs(lambda k, c0, cn: ffn_y[:, k, c0:c0 + cn], KT, own, ones, D,
                                              write_residual(lambda k, c0: scal(1, k, c0)))

            def low(k, c0, cn):
                return q_low[:, k, c0:c0 + cn]

            def kv(k, c0, cn):
                return kv_low[:, c0:c0 + cn]
            jobs = norm_jobs(kv, 1, BOTH, ones, 128, write_scaled(kv, lambda k, c0, l=l: pc(f"mla_kv{l}")))
            jobs += norm_jobs(low, 2, own, ones, 256, write_scaled(low, lambda k, c0, l=l: pc(f"mla_q{l}", k)))
            for t in range(4):
                def gq(k, c0, cn, t=t):
                    return gqa_q[:, t, c0:c0 + cn]
                jobs += norm_jobs(gq, 1, own, ones64, 64, write_scaled(gq, lambda k, c0, l=l: pc(f"gqa_q{l}")))

            def gk(k, c0, cn):
                return gqa_k[:, c0:c0 + cn]
            jobs += norm_jobs(gk, 1, BOTH, ones64, 64, write_scaled(gk, lambda k, c0, l=l: pc(f"gqa_k{l}")))
            job_of["low", l] = jobs
            jobs = []
            for t in range(2):
                def dd(k, c0, cn, t=t):
                    return out_1[:, t, c0:c0 + cn]
                jobs += norm_jobs(dd, 1, own, ones64, 64, write_scaled(
                    lambda k, c0, cn, t=t: h[:, 2 + t, c0:c0 + cn], lambda k, c0: cols[:, 6:7]))
            for job in jobs:
                job["slots"] = (6, 7)
            job_of["diff", l] = jobs

        chunks = Chunks()

        def take(pe, i=None, first=0, count=1):
            b = chunks.block
            n, o = b // BLOCKS, b % BLOCKS
            if o == 0:
                if i is None:
                    pe.wait_ge(loaded[n % RING], 16 * (n // RING + 1))
                else:
                    pe.wait_ge(loaded[n % RING], i * (16 * UNIT_CHUNKS // RING) + 16 * (n // RING + 1))
            chunks.block += count
            return ring[:, n % RING, o * P:(o + count) * P]

        def chunk_end():
            return ("chunk", chunks.block // BLOCKS - 1) if chunks.block % BLOCKS == 0 else None

        def group(pe, key, banks, rhs, K, pieces, out_cols=None, i=None):
            for k in range(K):
                w = take(pe, i)
                for pi, (c0, cn) in enumerate(pieces):
                    mm = pe.matmul(ps[:, banks[pi], 0:cn], w, rhs(k, c0, cn), start=(k == 0), stop=(k == K - 1))
                    last = pi == len(pieces) - 1
                    also = chunk_end() if last else None
                    if k == K - 1:
                        mm.then_inc(*streamed.on(*key, pi, also=also))
                    elif also:
                        mm.then_inc(*streamed.on(*also))

        def after_norm(pe, tag, shifted=False):
            for j in range(max(0, len(job_of[tag]) - 2), len(job_of[tag])):
                pe.wait_ge(*rooted.at(tag, j))

            def ready(k, pi):
                pe.wait_ge(*normed.at(tag, pi, "end" if k == KT - 1 else f"shifted{k}" if shifted else k))
            return ready

        def first_chunk(pe, keys, banks, rhs, pieces, ready):
            w = [[take(pe) for _ in range(KT)] for _ in keys]
            for pi, (c0, cn) in enumerate(pieces):
                for t, key in enumerate(keys):
                    for k in range(KT):
                        if t == 0:
                            ready(k, pi)
                        mm = pe.matmul(ps[:, banks[t][pi], 0:cn], w[t][k], rhs(k, c0, cn), start=(k == 0),
                                       stop=(k == KT - 1))
                    last = pi == len(pieces) - 1 and t == len(keys) - 1
                    mm.then_inc(*streamed.on(*key, pi, also=chunk_end() if last else None))

        def tiles(ms, pieces_of):
            g = 0
            for m in range(ms):
                for pi, (c0, cn) in enumerate(pieces_of(m)):
                    yield g, m, pi, c0, cn
                    g += 1

        def moved_at(tag, g):
            return (act_moved if g % 2 == 0 else dve_moved).at(tag, g)

        def project_pe(pe, tag, ms, K, rhs, pieces_of, ready=None):
            g = 0
            for m in range(ms):
                pieces = pieces_of(m)
                if ready and m < 2:
                    if m == 0:
                        n = len(pieces)
                        first_chunk(pe, [(tag, 0), (tag, 1)], [list(range(n)), list(range(n, 2 * n))], rhs, pieces, ready)
                    g += len(pieces)
                    continue
                for pi in range(len(pieces)):
                    if g + pi >= 8:
                        pe.wait_ge(*moved_at(tag, g + pi - 8))
                group(pe, (tag, m), [(g + pi) % 8 for pi in range(len(pieces))], rhs, K, pieces)
                g += len(pieces)

        def project_move(engine, which, tag, ms, pieces_of, dst):
            for g, m, pi, c0, cn in tiles(ms, pieces_of):
                if g % 2 != which:
                    continue
                engine.wait_ge(*streamed.at(tag, m, pi))
                d, s = dst(m, c0, cn, ps[:, g % 8, 0:cn])
                if which == 0:
                    nc.scalar.activation(d, s, ACT.Copy).then_inc(*act_moved.on(tag, g))
                else:
                    nc.vector.tensor_copy(d, s).then_inc(*dve_moved.on(tag, g))

        def values_pe(pe, tag, token_tiles, lhs, nb, g0=0):
            start = chunks.block
            taken = [take(pe, count=nb) for _ in range(KT)]
            for t in range(token_tiles):
                if g0 + t >= 8:
                    pe.wait_ge(*moved_at(tag, g0 + t - 8))
                for k in range(KT):
                    mm = pe.matmul(ps[:, (g0 + t) % 8, 0:nb * P], lhs(k, t), taken[k],
                                   start=(k == 0), stop=(k == KT - 1))
                    used = start + (k + 1) * nb
                    if t == token_tiles - 1 and k < KT - 1 and used % BLOCKS == 0:
                        mm.then_inc(*streamed.on("chunk", used // BLOCKS - 1))
                mm.then_inc(*streamed.on(tag, g0 + t, also=chunk_end() if t == token_tiles - 1 else None))

        def values_move(engine, which, tag, token_tiles, dst, width, g0=0):
            for t in range(token_tiles):
                if (g0 + t) % 2 != which:
                    continue
                engine.wait_ge(*streamed.at(tag, g0 + t))
                s = ps[:, (g0 + t) % 8, 0:width]
                if which == 0:
                    nc.scalar.activation(dst(t), s, ACT.Copy).then_inc(*act_moved.on(tag, g0 + t))
                else:
                    nc.vector.tensor_copy(dst(t), s).then_inc(*dve_moved.on(tag, g0 + t))

        def branch_pe(pe, tag, K, rhs):
            for m in range(KT):
                for b, (what, kk, r) in enumerate((("gate", KT, hs), ("y", K, rhs))):
                    if m >= 3:
                        pe.wait_ge(*(gated.at(tag, m - 3) if b == 0 else fused.at(tag, m - 3, "y")))
                    for half in range(2):
                        for k in range(half * kk // 2, (half + 1) * kk // 2):
                            w = take(pe)
                            mm = pe.matmul(ps[:, (2 * m + b) % 6, :], w, r(k, 0, SEQ), start=(k == 0), stop=(k == kk - 1))
                            if k == kk - 1:
                                mm.then_inc(*streamed.on(tag, what, m, 0, also=chunk_end()))
                            elif chunk_end():
                                mm.then_inc(*streamed.on(*chunk_end()))
                        a = 2 * b + half
                        if a == 0 and m >= 2:
                            pe.wait_ge(*dve_moved.at(tag, "ada", m - 2))
                        for k in range(KT):
                            w = take(pe)
                            mm = pe.matmul(ps[:, 6 + m % 2, 2 * a:2 * a + 2], w, silu_c[:, k, :],
                                           start=(k == 0), stop=(k == KT - 1))
                            if a == ADA_STEP - 1 and k == KT - 1:
                                mm.then_inc(*streamed.on(tag, "ada", m, also=chunk_end()))
                            elif chunk_end():
                                mm.then_inc(*streamed.on(*chunk_end()))

        def branch_act(act, tag):
            for m in range(KT):
                act.wait_ge(*streamed.at(tag, "gate", m, 0))
                if m >= 2:
                    act.wait_ge(*fused.at(tag, m - 2, "y"))
                nc.scalar.activation(tmp[:, m % 2, :], ps[:, (2 * m) % 6, :], ACT.Sigmoid).then_inc(*gated.on(tag, m))

        def branch_dve(dve, tag, number):
            for m in range(KT):
                dve.wait_ge(*gated.at(tag, m))
                dve.wait_ge(*streamed.at(tag, "y", m, 0))
                y = ps[:, (2 * m + 1) % 6, :]
                if number == 0:
                    nc.vector.tensor_tensor(mixed_sum[:, m, :], tmp[:, m % 2, :], y, ALU.mult)\
                        .then_inc(*fused.on(tag, m, "y"))
                else:
                    if m >= 2:
                        dve.wait_ge(*fused.at(tag, m - 2, "sum"))
                    nc.vector.tensor_tensor(tmp[:, 2 + m % 2, :], tmp[:, m % 2, :], y, ALU.mult)\
                        .then_inc(*fused.on(tag, m, "y"))
                    dve.wait_ge(*fused.at(tag, m, "y"))
                    nc.vector.tensor_tensor(mixed_sum[:, m, :], mixed_sum[:, m, :], tmp[:, 2 + m % 2, :], ALU.add)\
                        .then_inc(*fused.on(tag, m, "sum"))
                dve.wait_ge(*streamed.at(tag, "ada", m))
                n, a = 2 * ADA_STEP, (number * KT + m) * 2 * ADA_STEP
                nc.vector.tensor_tensor(mods[:].rearrange("p a b -> p (a b)")[:, a:a + n], ps[:, 6 + m % 2, 0:n],
                                        pc("b_ada", a, n), ALU.add).then_inc(*dve_moved.on(tag, "ada", m))

        class Attention:
            def __init__(self, tag, heads, per_head, keys, scale, score, mix, dest, p, pt, bias=None):
                self.tag, self.heads, self.per_head, self.keys, self.scale = tag, heads, per_head, keys, scale
                self.score, self.mix, self.dest, self.p, self.pt, self.bias = score, mix, dest, p, pt, bias
                self.units, self.kt = heads * per_head, keys // P

            def s(self, u):
                return ps[:, 2 * (u % 2):2 * (u % 2) + 2, :].rearrange("p a b -> p (a b)")[:, 0:self.keys]

            def copies(self, u):
                return [act_moved.at(self.tag, "pt", u)] + ([dve_moved.at(self.tag, "pt", u)] if self.kt > 4 else [])

        def attend_pe(pe, a):
            tag = a.tag
            for step in range(a.units + 3):
                u = step
                if u < a.units:
                    if u >= 2:
                        pe.wait_ge(*(fused.at(tag, "biased", u - 2) if a.bias else exped.at(tag, u - 2)))
                    for k0 in range(0, a.keys, 512):
                        kn = min(512, a.keys - k0)
                        lhs, rhs = a.score(u, k0, kn)
                        mm = pe.matmul(ps[:, 2 * (u % 2) + k0 // 512, 0:kn], lhs, rhs, start=True, stop=True)
                    mm.then_inc(*scored.on(tag, u))
                u = step - 2
                if 0 <= u < a.units:
                    pe.wait_ge(*scaled.at(tag, u))
                    if u >= 1:
                        for w in a.copies(u - 1):
                            pe.wait_ge(*w)
                    for t in range(a.kt):
                        mm = pe.transpose(ps[:, 4 + t // 4, (t % 4) * P:(t % 4 + 1) * P],
                                          a.p[:, u % 3, t * P:(t + 1) * P], ident)
                        if t == min(3, a.kt - 1):
                            mm.then_inc(*turned.on(tag, u, 0))
                        elif t == a.kt - 1:
                            mm.then_inc(*turned.on(tag, u, 1))
                u = step - 3
                if u >= 0 and u % a.per_head == a.per_head - 1:
                    hd = u // a.per_head
                    for w in a.copies(u):
                        pe.wait_ge(*w)
                    if hd >= 2:
                        pe.wait_ge(*dve_moved.at(tag, "out", hd - 2))
                    products = a.mix(hd)
                    for o, lhs, rhs, start, stop in products:
                        mm = pe.matmul(o, lhs, rhs, start=start, stop=stop)
                    mm.then_inc(*attended.on(tag, hd))

        def attend_act(act, a):
            tag = a.tag
            for step in range(a.units + 2):
                u = step
                if u < a.units:
                    act.wait_ge(*maxed.at(tag, "negated", u))
                    if u >= 3:
                        act.wait_ge(*turned.at(tag, u - 3, 1 if a.kt > 4 else 0))
                    nc.scalar.activation(a.p[:, u % 3, 0:a.keys], a.p[:, u % 3, 0:a.keys] if a.bias else a.s(u),
                                         ACT.Exp, bias=stat[:, u % 8, 1:2], scale=1.0 if a.bias else a.scale(u),
                                         accum_out=stat[:, u % 8, 2:3]).then_inc(*exped.on(tag, u))
                u = step - 2
                if u >= 0:
                    act.wait_ge(*turned.at(tag, u, 0))
                    hd, q = u // a.per_head, u % a.per_head
                    if hd >= 2 and q == 0:
                        act.wait_ge(*attended.at(tag, hd - 2))
                    n = min(4, a.kt)
                    nc.scalar.activation(a.pt[:, hd % 2, 0:n, q * P:(q + 1) * P],
                                         ps[:, 4, 0:n * P].rearrange("p (t q) -> p t q", t=n), ACT.Copy)\
                        .then_inc(*act_moved.on(tag, "pt", u))

        def attend_dve(dve, a):
            tag = a.tag
            for step in range(a.units + 3):
                u = step
                if u < a.units:
                    s, st = a.s(u), stat[:, u % 8]
                    dve.wait_ge(*scored.at(tag, u))
                    if a.bias:
                        if u >= 3:
                            dve.wait_ge(*turned.at(tag, u - 3, 0))
                        near, mask = a.bias(u)
                        buf = a.p[:, u % 3, 0:a.keys]
                        nc.vector.scalar_tensor_tensor(out=buf.rearrange("p (w r) -> p w r", w=WIN),
                                                       in0=s.rearrange("p (w r) -> p w r", w=WIN), scalar=a.scale(u),
                                                       in1=near, op0=ALU.mult, op1=ALU.add)\
                            .then_inc(*fused.on(tag, "biased", u))
                        dve.wait_ge(*fused.at(tag, "biased", u))
                        nc.vector.tensor_tensor(buf, buf, mask, ALU.add).then_inc(*fused.on(tag, "masked", u))
                        dve.wait_ge(*fused.at(tag, "masked", u))
                        s = buf
                    if u >= 8:
                        dve.wait_ge(*scaled.at(tag, u - 8))
                    nc.vector.reduce_max(st[:, 0:1], s, AX).then_inc(*maxed.on(tag, "max", u))
                    dve.wait_ge(*maxed.at(tag, "max", u))
                    nc.vector.tensor_scalar(st[:, 1:2], st[:, 0:1], -1.0 if a.bias else -a.scale(u), None, ALU.mult)\
                        .then_inc(*maxed.on(tag, "negated", u))
                u = step - 1
                if 0 <= u < a.units:
                    st = stat[:, u % 8]
                    dve.wait_ge(*exped.at(tag, u))
                    nc.vector.reciprocal(st[:, 3:4], st[:, 2:3]).then_inc(*inverted.on(tag, u))
                    dve.wait_ge(*inverted.at(tag, u))
                    nc.vector.tensor_scalar(a.p[:, u % 3, 0:a.keys], a.p[:, u % 3, 0:a.keys], st[:, 3:4], None,
                                            ALU.mult).then_inc(*scaled.on(tag, u))
                u = step - 2
                if 0 <= u < a.units and a.kt > 4:
                    dve.wait_ge(*turned.at(tag, u, 1))
                    hd, q = u // a.per_head, u % a.per_head
                    if hd >= 2 and q == 0:
                        dve.wait_ge(*attended.at(tag, hd - 2))
                    nc.vector.tensor_copy(a.pt[:, hd % 2, 4:6, q * P:(q + 1) * P],
                                          ps[:, 5, 0:2 * P].rearrange("p (t q) -> p t q", t=2))\
                        .then_inc(*dve_moved.on(tag, "pt", u))
                u = step - 3
                if u >= 0 and u % a.per_head == a.per_head - 1:
                    hd = u // a.per_head
                    dve.wait_ge(*attended.at(tag, hd))
                    d, s = a.dest(hd)
                    nc.vector.tensor_copy(d, s).then_inc(*dve_moved.on(tag, "out", hd))

        WIN_AT = [min(max(16 * t - 8, 0), GRID_W - WIN) for t in range(4)]

        def na_score(u, k0, kn):
            hd, t = u // 4, u % 4
            q0 = (hd % 2) * 64
            k0 = WIN_AT[t] * GRID_H
            return na_q[q0:q0 + 64, hd // 2, t * P:(t + 1) * P], na_k[q0:q0 + 64, hd // 2, k0:k0 + 256]

        def na_bias(u):
            hd, t = u // 4, u % 4
            shift = WIN_AT[t] - 16 * t + 15 + 1
            run = rpb[:, hd, shift:shift + 1]
            near = spread(run, (1, WIN), (31, GRID_H))
            kind = {0: 0, 1: 1, 2: 1, 3: 2}[t]
            return near, cc("mask")[:, kind * 256:(kind + 1) * 256]

        def na_mix(hd):
            q0 = (hd % 2) * 64
            return [(ps[q0:q0 + 64, 6 + hd % 2, t * P:(t + 1) * P], na_win[:, 2 * t + kt, hd * 64:(hd + 1) * 64],
                     b1_pt[:, hd % 2, kt, t * P:(t + 1) * P], kt == 0, kt == 1) for t in range(4) for kt in range(2)]

        def na_dest(hd):
            q0 = (hd % 2) * 64
            return (na_o[q0:q0 + 64, hd // 2, :].rearrange("p (r w) -> p r w", w=GRID_W),
                    ps[q0:q0 + 64, 6 + hd % 2, :].rearrange("p (w r) -> p r w", r=GRID_H))

        near_attention = Attention("na", NA_HEADS, 4, 256, lambda u: 64 ** -0.5, na_score, na_mix, na_dest, b1_p, b1_pt, na_bias)
        memory_attention = Attention(
            "xa", XA_HEADS, 4, 256, lambda u: 128 ** -0.5,
            lambda u, k0, kn: (xa_q[:, u // 4, (u % 4) * P:(u % 4 + 1) * P], xa_k[:, u // 4, :]),
            lambda hd: [(ps[:, 6 + hd % 2, :], xa_v[:, kt, hd * P:(hd + 1) * P], b1_pt[:, hd % 2, kt, :], kt == 0, kt == 1)
                        for kt in range(2)],
            lambda hd: (xa_o[:, hd, :], ps[:, 6 + hd % 2, :]), b1_p, b1_pt)

        def head_parts(kind, hd):
            if kind == "mla":
                return mla_q[0:96, hd, :], mla_k[0:96, hd, :], hd * 64, (h, hd // 2, hd % 2)
            if kind == "diff":
                a = (hd % 4) * 32
                return (diff_q[a:a + 32, hd // 4, :], diff_k[a:a + 32, hd // 4, :], 256 + (hd // 2) * 64,
                        ((out_1, out_2)[hd % 2], hd // 4, (hd // 2) % 2))
            a = (hd // 4) * 64
            return gqa_q[a:a + 64, hd % 4, :], gqa_k[a:a + 64, :], 512 + (hd // 4) * 64, (h, 4 + hd // 2, hd % 2)

        KINDS = [("mla", hd, 96 ** -0.5) for hd in range(MLA_H)] + [("gqa", hd, 64 ** -0.5) for hd in range(GQA_H)] + \
                [("diff", hd, 32 ** -0.5) for hd in range(2 * DIFF_H)]

        def block2_attention(l, on_context):
            q0, per_head = (SEQ, 2) if on_context else (0, 4)
            key0, keys = (SEQ, CTX) if on_context else (0, ALL)
            width = per_head * P

            def score(u, k0, kn):
                kind, hd, _ = KINDS[u // per_head]
                q, k, _, _ = head_parts(kind, hd)
                a = q0 + (u % per_head) * P
                return q[:, a:a + P], k[:, key0 + k0:key0 + k0 + kn]

            def mix(n):
                _, _, v0, (_, _, half) = head_parts(*KINDS[n][:2])
                o = ps[half * 64:half * 64 + 64, 6 + n % 2, 0:width]
                last = keys // P - 1
                return [(o, val[:, key0 // P + t, v0:v0 + 64], prob_t[:, n % 2, t, 0:width], t == 0, t == last)
                        for t in range(last + 1)]

            def dest(n):
                _, _, _, (buf, tile, half) = head_parts(*KINDS[n][:2])
                a = half * 64
                return buf[a:a + 64, tile, q0:q0 + width], ps[a:a + 64, 6 + n % 2, 0:width]
            return Attention(("heads", l, on_context), len(KINDS), per_head, keys, lambda u: KINDS[u // per_head][2],
                             score, mix, dest, prob, prob_t)

        attentions = {l: [block2_attention(l, c) for c in ([False, True] if l < LAYERS - 1 else [False])]
                      for l in range(LAYERS)}

        rope1 = [(ret_q[:, t, :], 0, P, "rot128", trig128[:, 0, :], trig128[:, 1, :]) for t in range(4)]
        rope1 += [(ret_k[:, t, :], 0, P, "rot128", trig128[:, 0, :], trig128[:, 1, :]) for t in range(4)]

        def full(kind, buf):
            return buf, 0, P, "rot64" if kind == "large" else "rot32", *(trig[:, (0 if kind == "large" else 2) + j, :]
                                                                         for j in range(2))

        rope2 = [full("large", gqa_q[:, t, 0:SEQ]) for t in range(4)] + [full("large", gqa_k[:, 0:SEQ])]
        rope2 += [full("small", b[:, t, 0:SEQ]) for b in (diff_q, diff_k) for t in range(2)]
        rope2 += [(b, 64, 32, "rot32", trig[:, 2, :], trig[:, 3, :])
                  for b in [k_pe[:, 0:SEQ]] + [mla_q[:, t, 0:SEQ] for t in range(4)]]

        def rope_pe(pe, tag, jobs):
            for j, (a, p0, n, m, c, s) in enumerate(jobs):
                if j >= 8:
                    pe.wait_ge(*roped.at(tag, "sine", j - 8))
                pe.matmul(ps[p0:p0 + n, j % 8, :], cc(m)[p0:p0 + n, p0:p0 + n], a[p0:p0 + n], start=True, stop=True)\
                    .then_inc(*multiplied.on(tag, j))

        def rope_dve(dve, tag, jobs):
            for j, (a, p0, n, m, c, s) in enumerate(jobs):
                a = a[p0:p0 + n]
                t = tmp[p0:p0 + n, j % 4, :]
                dve.wait_ge(*multiplied.at(tag, j))
                if j >= 4:
                    dve.wait_ge(*roped.at(tag, "sum", j - 4))
                nc.vector.tensor_tensor(t, ps[p0:p0 + n, j % 8, :], s[p0:p0 + n], ALU.mult).then_inc(*roped.on(tag, "sine", j))
                nc.vector.tensor_tensor(a, a, c[p0:p0 + n], ALU.mult).then_inc(*roped.on(tag, "cosine", j))
                dve.wait_ge(*roped.at(tag, "cosine", j))
                nc.vector.tensor_tensor(a, a, t, ALU.add).then_inc(*roped.on(tag, "sum", j))

        def to_tiles(*bufs):
            flat = [b[:, t, :] for b in bufs for t in range(b.shape[1])]
            return lambda m, c0, cn, s: (flat[m][:, c0:c0 + cn], s)

        def na_store(m, c0, cn, s):
            d = (na_q, na_k, na_v)[m // 4][:, m % 4, :]
            return d.rearrange("p (w r) -> p r w", r=GRID_H), s.rearrange("p (r w) -> p r w", w=GRID_W)

        def in2_store(m, c0, cn, s):
            flat = [q_low[:, 0], q_low[:, 1], diff_q[:, 0], diff_q[:, 1]] + [gqa_q[:, t] for t in range(4)] + \
                   [kv_low, k_pe, diff_k[:, 0], diff_k[:, 1], gqa_k]
            return flat[m][:, c0:c0 + cn], s

        def seq_only(m):
            return SEQ_ONLY

        def in2_pieces(l):
            return lambda m: SEQ_ONLY if m < 8 and l == LAYERS - 1 else BOTH

        plain = {
            "ret_qk": (8, KT, hs, seq_only, to_tiles(ret_q, ret_k)),
            "na_in": (12, KT, hs, seq_only, na_store),
            "xa_k": (4, KT, lambda k, c0, cn: h[:, k, SEQ:ALL], lambda m: [(0, CTX)], to_tiles(xa_k)),
            "xa_q": (4, KT, hs, seq_only, to_tiles(xa_q)),
        }
        for l in range(LAYERS):
            own = (lambda m: BOTH) if l < LAYERS - 1 else seq_only
            plain["in2", l] = (13, KT, hs, in2_pieces(l), in2_store)
            plain["out2", l] = (KT, KT, hs, own, to_tiles(attn_y))
            plain["down", l] = (KT, HT, lambda k, c0, cn: ffn_hid[:, k, c0:c0 + cn], own, to_tiles(ffn_y))

        def run_plain(e, which, tag, ready=None):
            ms, K, rhs, pieces_of, dst = plain[tag]
            if which == "pe":
                project_pe(e, tag, ms, K, rhs, pieces_of, ready)
            else:
                project_move(e, which, tag, ms, pieces_of, dst)

        def h_tokens(c):
            return lambda k, t: h[:, k, c + t * P:c + (t + 1) * P]

        value_stages = {
            "ret_v0": (4, h_tokens(0), 4, lambda t: ret_v[:, t, 0:512]),
            "ret_v1": (4, h_tokens(0), 4, lambda t: ret_v[:, t, 512:1024]),
            "xa_v": (2, h_tokens(SEQ), 4, lambda t: xa_v[:, t, :]),
        }
        for l in range(LAYERS):
            value_stages["diff_v", l] = (6, h_tokens(0), 2, lambda t: val[:, t, 256:512])
            value_stages["gqa_v", l] = (6, h_tokens(0), 1, lambda t: val[:, t, 512:640])

        def run_values(e, which, tag):
            n, lhs, nb, dst = value_stages[tag]
            if which == "pe":
                values_pe(e, tag, n, lhs, nb)
            else:
                values_move(e, which, tag, n, dst, nb * P)

        qb = w_small[:, 0:768].rearrange("p (k n) -> p k n", k=2)
        kvb = w_small[:, 768:1280]

        def lifts(l):
            own = BOTH if l < LAYERS - 1 else SEQ_ONLY
            jobs = []
            for hd in range(MLA_H):
                for c0, cn in own:
                    jobs.append((96, cn, [(qb[:, k, hd * 96:hd * 96 + 96], q_low[:, k, c0:c0 + cn]) for k in range(2)],
                                 mla_q[0:96, hd, c0:c0 + cn]))
                for c0, cn in BOTH:
                    jobs.append((64, cn, [(kvb[:, hd * P:hd * P + 64], kv_low[:, c0:c0 + cn])], mla_k[0:64, hd, c0:c0 + cn]))
            v = kvb.rearrange("p (h n) -> p h n", h=MLA_H)[:, :, 64:128]
            for t in range(6):
                jobs.append((P, 256, [(kv_low[:, t * P:(t + 1) * P], v)], val[:, t, 0:256]))
            return jobs

        def lift_pe(pe, l):
            jobs = lifts(l)
            for g, (n, cn, products, _) in enumerate(jobs):
                if g >= 8:
                    pe.wait_ge(*moved_at(("lift", l), g - 8))
                for k, (lhs, rhs) in enumerate(products):
                    mm = pe.matmul(ps[0:n, g % 8, 0:cn], lhs, rhs, start=(k == 0), stop=(k == len(products) - 1))
                mm.then_inc(*multiplied.on("lift", l, g))

        def lift_move(e, which, l):
            jobs = lifts(l)
            for g, (n, cn, _, d) in enumerate(jobs):
                if g % 2 != which:
                    continue
                e.wait_ge(*multiplied.at("lift", l, g))
                also = ("lift done", l) if g >= len(jobs) - 2 else None
                s = ps[0:n, g % 8, 0:cn]
                if which == 0:
                    nc.scalar.activation(d, s, ACT.Copy).then_inc(*act_moved.on(("lift", l), g, also=also))
                else:
                    nc.vector.tensor_copy(d, s).then_inc(*dve_moved.on(("lift", l), g, also=also))

        FFN_LOOP = HT // RING

        @block.tensor
        def _(pe):
            def begin(wait=True):
                stage("pe", pe, wait)

            pe.wait_ge(inputs_loaded, 16 * 8)
            norm_pe(pe, "norm_x", job_of["norm_x"])
            begin(wait=False)
            run_plain(pe, "pe", "ret_qk", after_norm(pe, "norm_x"))
            begin()
            run_values(pe, "pe", "ret_v0")
            begin()
            run_values(pe, "pe", "ret_v1")
            begin()
            rope_pe(pe, "rope1", rope1)
            begin()
            for hd in range(RET_HEADS):
                for jt in range(4):
                    if hd:
                        pe.wait_ge(*fused.at("decayed", hd - 1, jt))
                    pe.matmul(ps[:, jt, :], ret_k[:, hd, jt * P:(jt + 1) * P], ret_q[:, hd, :], start=True, stop=True)\
                        .then_inc(*scored.on("ret", hd, jt))
                for e in range(2):
                    if hd:
                        pe.wait_ge(*act_moved.at("ret_y", hd - 1, e))
                    for jt in range(4):
                        pe.wait_ge(*fused.at("decayed", hd, jt))
                        mm = pe.matmul(ps[:, 4 + e, :], ret_v[:, jt, hd * 256 + e * P:hd * 256 + (e + 1) * P],
                                       ret_s[:, jt, :], start=(jt == 0), stop=(jt == 3))
                    mm.then_inc(*attended.on("ret", hd, e))
            begin()
            for hd in range(RET_HEADS):
                for e in range(2):
                    mm = pe.matmul(ps[:, hd, :], ones, ret_y[:, 2 * hd + e, :], start=(e == 0), stop=(e == 1))
                mm.then_inc(*summed.on("ret_mean", hd))
            begin()
            norm_pe(pe, "ret_norm", job_of["ret_norm"])
            begin()
            for m in range(8):
                group(pe, ("ret_gate", m), [m], hs, KT, SEQ_ONLY)
            begin()
            branch_pe(pe, "ret_out", 8, lambda k, c0, cn: ret_y[:, k, :])
            begin()
            run_plain(pe, "pe", "na_in")
            begin()
            for w in range(8):
                k0 = WIN_AT[w // 2] * GRID_H + (w % 2) * P
                for c in range(4):
                    mm = pe.transpose(ps[:, w, c * P:(c + 1) * P], na_v[:, c, k0:k0 + P], ident)
                mm.then_inc(*turned.on("windows", w))
            begin()
            attend_pe(pe, near_attention)
            begin()
            branch_pe(pe, "na_out", 4, lambda k, c0, cn: na_o[:, k, :])
            begin()
            run_plain(pe, "pe", "xa_k")
            begin()
            run_values(pe, "pe", "xa_v")
            begin()
            run_plain(pe, "pe", "xa_q")
            begin()
            attend_pe(pe, memory_attention)
            begin()
            branch_pe(pe, "xa_out", 4, lambda k, c0, cn: xa_o[:, k, :])
            begin()
            for m in range(KT):
                group(pe, ("mix_out", m), [m], lambda k, c0, cn: mixed_sum[:, k, :], KT, SEQ_ONLY)
            begin()
            norm_pe(pe, "norm_moe", job_of["norm_moe"])
            begin(wait=False)
            ready = after_norm(pe, "norm_moe")
            for t in range(4):
                for k in range(KT):
                    if t == 0:
                        ready(k, 0)
                    mm = pe.matmul(ps[:, 0, t * 20:(t + 1) * 20], h[:, k, t * P:(t + 1) * P], w_router[:, k, :],
                                   start=(k == 0), stop=(k == KT - 1))
            mm.then_inc(*multiplied.on("logits"))
            for t in range(4):
                for half in range(2):
                    g = 2 * t + half
                    bank = 4 + g % 4
                    if g >= 4:
                        pe.wait_ge(*act_moved.at("h_tok", g - 4))
                    for k in range(4):
                        mm = pe.transpose(ps[:, bank, k * P:(k + 1) * P], h[:, 4 * half + k, t * P:(t + 1) * P], ident)
                    mm.then_inc(*turned.on("h_tok", g))
            pe.wait_ge(*small.at("group", "hit"))
            for t in range(4):
                for t2 in range(t + 1):
                    pe.matmul(ps[:, 1, t * 4:t * 4 + 4], ones if t2 < t else cc("before"), R["g1"][:, t2, :],
                              start=(t2 == 0), stop=(t2 == t))
            for t in range(4):
                mm = pe.matmul(ps[:, 1, 16:20], ones, R["g1"][:, t, :], start=(t == 0), stop=(t == 3))
            mm.then_inc(*multiplied.on("places"))
            pe.wait_ge(*small.at("slot diagonal", 3))
            pe.matmul(ps[:, 2, :], ones, tmp[:, 0, :], start=True, stop=True).then_inc(*multiplied.on("slot row"))
            pe.wait_ge(*small.at("picked", 3))
            pe.wait_ge(*small.at("expert weights"))
            for u in range(UNITS):
                for t in range(4):
                    mm = pe.matmul(ps[:, 3, 4 * u:4 * u + 4], pick[:, t, u * P:(u + 1) * P], R["ee"][:, t, :],
                                   start=(t == 0), stop=(t == 3))
            mm.then_inc(*multiplied.on("slot weights"))

            def gather(slots_of, bank, half, key):
                for k in range(4):
                    for t in range(4):
                        mm = pe.matmul(ps[:, bank, k * P:(k + 1) * P],
                                       h_tok[:, t, (4 * half + k) * P:(4 * half + k + 1) * P], slots_of(t),
                                       start=(t == 0), stop=(t == 3))
                mm.then_inc(*attended.on("gather", key, half))

            for half in range(2):
                pe.wait_ge(*act_moved.at("h_tok", 7))
                gather(lambda t: pick[:, t, 0:P], (7, 0)[half], half, "first")
            begin()
            assert chunks.block == MOE_FIRST * BLOCKS
            with repeated(pe, UNITS, signals["pe"]) as i:
                before = chunks.block

                def gate_or_up(e, what, bank):
                    for k in range(KT):
                        w = take(pe, i, count=4)
                        mm = pe.matmul(ps[:, bank, :], unit_h[:, k, :], w, start=(k == 0), stop=(k == KT - 1))
                        if k == KT - 1:
                            mm.then_inc(*streamed.on("moe", what, e, also=chunk_end()))
                        elif chunk_end():
                            mm.then_inc(*streamed.on(*chunk_end()))

                def turn(e):
                    pe.wait_ge(*fused.at("moe", "hid", e, i=i))
                    if e == IN_GROUP - 1:
                        pe.wait_ge(*act_moved.at("moe", "hid_t", e - 1, i=i))
                    for f in range(4):
                        mm = pe.transpose(ps[:, 4, f * P:(f + 1) * P], hid[:, e % 2, f * P:(f + 1) * P], ident)
                    mm.then_inc(*turned.on("moe", e))

                def down(e):
                    pe.wait_ge(*act_moved.at("moe", "hid_t", e, i=i))
                    for k in range(4):
                        for half in range(2):
                            w = take(pe, i, count=4)
                            mm = pe.matmul(ps[:, 5 + half, :], hid_t[:, e % 2, k, :], w, start=(e == 0 and k == 0),
                                           stop=(e == IN_GROUP - 1 and k == 3))
                            if e == IN_GROUP - 1 and k == 3:
                                mm.then_inc(*streamed.on("moe", "down", half, also=chunk_end()))
                            elif chunk_end():
                                mm.then_inc(*streamed.on(*chunk_end()))

                pe.wait_ge(*act_moved.at("gather", "next", i=i - 1))
                pe.wait_ge(*dve_moved.at("gather", "next", i=i - 1))
                for e in range(IN_GROUP):
                    if e >= 2:
                        pe.wait_ge(*gated.at("moe", e - 2, i=i))
                    gate_or_up(e, "gate", 2 * (e % 2))
                    if e >= 1:
                        turn(e - 1)
                    if e >= 2:
                        pe.wait_ge(*fused.at("moe", "hid", e - 2, i=i))
                    gate_or_up(e, "up", 2 * (e % 2) + 1)
                    if e == 1:
                        pe.wait_ge(*act_moved.at("moe", "y", i=i - 1))
                        pe.wait_ge(*dve_moved.at("moe", "y", i=i - 1))
                    if 1 <= e < IN_GROUP - 1:
                        down(e - 1)
                for half in range(2):
                    gather(lambda t: pick[:, t, bass.ds(i * P + P, P)], (7, 0)[half], half, "next")
                turn(IN_GROUP - 1)
                down(IN_GROUP - 2)
                down(IN_GROUP - 1)
                assert chunks.block - before == UNIT_CHUNKS * BLOCKS
            chunks.block += UNIT_CHUNKS * BLOCKS * (UNITS - 1)
            begin()
            for m in range(KT):
                for u in range(UNITS):
                    pe.wait_ge(*small.at("put", u))
                    mm = pe.matmul(ps[:, m, :], unit_y[:, u * D + m * P:u * D + (m + 1) * P], put[:, u, :],
                                   start=(u == 0), stop=(u == UNITS - 1))
                mm.then_inc(*attended.on("put", m))
            begin()
            norm_pe(pe, "norm_first", job_of["norm_first"])
            begin()
            for l in range(LAYERS):
                own = BOTH if l < LAYERS - 1 else SEQ_ONLY
                norm_pe(pe, ("attn_pre", l), job_of["attn_pre", l])
                pe.wait_ge(*small.at("lambda products", l))
                pe.matmul(ps[:, 7, 0:2], ones[0:32, :], cols[0:32, 2:4], start=True, stop=True)\
                    .then_inc(*multiplied.on("lambda", l))
                begin(wait=False)
                ready = after_norm(pe, ("attn_pre", l), shifted=True)
                pe.wait_ge(*exped.at("lambda", l))
                if l == LAYERS - 1:
                    for k in range(KT):
                        ready(k, 1)
                run_plain(pe, "pe", ("in2", l), ready)
                begin()
                run_values(pe, "pe", ("diff_v", l))
                begin()
                run_values(pe, "pe", ("gqa_v", l))
                begin()
                norm_pe(pe, ("low", l), job_of["low", l])
                begin()
                pe.wait_ge(late_loaded, 16 * (2 + l))
                lift_pe(pe, l)
                begin()
                rope_pe(pe, ("rope2", l), rope2)
                begin()
                for a in attentions[l]:
                    attend_pe(pe, a)
                    begin()
                begin()
                norm_pe(pe, ("diff", l), job_of["diff", l])
                begin()
                run_plain(pe, "pe", ("out2", l))
                begin()
                norm_pe(pe, ("attn_post", l), job_of["attn_post", l])
                begin()
                norm_pe(pe, ("ffn_pre", l), job_of["ffn_pre", l])
                begin(wait=False)
                n = len(own)
                first_chunk(pe, [("ffn", l, what, 0) for what in ("gate", "up")],
                            [[2 * b + pi for pi in range(n)] for b in range(2)], hs, own,
                            after_norm(pe, ("ffn_pre", l), shifted=True))
                for m in range(1, HT):
                    for b, what in enumerate(("gate", "up")):
                        if m >= 2:
                            for pi in range(n):
                                pe.wait_ge(*(gated if b == 0 else fused).at("ffn", l, m - 2, pi))
                        group(pe, ("ffn", l, what, m), [4 * (m % 2) + 2 * b + pi for pi in range(n)], hs, KT, own)
                begin()
                run_plain(pe, "pe", ("down", l))
                begin()
                norm_pe(pe, ("ffn_post", l), job_of["ffn_post", l])
                begin()
            assert chunks.block == (n_chunks + (UNITS - GROUPS) * UNIT_CHUNKS) * BLOCKS

        @block.scalar
        def _(act):
            def begin(wait=True):
                stage("act", act, wait)

            act.wait_ge(inputs_loaded, 16 * 8)
            act.wait_ge(*small.at("epsilons"))
            norm_act(act, "norm_x", job_of["norm_x"])
            begin()
            nc.scalar.activation(silu_c[:].rearrange("p a b -> p (a b)"), pc("c", 0, 16), ACT.Silu).then_inc(*act_moved.on("silu_c"))
            nc.scalar.activation(route[:, 0:8], pc("decay", 0, 8), ACT.Abs).then_inc(*act_moved.on("abs"))
            act.wait_ge(*act_moved.at("abs"))
            nc.scalar.activation(route[:, 8:16], route[:, 0:8], ACT.Exp, scale=-1.0).then_inc(*exped.on("decay"))
            act.wait_ge(*small.at("one plus"))
            nc.scalar.activation(route[:, 24:32], route[:, 16:24], ACT.Ln).then_inc(*exped.on("decay log"))
            run_plain(act, 0, "ret_qk")
            begin()
            run_values(act, 0, "ret_v0")
            begin()
            run_values(act, 0, "ret_v1")
            begin()
            begin()
            for hd in range(RET_HEADS):
                act.wait_ge(*fused.at("exponent", hd))
                if hd >= 2:
                    act.wait_ge(*fused.at("decayed", hd - 2, 3))
                nc.scalar.activation(ret_e[:, hd % 2, :], ret_t, ACT.Exp).then_inc(*exped.on("ret", hd))
                for e in range(2):
                    act.wait_ge(*attended.at("ret", hd, e))
                    nc.scalar.activation(ret_y[:, 2 * hd + e, :], ps[:, 4 + e, :], ACT.Copy).then_inc(*act_moved.on("ret_y", hd, e))
            begin()
            begin()
            norm_act(act, "ret_norm", job_of["ret_norm"])
            begin()
            for m in range(8):
                act.wait_ge(*streamed.at("ret_gate", m, 0))
                nc.scalar.activation(tmp[:, m, :], ps[:, m, :], ACT.Silu).then_inc(*gated.on("ret_gate", m))
            begin()
            branch_act(act, "ret_out")
            begin()
            run_plain(act, 0, "na_in")
            begin()
            for w in range(0, 8, 2):
                act.wait_ge(*turned.at("windows", w))
                nc.scalar.activation(na_win[:, w, :], ps[:, w, :], ACT.Copy).then_inc(*act_moved.on("windows", w))
            begin()
            attend_act(act, near_attention)
            begin()
            branch_act(act, "na_out")
            begin()
            run_plain(act, 0, "xa_k")
            begin()
            run_values(act, 0, "xa_v")
            begin()
            run_plain(act, 0, "xa_q")
            begin()
            attend_act(act, memory_attention)
            begin()
            branch_act(act, "xa_out")
            begin()
            begin()
            norm_act(act, "norm_moe", job_of["norm_moe"])
            begin()
            act.wait_ge(*small.at("group distance"))
            nc.scalar.activation(R["ge"], R["gd"], ACT.Exp).then_inc(*exped.on("groups"))
            act.wait_ge(*small.at("expert distance"))
            nc.scalar.activation(R["ee"], R["ed"], ACT.Exp).then_inc(*exped.on("experts"))
            for g in range(8):
                act.wait_ge(*turned.at("h_tok", g))
                nc.scalar.activation(h_tok[:, g // 2, (g % 2) * 512:(g % 2) * 512 + 512], ps[:, 4 + g % 4, :], ACT.Copy)\
                    .then_inc(*act_moved.on("h_tok", g))
            act.wait_ge(*attended.at("gather", "first", 0))
            nc.scalar.activation(unit_h[:, 0:4, :].rearrange("p a b -> p (a b)"), ps[:, 7, :], ACT.Copy)\
                .then_inc(*act_moved.on("gather", "first"))
            begin()
            with repeated(act, UNITS, signals["act"]) as i:
                for e in range(IN_GROUP):
                    act.wait_ge(*streamed.at("moe", "gate", e, i=i))
                    if e >= 2:
                        act.wait_ge(*fused.at("moe", "hid", e - 2, i=i))
                    nc.scalar.activation(tmp[:, e % 2, :], ps[:, 2 * (e % 2), :], ACT.Silu).then_inc(*gated.on("moe", e))
                    if e >= 1:
                        act.wait_ge(*turned.at("moe", e - 1, i=i))
                        nc.scalar.activation(hid_t[:, (e - 1) % 2].rearrange("p a b -> p (a b)"), ps[:, 4, :], ACT.Copy)\
                            .then_inc(*act_moved.on("moe", "hid_t", e - 1))
                act.wait_ge(*attended.at("gather", "next", 0, i=i))
                nc.scalar.activation(unit_h[:, 0:4, :].rearrange("p a b -> p (a b)"), ps[:, 7, :], ACT.Copy)\
                    .then_inc(*act_moved.on("gather", "next"))
                e = IN_GROUP - 1
                act.wait_ge(*turned.at("moe", e, i=i))
                nc.scalar.activation(hid_t[:, e % 2].rearrange("p a b -> p (a b)"), ps[:, 4, :], ACT.Copy)\
                    .then_inc(*act_moved.on("moe", "hid_t", e))
                act.wait_ge(*streamed.at("moe", "down", 0, i=i))
                nc.scalar.activation(unit_y[:, bass.ds(i * D, 512)], ps[:, 5, :], ACT.Copy).then_inc(*act_moved.on("moe", "y"))
            begin()
            begin()
            norm_act(act, "norm_first", job_of["norm_first"])
            begin()
            for l in range(LAYERS):
                own = BOTH if l < LAYERS - 1 else SEQ_ONLY
                if l == 0:
                    act.wait_ge(context_loaded, 16)
                norm_act(act, ("attn_pre", l), job_of["attn_pre", l], x_ready(("ffn_post", l - 1)) if l else None)
                act.wait_ge(*multiplied.at("lambda", l))
                nc.scalar.activation(cols[:, 4:6], ps[:, 7, 0:2], ACT.Exp).then_inc(*exped.on("lambda", l))
                begin()
                run_plain(act, 0, ("in2", l))
                begin()
                run_values(act, 0, ("diff_v", l))
                begin()
                run_values(act, 0, ("gqa_v", l))
                begin()
                norm_act(act, ("low", l), job_of["low", l])
                begin()
                lift_move(act, 0, l)
                begin()
                begin()
                for a in attentions[l]:
                    attend_act(act, a)
                    begin()
                begin()
                norm_act(act, ("diff", l), job_of["diff", l])
                begin()
                run_plain(act, 0, ("out2", l))
                begin(wait=False)
                norm_act(act, ("attn_post", l), job_of["attn_post", l], moved_ready(("out2", l), len(own)))
                begin(wait=False)
                norm_act(act, ("ffn_pre", l), job_of["ffn_pre", l], x_ready(("attn_post", l)))
                begin()
                for m in range(HT):
                    for pi, (c0, cn) in enumerate(own):
                        act.wait_ge(*streamed.at("ffn", l, "gate", m, pi))
                        if m >= 2:
                            act.wait_ge(*fused.at("ffn", l, m - 2, pi))
                        nc.scalar.activation(tmp[:, 2 * (m % 2) + pi, 0:cn], ps[:, 4 * (m % 2) + pi, 0:cn], ACT.Silu)\
                            .then_inc(*gated.on("ffn", l, m, pi))
                begin()
                run_plain(act, 0, ("down", l))
                begin(wait=False)
                norm_act(act, ("ffn_post", l), job_of["ffn_post", l], moved_ready(("down", l), len(own)))
                begin(wait=False)

        @block.vector
        def _(dve):
            def begin(wait=True):
                stage("dve", dve, wait)

            def then(instruction, *key):
                instruction.then_inc(*small.on(*key))
                dve.wait_ge(*small.at(*key))

            nc.vector.memset(cols[:, 0:1], 1e-6).then_inc(*small.on("epsilon norm"))
            nc.vector.memset(cols[:, 1:2], 1e-5).then_inc(*small.on("epsilons"))
            dve.wait_ge(inputs_loaded, 16 * 8)
            norm_dve(dve, "norm_x", job_of["norm_x"])
            begin()
            e_, one_e, ln_e, d_, eq_, t_ = (route[:, a:a + 8] for a in (8, 16, 24, 32, 40, 48))
            dve.wait_ge(*exped.at("decay"))
            nc.vector.tensor_scalar(one_e, e_, 1.0, None, ALU.add).then_inc(*small.on("one plus"))
            dve.wait_ge(*small.at("one plus"))
            then(nc.vector.tensor_scalar(d_, one_e, -1.0, None, ALU.add), "lg", 0)
            then(nc.vector.tensor_scalar(eq_, d_, 0.0, None, ALU.is_equal), "lg", 1)
            then(nc.vector.tensor_tensor(d_, d_, eq_, ALU.add), "lg", 2)
            then(nc.vector.reciprocal(d_, d_), "lg", 3)
            dve.wait_ge(*exped.at("decay log"))
            then(nc.vector.tensor_tensor(ln_e, ln_e, eq_, ALU.add), "lg", 4)
            then(nc.vector.tensor_tensor(d_, d_, e_, ALU.mult), "lg", 5)
            then(nc.vector.tensor_tensor(d_, d_, ln_e, ALU.mult), "lg", 6)
            then(nc.vector.tensor_scalar(t_, pc("decay", 0, 8), 0.0, None, ALU.min), "lg", 7)
            then(nc.vector.tensor_tensor(route[:, 56:64], t_, d_, ALU.subtract), "lg", 8)
            lg = route[:, 56:64]
            run_plain(dve, 1, "ret_qk")
            begin()
            run_values(dve, 1, "ret_v0")
            begin()
            run_values(dve, 1, "ret_v1")
            begin()
            rope_dve(dve, "rope1", rope1)
            begin()
            for hd in range(RET_HEADS):
                if hd:
                    dve.wait_ge(*exped.at("ret", hd - 1))
                nc.vector.tensor_scalar(ret_t, dist[:, 1, :], lg[:, 4 + hd:5 + hd], None, ALU.mult)\
                    .then_inc(*fused.on("backward", hd))
                dve.wait_ge(*fused.at("backward", hd))
                nc.vector.scalar_tensor_tensor(out=ret_t, in0=dist[:, 0, :], scalar=lg[:, hd:hd + 1], in1=ret_t,
                                               op0=ALU.mult, op1=ALU.add).then_inc(*fused.on("exponent", hd))
                dve.wait_ge(*exped.at("ret", hd))
                for jt in range(4):
                    dve.wait_ge(*scored.at("ret", hd, jt))
                    if hd:
                        dve.wait_ge(*attended.at("ret", hd - 1, 1))
                    a = 3 * P - jt * P
                    nc.vector.scalar_tensor_tensor(out=ret_s[:, jt, :], in0=ps[:, jt, :], scalar=128 ** -0.5,
                                                   in1=ret_e[:, hd % 2, a:a + SEQ], op0=ALU.mult, op1=ALU.mult)\
                        .then_inc(*fused.on("decayed", hd, jt))
            begin()
            for hd in range(RET_HEADS):
                dve.wait_ge(*summed.at("ret_mean", hd))
                for e in range(2):
                    nc.vector.scalar_tensor_tensor(out=ret_y[:, 2 * hd + e, :], in0=ps[:, hd, :], scalar=-1.0 / 256,
                                                   in1=ret_y[:, 2 * hd + e, :], op0=ALU.mult, op1=ALU.add)\
                        .then_inc(*fused.on("centred", hd, e))
            begin()
            norm_dve(dve, "ret_norm", job_of["ret_norm"])
            begin()
            for m in range(8):
                dve.wait_ge(*gated.at("ret_gate", m))
                nc.vector.tensor_tensor(ret_y[:, m, :], ret_y[:, m, :], tmp[:, m, :], ALU.mult).then_inc(*fused.on("ret_gated", m))
            begin()
            branch_dve(dve, "ret_out", 0)
            begin()
            run_plain(dve, 1, "na_in")
            begin()
            for w in range(1, 8, 2):
                dve.wait_ge(*turned.at("windows", w))
                nc.vector.tensor_copy(na_win[:, w, :], ps[:, w, :]).then_inc(*dve_moved.on("windows", w))
            begin()
            attend_dve(dve, near_attention)
            begin()
            branch_dve(dve, "na_out", 1)
            begin()
            run_plain(dve, 1, "xa_k")
            begin()
            run_values(dve, 1, "xa_v")
            begin()
            run_plain(dve, 1, "xa_q")
            begin()
            attend_dve(dve, memory_attention)
            begin()
            branch_dve(dve, "xa_out", 2)
            begin()
            for m in range(KT):
                dve.wait_ge(*streamed.at("mix_out", m, 0))
                nc.vector.tensor_tensor(x[:, m, 0:SEQ], x[:, m, 0:SEQ], ps[:, m, :], ALU.add).then_inc(*dve_moved.on("mix_out", m))
            begin()
            norm_dve(dve, "norm_moe", job_of["norm_moe"])
            begin()
            def wide(ap):
                return spread(ap, (1, 4), (0, 4))

            def first_best(hit, out_, *key):
                then(nc.vector.tensor_tensor(R["cand"], hit, R["rank"], ALU.mult), *key, "rank")
                then(nc.vector.reduce_max(R["best"], R["cand"], AX), *key, "best")
                then(nc.vector.tensor_tensor(out_, R["cand"], wide(R["best"]), ALU.is_equal), *key, "hit")

            dve.wait_ge(*multiplied.at("logits"))
            then(nc.vector.tensor_tensor(R["lg"], ps[:, 0, 0:80].rearrange("p (t n) -> p t n", t=4),
                                         pc("router_bias", 0, 80).rearrange("p (t n) -> p t n", t=4), ALU.add), "logits")
            gl, el = R["lg"][:, :, 0:4], R["lg"][:, :, 4:20]
            then(nc.vector.reduce_max(R["gm"], gl, AX), "group max")
            then(nc.vector.tensor_tensor(R["gd"], gl, wide(R["gm"]), ALU.subtract), "group distance")
            then(nc.vector.tensor_scalar(R["eq"], R["gd"], 0.0, None, ALU.is_ge), "group hits")
            first_best(R["eq"], R["g1"], "group")
            dve.wait_ge(*exped.at("groups"))
            then(nc.vector.reduce_sum(R["gw"], R["ge"], axis=AX), "group sum")
            then(nc.vector.reciprocal(R["gw"], R["gw"]), "group weight")
            g1_wide = spread(R["g1"], (4, 4), (1, 4), (0, 4))
            then(nc.vector.tensor_tensor(R["sel"], el.rearrange("p t (g e) -> p t g e", g=4), g1_wide, ALU.mult), "chosen")
            sel_a = R["sel"]
            then(nc.vector.reduce_sum(R["ig"], sel_a.rearrange("p t g e -> p t e g"), axis=AX), "in group")
            then(nc.vector.reduce_max(R["em"], R["ig"], AX), "expert max")
            then(nc.vector.tensor_tensor(R["ed"], R["ig"], wide(R["em"]), ALU.subtract), "expert distance")
            then(nc.vector.tensor_scalar(R["eq"], R["ed"], 0.0, None, ALU.is_ge), "expert hits")
            first_best(R["eq"], R["o1"], "first")
            then(nc.vector.scalar_tensor_tensor(out=R["e2"], in0=R["o1"], scalar=-BIG, in1=R["ed"], op0=ALU.mult,
                                                op1=ALU.add), "without the first")
            then(nc.vector.reduce_max(R["em"], R["e2"], AX), "second max")
            then(nc.vector.tensor_tensor(R["eq"], R["e2"], wide(R["em"]), ALU.is_equal), "second hits")
            first_best(R["eq"], R["o2"], "second")
            then(nc.vector.tensor_tensor(R["o1"], R["o1"], R["o2"], ALU.add), "both")
            dve.wait_ge(*exped.at("experts"))
            then(nc.vector.tensor_tensor(R["ee"], R["ee"], R["o1"], ALU.mult), "two weights")
            then(nc.vector.reduce_sum(R["em"], R["ee"], axis=AX), "their sum")
            then(nc.vector.reciprocal(R["em"], R["em"]), "its reciprocal")
            then(nc.vector.tensor_tensor(R["em"], R["em"], R["gw"], ALU.mult), "with the group's weight")
            then(nc.vector.tensor_tensor(R["ee"], R["ee"], wide(R["em"]), ALU.mult), "expert weights")
            dve.wait_ge(*multiplied.at("places"))
            then(nc.vector.tensor_copy(R["rk"].rearrange("p a b -> p (a b)"), ps[:, 1, 0:16]), "ranks")
            then(nc.vector.tensor_copy(R["n"], ps[:, 1, 16:20]), "sizes")
            steps = cc("steps").rearrange("p (t n) -> p t n", t=4)
            then(nc.vector.tensor_tensor(R["cmp"], wide(R["n"]), steps, ALU.is_gt), "size steps")
            then(nc.vector.reduce_sum(R["units"], R["cmp"], axis=AX), "units of each group")
            then(nc.vector.memset(R["from"][:, 0:1], 0.0), "first unit", 0)
            for g in range(GROUPS):
                then(nc.vector.tensor_tensor(R["from"][:, g + 1:g + 2], R["from"][:, g:g + 1], R["units"][:, g:g + 1],
                                             ALU.add), "first unit", g + 1)
            no = cc("unit_no").rearrange("p (u g) -> p u g", g=4)
            over = R["over"].rearrange("p (u g) -> p u g", g=4)
            then(nc.vector.tensor_tensor(over, spread(R["from"][:, 1:5], (0, UNITS), (1, 4)), no, ALU.is_le), "groups before")
            then(nc.vector.reduce_sum(R["ug"], over, axis=AX), "group of each unit")
            then(nc.vector.tensor_scalar(unit_group[:, 0:UNITS], R["ug"], float(GROUPS - 1), None, ALU.min), "unit groups")
            then(nc.vector.scalar_tensor_tensor(out=R["rk"], in0=spread(R["from"], (0, 4), (1, 4)), scalar=float(P),
                                                in1=R["rk"], op0=ALU.mult, op1=ALU.add), "slots if in group")
            then(nc.vector.tensor_tensor(R["rk"], R["rk"], R["g1"], ALU.mult), "slot of its group")
            then(nc.vector.reduce_sum(R["slot"], R["rk"], axis=AX), "slots")
            for t in range(4):
                nc.vector.tensor_scalar(tmp[:, 0, t * P:(t + 1) * P], ident, R["slot"][:, t:t + 1], None, ALU.mult)\
                    .then_inc(*small.on("slot diagonal", t))
            dve.wait_ge(slots_loaded, 16)
            for t in range(4):
                nc.vector.tensor_scalar(pick[:, t, :], slot_row, R["slot"][:, t:t + 1], None, ALU.is_equal)\
                    .then_inc(*small.on("picked", t))
            dve.wait_ge(*multiplied.at("slot weights"))
            nc.vector.tensor_copy(R["w"], ps[:, 3, 0:4 * UNITS]).then_inc(*small.on("slot weights"))
            dve.wait_ge(*attended.at("gather", "first", 1))
            nc.vector.tensor_copy(unit_h[:, 4:8, :].rearrange("p a b -> p (a b)"), ps[:, 0, :])\
                .then_inc(*dve_moved.on("gather", "first"))
            for u in range(UNITS):
                nc.vector.tensor_scalar(put[:, u, :], ps[:, 2, :], cc("slot_no")[:, u:u + 1], None, ALU.is_equal)\
                    .then_inc(*small.on("put", u))
            begin()
            with repeated(dve, UNITS, signals["dve"]) as i:
                for e in range(IN_GROUP):
                    dve.wait_ge(*gated.at("moe", e, i=i))
                    dve.wait_ge(*streamed.at("moe", "up", e, i=i))
                    nc.vector.scalar_tensor_tensor(out=hid[:, e % 2, :], in0=tmp[:, e % 2, :],
                                                   scalar=R["w"][:, bass.ds(i * 4 + e, 1)],
                                                   in1=ps[:, 2 * (e % 2) + 1, :], op0=ALU.mult, op1=ALU.mult)\
                        .then_inc(*fused.on("moe", "hid", e))
                dve.wait_ge(*attended.at("gather", "next", 1, i=i))
                nc.vector.tensor_copy(unit_h[:, 4:8, :].rearrange("p a b -> p (a b)"), ps[:, 0, :])\
                    .then_inc(*dve_moved.on("gather", "next"))
                dve.wait_ge(*streamed.at("moe", "down", 1, i=i))
                nc.vector.tensor_copy(unit_y[:, bass.ds(i * D + 512, 512)], ps[:, 6, :]).then_inc(*dve_moved.on("moe", "y"))
            begin()
            for m in range(KT):
                dve.wait_ge(*attended.at("put", m))
                nc.vector.tensor_tensor(x[:, m, 0:SEQ], x[:, m, 0:SEQ], ps[:, m, :], ALU.add)\
                    .then_inc(*dve_moved.on("moe result", m, also=("moe done",) if m == KT - 1 else None))
            begin()
            norm_dve(dve, "norm_first", job_of["norm_first"])
            begin()
            for l in range(LAYERS):
                own = BOTH if l < LAYERS - 1 else SEQ_ONLY
                lam = pc(f"lambda{l}", 0, 4)
                nc.vector.tensor_tensor(cols[:, 2:4], spread(lam, (2, 2)), spread(lam[:, 1:2], (2, 2)), ALU.mult)\
                    .then_inc(*small.on("lambda products", l))

                def gains(kind, name, which, plus, *key):
                    for s in range(2):
                        a = 8 + (kind * 2 + s) * 8
                        m = spread(mods[:, l * 48 + which * 8, s:s + 1], (2, 8))
                        then(nc.vector.scalar_tensor_tensor(out=cols[:, a:a + 8], in0=m, scalar=plus, in1=pc(name, 0, 8),
                                                            op0=ALU.add, op1=ALU.mult), *key, s)
                gains(0, f"attn_pre{l}", 1, 1.0, "attn_pre", l)
                gains(1, f"attn_post{l}", 2, 0.0, "attn_post", l)
                if l == 0:
                    dve.wait_ge(context_loaded, 16)
                norm_dve(dve, ("attn_pre", l), job_of["attn_pre", l])
                dve.wait_ge(*exped.at("lambda", l))
                then(nc.vector.tensor_tensor(cols[:, 7:8], cols[:, 5:6], cols[:, 4:5], ALU.subtract), "lambda", l, 0)
                then(nc.vector.tensor_scalar(cols[:, 7:8], cols[:, 7:8], -LAM_INIT[l], None, ALU.add), "lambda", l, 1)
                then(nc.vector.tensor_scalar(cols[:, 6:7], pc(f"diff_sub{l}"), 1.0 - LAM_INIT[l], None, ALU.mult),
                     "lambda", l, 2)
                begin()
                run_plain(dve, 1, ("in2", l))
                begin()
                run_values(dve, 1, ("diff_v", l))
                begin()
                run_values(dve, 1, ("gqa_v", l))
                begin()
                norm_dve(dve, ("low", l), job_of["low", l])
                begin()
                lift_move(dve, 1, l)
                begin()
                rope_dve(dve, ("rope2", l), rope2)
                dve.wait_ge(*roped.at(("rope2", l), "sum", 9))
                for hd in range(MLA_H):
                    nc.vector.tensor_copy(mla_k[64:96, hd, :], k_pe[64:96, :]).then_inc(*dve_moved.on("k_pe", l, hd))
                begin()
                for a in attentions[l]:
                    attend_dve(dve, a)
                    begin()
                for t in range(2):
                    w = ALL if l < LAYERS - 1 else SEQ
                    nc.vector.scalar_tensor_tensor(out=out_1[:, t, 0:w], in0=out_2[:, t, 0:w], scalar=cols[:, 7:8],
                                                   in1=out_1[:, t, 0:w], op0=ALU.mult, op1=ALU.add)\
                        .then_inc(*fused.on("difference", l, t))
                begin()
                norm_dve(dve, ("diff", l), job_of["diff", l])
                begin()
                run_plain(dve, 1, ("out2", l))
                begin()
                norm_dve(dve, ("attn_post", l), job_of["attn_post", l])
                begin()
                gains(0, f"ffn_pre{l}", 4, 1.0, "ffn_pre", l)
                gains(1, f"ffn_post{l}", 5, 0.0, "ffn_post", l)
                norm_dve(dve, ("ffn_pre", l), job_of["ffn_pre", l])
                begin()
                for m in range(HT):
                    for pi, (c0, cn) in enumerate(own):
                        dve.wait_ge(*gated.at("ffn", l, m, pi))
                        dve.wait_ge(*streamed.at("ffn", l, "up", m, pi))
                        nc.vector.tensor_tensor(ffn_hid[:, m, c0:c0 + cn], tmp[:, 2 * (m % 2) + pi, 0:cn],
                                                ps[:, 4 * (m % 2) + 2 + pi, 0:cn], ALU.mult)\
                            .then_inc(*fused.on("ffn", l, m, pi))
                begin()
                run_plain(dve, 1, ("down", l))
                begin()
                norm_dve(dve, ("ffn_post", l), job_of["ffn_post", l])
                begin()
            normed.points[("final",)] = (normed.n, 0, 1)
    return {**{s.name: s.points for v in signals.values() for s in v}, "ends": ends}


def _blocks(w):
    k, m = w.shape
    return w.reshape(k // P, P, m // P, P).transpose(2, 0, 1, 3).reshape(-1, P, P)


def _side_by_side(w):
    k, m = w.shape
    return w.reshape(k // P, P, m // P, P).transpose(0, 2, 1, 3).reshape(-1, P, P)


def _interleaved(*ws):
    tiles = [_blocks(w).reshape(w.shape[1] // P, w.shape[0] // P, P, P) for w in ws]
    return np.concatenate([t[m] for m in range(tiles[0].shape[0]) for t in tiles])


def _stream(a):
    w, kvw = a["w_in"][0], a["w_mem_kv"][0]
    gates = [w[:, 5120 + b * D:5120 + (b + 1) * D] for b in range(3)]
    ada = _blocks(np.concatenate([a["w_ada_2"][l] for l in range(LAYERS)], axis=1)).reshape(3, KT, ADA_STEP, KT, P, P)

    def branch(b, y):
        out = []
        for m in range(KT):
            for j, v in enumerate((gates[b], y)):
                v = _blocks(v[:, m * P:(m + 1) * P])
                half = v.shape[0] // 2
                out += [v[:half], ada[b, m, 2 * j], v[half:], ada[b, m, 2 * j + 1]]
        return np.concatenate(out)

    out = [_blocks(w[:, 0:1024]), _side_by_side(w[:, 1024:1536]), _side_by_side(w[:, 1536:2048]),
           _blocks(w[:, 2048:3072]), branch(0, a["w_ret_o"][0]), _blocks(w[:, 3072:4608]),
           branch(1, a["w_na_o"][0]), _blocks(kvw[:, 0:512]), _side_by_side(kvw[:, 512:1024]),
           _blocks(w[:, 4608:5120]), branch(2, a["w_xa_o"][0]), _blocks(a["w_out"][0])]
    for g in range(GROUPS):
        gate, up, down = (a[f"w_exp_{n}"][0, g] for n in ("gate", "up", "down"))
        for e in range(IN_GROUP):
            out += [_side_by_side(gate[e]), _side_by_side(up[e])]
            if 1 <= e < IN_GROUP - 1:
                out.append(_side_by_side(down[e - 1]))
        out += [_side_by_side(down[IN_GROUP - 2]), _side_by_side(down[IN_GROUP - 1])]
    for l in range(LAYERS):
        v = a["w_in_2"][l]
        k_pe = np.zeros((D, P), v.dtype)
        k_pe[:, 64:96] = v[:, 384:416]
        gq = v[:, 1184:1696].reshape(D, 2, 4, 64).transpose(0, 2, 1, 3).reshape(D, 512)
        out += [_blocks(np.concatenate([v[:, 0:256], v[:, 416:672], gq, v[:, 256:384], k_pe, v[:, 672:928],
                                        v[:, 1696:1824]], axis=1)),
                _side_by_side(v[:, 928:1184]), _side_by_side(v[:, 1824:1952]), _blocks(a["w_out_2"][l]),
                _interleaved(a["w_ffn_gate_2"][l], a["w_ffn_up_2"][l]), _blocks(a["w_ffn_down_2"][l])]
    out = np.concatenate(out)
    n = out.shape[0] // BLOCKS
    return np.ascontiguousarray(out.reshape(n, BLOCKS, P, P).transpose(0, 2, 1, 3).reshape(n, P, CHUNK))


def _columns(v):
    return v.reshape(-1, P).T


def _params(a):
    lay, n = param_layout()
    out = np.zeros((P, n), np.float32)

    def put(name, v):
        first, w = lay[name]
        out[:v.shape[0], first:first + w] = v

    put("g_mix", _columns(a["g_mix"][0]))
    put("ret_gain", _columns(a["ret_norm_gain"][0]))
    put("g_mem", _columns(a["g_mem"][0]))
    put("g_ffn", _columns(a["g_ffn"][0]))
    put("g_final", _columns(a["g_final"]))
    put("decay", np.broadcast_to(np.concatenate([a["ret_decay_fwd"][0], a["ret_decay_bwd"][0]]), (P, 8)))
    put("router_bias", np.broadcast_to(np.tile(np.concatenate([a["b_router_group"][0], a["b_router_expert"][0]]), 4),
                                       (P, 80)))
    put("c", np.stack([_columns(a["c_2"][0]), _columns(a["c_ctx_2"])], axis=2).reshape(P, 16))
    put("b_ada", np.repeat(_columns(a["b_ada_2"].reshape(-1)), 2, axis=1))
    for l in range(LAYERS):
        for name, source in (("attn_pre", "g_attn_pre_2"), ("attn_post", "g_attn_post_2"), ("mla_q", "g_mla_q_2"),
                             ("mla_kv", "g_mla_kv_2"), ("ffn_pre", "g_ffn_pre_2"), ("ffn_post", "g_ffn_post_2")):
            put(f"{name}{l}", _columns(a[source][l]))
        for name, source in (("diff_sub", "g_diff_sub_2"), ("gqa_q", "g_gqa_q_2"), ("gqa_k", "g_gqa_k_2")):
            put(f"{name}{l}", _columns(np.tile(a[source][l], 2)))
        put(f"lambda{l}", np.stack([a[f"lambda_{n}_2"][l] for n in ("q1", "k1", "q2", "k2")], axis=1))
    return out


def _rotation(half):
    out = np.zeros((P, P), np.float32)
    for m in range(P):
        first = m % (2 * half) < half
        out[m + half if first else m - half, m] = -1.0 if first else 1.0
    return out


def _constants():
    f = np.float32
    lay, n = const_layout()
    con = np.zeros((P, n), f)

    def put(name, v):
        first, w = lay[name]
        con[:, first:first + w] = v

    put("ident", np.eye(P))
    put("ones", 1.0)
    put("ones64", np.kron(np.eye(2), np.ones((64, 64))))
    for half in (64, 32, 16):
        put(f"rot{2 * half}", _rotation(half))
    mask = np.zeros((P, 3, 256), f)
    for kind, (t, start) in enumerate(((0, 0), (1, 8), (3, 32))):
        q = 16 * t + np.arange(P) // 8
        off = (start + np.arange(256) // GRID_H)[None, :] - np.clip(q - 8, 0, 48)[:, None]
        mask[:, kind] = np.where((off >= 0) & (off < 16), 0.0, -BIG)
    put("mask", mask.reshape(P, -1))
    put("rank", np.tile([4.0, 3.0, 2.0, 1.0], 4))
    put("before", np.triu(np.ones((P, P)), 1))
    put("steps", np.tile(np.arange(4.0) * P, 4))
    put("unit_no", np.repeat(np.arange(UNITS), 4))
    put("slot_no", np.arange(P)[:, None] + P * np.arange(UNITS)[None, :])
    delta = np.arange(DIFFS)[None, :] - 3 * P - np.arange(P)[:, None]
    dist = np.stack([np.maximum(delta, 0), np.maximum(-delta, 0)], axis=1).astype(f)

    def trig(ang):
        return [np.cos(ang).T.astype(f), np.sin(ang).T.astype(f)]

    s = np.arange(SEQ, dtype=f)
    inv = (f(10000.0) ** (-np.arange(64, dtype=f) / f(64))).astype(f)
    trig128 = np.stack(trig((s[:, None] * inv[None, :])[:, np.arange(P) % 64]), axis=1)
    both = []
    for quarter in (16, 8):
        inv = (f(10000.0) ** (-np.arange(quarter, dtype=f) / f(quarter))).astype(f)
        row, col = np.floor(s / GRID_W).astype(f), (s % GRID_W).astype(f)
        ang = np.concatenate([row[:, None] * inv, col[:, None] * inv], axis=1)
        both += trig(ang[:, np.arange(P) % (2 * quarter)])
    return {"con": con, "slot_row": np.tile(np.arange(SLOTS, dtype=f), (P, 1)), "dist": dist, "trig128": trig128, "trig": np.stack(both, axis=1)}


def _near_bias(rpb):
    flat = np.pad(rpb.reshape(-1), (16, 32))
    q = np.arange(P)
    first = 16 + (7 - q % 8) * 31 - q // 8 - 1
    at = first[:, None, None] + 465 * np.arange(NA_HEADS)[None, :, None] + np.arange(RPB_RUN)[None, None, :]
    return flat[at]


def _feature_major(v):
    return np.ascontiguousarray(v.reshape(-1, KT, P).transpose(2, 1, 0))


def kernel(**inputs):
    import concourse.bacc as bacc
    from concourse.bass_utils import run_bass_kernel_spmd

    a = {k: np.asarray(v) for k, v in inputs.items()}
    small = [np.concatenate([a["w_mla_qb_2"][l].reshape(2, P, 384).transpose(1, 0, 2).reshape(P, 768),
                             a["w_mla_kvb_2"][l]], axis=1) for l in range(LAYERS)]
    arrays = {"stream": _stream(a), "xT": _feature_major(a["x"][0]), "memT": _feature_major(a["mem"][0]),
              "ctxT": _feature_major(a["ctx_2"][0]), "par": _params(a), "rpb": _near_bias(a["na_rpb"][0]),
              "w_router": np.concatenate([a["w_router_group"][0], a["w_router_expert"][0]], axis=1)
              .reshape(KT, P, 20).transpose(1, 0, 2), "w_small": np.stack(small), **_constants()}
    arrays = {k: np.ascontiguousarray(v) for k, v in arrays.items()}

    def build(known):
        nc = bacc.Bacc("TRN2", target_bir_lowering=False, num_devices=1)
        ins = {n: nc.dram_tensor(f"in_{n}", v.shape, mybir.dt.from_np(v.dtype), kind="ExternalInput").ap()
               for n, v in arrays.items()}
        out = nc.dram_tensor("out_0", (P, KT, SEQ), F32, kind="ExternalOutput").ap()
        return nc, program(nc, ins, out, known)

    _, counted = build({})
    nc, again = build(counted)
    assert again == counted or all(again[k] == counted[k] for k in counted if k != "ends")
    r = run_bass_kernel_spmd(nc, [{f"in_{n}": v for n, v in arrays.items()}], core_ids=[0])
    y = r.results[0]["out_0"]
    return np.ascontiguousarray(y.transpose(2, 1, 0)).reshape(1, SEQ, D)
```

```python
import math
from contextlib import ExitStack, contextmanager

import numpy as np

import concourse.bass as bass
from concourse import mybir

P = 128
D = 1024
KT = D // P
SEQ = 512
CTX = 256
ALL = SEQ + CTX
F32 = mybir.dt.float32
F32R = mybir.dt.float32r
ACT = mybir.ActivationFunctionType
ALU = mybir.AluOpType
AX = mybir.AxisListType.X

BLOCKS = 16
CHUNK = BLOCKS * P
RING = 3

RET_HEADS, NA_HEADS, XA_HEADS = 4, 8, 4
GRID_W, GRID_H, WIN = 64, 8, 32
EXPERTS, D_FF = 16, 512
HIDDEN = 2816
HT = HIDDEN // P
PART = 4
FFN_LOOPS, LAST_PART = HT // PART, HT % PART
HALF = 8
SPLITS = 3
FFN_HALVES = 3 * HT
LAYERS = 2
MLA_H, DIFF_H, GQA_H = 4, 4, 8
LAM_INIT = [0.8 - 0.6 * math.exp(-0.3 * l) for l in range(LAYERS)]
RPB_RUN = 7 * 31 + WIN + 16
DIFFS = SEQ + 3 * P
BIG = 1e30
ARENA = 25184

ADA_TILES = LAYERS * 48
ADA_STEP = ADA_TILES // (3 * KT)
MOE_FIRST = 96
GROUPS, IN_GROUP = 4, EXPERTS // 4
EXPERT_CHUNKS = 3 * D * D_FF // (P * CHUNK)
UNIT_CHUNKS = IN_GROUP * EXPERT_CHUNKS
UNITS = SEQ // P + GROUPS - 1
FFN_FIRST = [MOE_FIRST + UNITS * UNIT_CHUNKS + l * (12 + FFN_HALVES // 2) + 12 for l in range(LAYERS)]
OUT2_HALVES = KT
OUT2_FIRST = [first - OUT2_HALVES // 2 for first in FFN_FIRST]
SPLIT_HALVES = OUT2_HALVES + FFN_HALVES
SLOTS = (UNITS + 1) * P


def param_layout():
    at, out = 0, {}
    items = [("g_mix", 8), ("ret_gain", 8), ("g_mem", 8), ("g_ffn", 8), ("g_final", 8), ("decay", 8),
             ("router_bias", 80), ("c", 16), ("b_ada", 2 * ADA_TILES)]
    for l in range(LAYERS):
        items += [(f"{n}{l}", w) for n, w in (
            ("attn_pre", 8), ("attn_post", 8), ("mla_q", 2), ("mla_kv", 1), ("diff_sub", 1), ("gqa_q", 1),
            ("gqa_k", 1), ("ffn_pre", 8), ("ffn_post", 8), ("lambda", 4))]
    for n, w in items:
        out[n] = (at, w)
        at += w
    return out, at


def const_layout():
    at, out = 0, {}
    for n, w in (("ident", P), ("ones", P), ("ones64", P), ("rot128", P), ("rot64", P), ("rot32", P),
                 ("mask", 3 * 256), ("rank", 16), ("before", P), ("steps", 16), ("unit_no", 4 * UNITS),
                 ("slot_no", UNITS)):
        out[n] = (at, w)
        at += w
    return out, at


class Signal:

    def __init__(self, nc, ctx, name, known):
        self.name, self.sem = name, ctx.enter_context(nc.semaphore(name))
        self.n, self.points, self.new, self.known = 0, {}, [], known.get(name)

    def on(self, *key, also=None):
        self.n += 1
        for k in (key, also):
            if k is not None:
                assert k not in self.points, k
                self.points[k] = (self.n, 0, 1)
                self.new.append(k)
        return self.sem, 1

    def at(self, *key, i=None):
        if self.known is None:
            return self.sem, 1
        first, step, trips = self.known[key]
        if i is None:
            return self.sem, first + step * (trips - 1)
        return self.sem, i * step + first


@contextmanager
def repeated(engine, trips, signals):
    start = [s.n for s in signals]
    for s in signals:
        s.new = []
    with engine.Fori(0, trips) as i:
        yield i
    for s, n0 in zip(signals, start):
        step = s.n - n0
        for k in s.new:
            s.points[k] = (s.points[k][0], step, trips)
        s.n = n0 + step * trips


class Chunks:

    def __init__(self):
        self.block = 0


def program(nc, ins, out, known):
    PAR, n_par = param_layout()
    CON, n_con = const_layout()
    stream = ins["stream"]
    n_chunks = stream.shape[0]
    with ExitStack() as ctx:
        def sb(name, *shape):
            return ctx.enter_context(nc.sbuf_tensor(name, [P, *shape], F32))

        def sem(name):
            return ctx.enter_context(nc.semaphore(name))

        ring = sb("ring", RING, CHUNK)
        x = sb("x", KT, ALL)
        h_at = nc.sbuf_base
        h = sb("h", KT, ALL)
        work = sb("work", 12, SEQ)
        tmp, std, rstd = work[:, 0:8], work[:, 8:10], work[:, 10:12]
        par = sb("par", n_par)
        con = sb("con", n_con)
        w_router = sb("w_router", KT, 20)
        mods = sb("mods", ADA_TILES, 2)
        silu_c = sb("silu_c", KT, 2)
        cols = sb("cols", 64)
        stat = sb("stat", 8, 4)
        route = sb("route", 640)
        unit_group = ctx.enter_context(nc.sbuf_tensor("unit_group", [P, 8], mybir.dt.int32))
        arena_at = nc.sbuf_base
        arena = sb("arena", ARENA)
        h_round = nc.alloc_sbuf_tensor_at("h_round", [P, KT, ALL], F32R, offset=h_at)
        arena_round = nc.alloc_sbuf_tensor_at("arena_round", [P, ARENA], F32R, offset=arena_at)
        ps = ctx.enter_context(nc.psum_tensor("ps", [P, 8, 512], F32))

        def pc(name, j=0, w=1):
            a = PAR[name][0] + j
            return par[:, a:a + w]

        def cc(name):
            a, w = CON[name]
            return con[:, a:a + w]

        def area(offset, *dims):
            n = int(np.prod(dims))
            assert offset + n <= ARENA, (offset, dims)
            v = arena[:, offset:offset + n]
            if len(dims) == 2:
                v = v.rearrange("p (a b) -> p a b", a=dims[0])
            if len(dims) == 3:
                v = v.rearrange("p (a b c) -> p a b c", a=dims[0], b=dims[1])
            return v

        def spread(ap, *dims):
            return bass.AP(tensor=ap.tensor, offset=ap.offset, ap=[list(ap.ap[0])] + [list(d) for d in dims])

        ident, ones, ones64 = cc("ident"), cc("ones"), cc("ones64")
        mixed_sum = area(0, 8, SEQ)
        ret_q, ret_k = area(4096, 4, SEQ), area(6144, 4, SEQ)
        ret_v = area(8192, 4, 1024)
        ret_y = area(12288, 8, SEQ)
        ret_s = area(16384, 4, SEQ)
        dist = area(18432, 2, DIFFS)
        ret_e = area(20224, 2, DIFFS)
        ret_t = work[:, 0:2, :].rearrange("p a b -> p (a b)")[:, 0:DIFFS]
        trig128 = area(22016, 2, SEQ)
        rpb = area(23040, NA_HEADS, RPB_RUN)
        na_q, na_k, na_v = area(4096, 4, SEQ), area(6144, 4, SEQ), area(8192, 4, SEQ)
        na_win = area(10240, 8, SEQ)
        na_o = area(14336, 4, SEQ)
        b1_p = area(16384, 3, 256)
        b1_pt = area(17152, 2, 2, SEQ)
        near_mask = area(19200, 4, 256)
        xa_q, xa_k, xa_v, xa_o = area(4096, 4, SEQ), area(6144, 4, CTX), area(7168, 2, SEQ), area(8192, 4, SEQ)
        h_tok = area(0, 4, D)
        pick = area(4096, 4, SLOTS)
        unit_y = area(8192, UNITS * D)
        unit_h = area(15360, KT, P)
        hid = area(16384, 2, D_FF)
        hid_t = area(17408, 2, 4, P)
        put = area(18432, UNITS, SEQ)
        slot_row = area(22528, SLOTS)
        mla_q, mla_k = area(0, 4, ALL), area(3072, 4, ALL)
        diff_q, diff_k = area(6144, 2, ALL), area(7680, 2, ALL)
        gqa_q, gqa_k = area(9216, 4, ALL), area(12288, ALL)
        val = area(13056, 6, 640)
        prob = work[:, :, :].rearrange("p a b -> p (a b)")[:, 3072:3072 + 3 * ALL].rearrange("p (a b) -> p a b", a=3)
        prob_t = area(16896, 2, 6, SEQ)
        inverse = work[:, :, :].rearrange("p a b -> p (a b)")[:, 5376:5376 + 3 * P].rearrange("p (a b) -> p a b", a=3)
        q_low, kv_low, k_pe = area(16896, 2, ALL), area(18432, ALL), area(19200, ALL)
        w_small = area(19968, 2 * 384 + 512)
        trig = area(23040, 4, SEQ)
        out_1 = tmp[:, 0:3, :].rearrange("p a b -> p (a b)").rearrange("p (a b) -> p a b", a=2)
        out_2 = tmp[:, 3:6, :].rearrange("p a b -> p (a b)").rearrange("p (a b) -> p a b", a=2)
        attn_y = area(0, KT, ALL)
        def pair(offset, *dims):
            n = int(np.prod(dims))
            return (area(offset, *dims),
                    arena_round[:, offset:offset + n].rearrange("p (a b) -> p a b", a=dims[0]) if len(dims) == 2
                    else arena_round[:, offset:offset + n])

        h_rest, h_low = pair(0, KT, ALL)
        _, hid_high = pair(6144, PART, ALL)
        hid_rest, hid_low = pair(6144 + PART * ALL, PART, ALL)
        _, heads_high = pair(6144, KT, ALL)
        _, w_high = pair(12288, SPLITS, HALF * P)
        _, w_low = pair(12288 + SPLITS * HALF * P, SPLITS, HALF * P)
        ffn_y = area(18432, KT, ALL)

        R, at = {"rank": cc("rank").rearrange("p (t n) -> p t n", t=4)}, 64
        for name, w in (("lg", 20), ("gd", 4), ("eq", 4), ("cand", 4), ("g1", 4), ("ge", 4), ("ig", 4), ("ed", 4),
                        ("ee", 4), ("e2", 4), ("o1", 4), ("o2", 4), ("rk", 4), ("cmp", 4)):
            R[name] = route[:, at:at + 4 * w].rearrange("p (t n) -> p t n", t=4)
            at += 4 * w
        for name, w in (("gm", 4), ("best", 4), ("gw", 4), ("em", 4), ("n", 4), ("units", 4), ("slot", 4), ("from", 8),
                        ("over", 4 * UNITS), ("ug", UNITS), ("w", 4 * UNITS)):
            R[name] = route[:, at:at + w]
            at += w
        R["sel"] = route[:, at:at + 64].rearrange("p (t g e) -> p t g e", t=4, g=4)

        signals = {}

        def signal(engine, name):
            s = Signal(nc, ctx, name, known)
            signals.setdefault(engine, []).append(s)
            return s

        loaded = [sem(f"chunk_loaded{r}") for r in range(RING)]
        inputs_loaded = sem("inputs_loaded")
        context_loaded = sem("context_loaded")
        slots_loaded = sem("slots_loaded")
        late_loaded = sem("late_loaded")
        stored = sem("stored")
        streamed, summed, scored = signal("pe", "streamed"), signal("pe", "summed"), signal("pe", "scored")
        turned, attended, multiplied = signal("pe", "turned"), signal("pe", "attended"), signal("pe", "multiplied")
        squared, rooted, exped = signal("act", "squared"), signal("act", "rooted"), signal("act", "exped")
        act_moved, gated = signal("act", "act_moved"), signal("act", "gated")
        high_split, low_split = sem("high_split"), sem("low_split")
        cleared = sem("cleared")
        near_masked = sem("near_masked")
        cosines = sem("cosines")
        normed, inverted, maxed = signal("dve", "normed"), signal("dve", "inverted"), signal("dve", "maxed")
        dve_moved, fused, scaled = signal("dve", "dve_moved"), signal("dve", "fused"), signal("dve", "scaled")
        small, roped = signal("dve", "small"), signal("dve", "roped")
        ends = {}
        known_ends = known.get("ends")
        seen = {}

        def stage(name, e, wait=True):
            before = seen.setdefault(name, [0, {}])
            n = before[0]
            before[0] += 1
            ends[(name, n)] = [s.n for s in signals[name]]
            if known_ends is None or not wait:
                return
            for other in ("pe", "act", "dve"):
                for s, value in zip(signals[other], known_ends[(other, n)]):
                    if value > before[1].get(s.name, 0):
                        e.wait_ge(s.sem, value)
                        before[1][s.name] = value

        block = ctx.enter_context(nc.Block())

        @block.sync
        def _(sp):
            for dst, src in ((x[:, :, 0:SEQ], ins["xT"]), (x[:, :, SEQ:ALL], ins["memT"]), (par[:], ins["par"]),
                             (con[:], ins["con"]), (trig128, ins["trig128"]), (dist, ins["dist"]),
                             (rpb, ins["rpb"]), (w_router[:], ins["w_router"])):
                sp.dma_start(dst, src).then_inc(inputs_loaded, 16)

            def load(n, source, i=None):
                sp.dma_start(ring[:, n % RING], source).then_inc(loaded[n % RING], 16)

            for n in range(MOE_FIRST):
                if n >= RING:
                    sp.wait_ge(*streamed.at("chunk", n - RING))
                load(n, stream[n])

            def unit_chunk(group, j):
                return stream[group * UNIT_CHUNKS + (MOE_FIRST + j)]

            sp.wait_ge(*small.at("unit groups"))
            group = sp.value_load(unit_group[0:1, 0:1], min_val=0, max_val=GROUPS - 1)
            for j in range(UNIT_CHUNKS):
                n = MOE_FIRST + j
                sp.wait_ge(*(streamed.at("chunk", n - RING, i=0) if j >= RING else streamed.at("chunk", n - RING)))
                load(n, unit_chunk(group, j))
            with sp.Fori(1, UNITS) as i:
                group = sp.value_load(unit_group[0:1, bass.ds(i, 1)], min_val=0, max_val=GROUPS - 1)
                for j in range(UNIT_CHUNKS):
                    n = MOE_FIRST + j
                    if j >= RING:
                        sp.wait_ge(*streamed.at("chunk", n - RING, i=i))
                    else:
                        sp.wait_ge(*streamed.at("chunk", n + UNIT_CHUNKS - RING, i=i - 1))
                    load(n, unit_chunk(group, j))
            after = MOE_FIRST + UNITS * UNIT_CHUNKS
            for n in range(after, n_chunks + (UNITS - GROUPS) * UNIT_CHUNKS):
                last = n - RING
                layer = [l for l in range(LAYERS) if OUT2_FIRST[l] <= last < FFN_FIRST[l] + FFN_HALVES // 2]
                if layer:
                    sp.wait_ge(low_split, SPLIT_HALVES * layer[0] + 2 * (last - OUT2_FIRST[layer[0]]) + 2)
                elif last < after:
                    sp.wait_ge(*streamed.at("chunk", last - (UNITS - 1) * UNIT_CHUNKS))
                else:
                    sp.wait_ge(*streamed.at("chunk", last))
                load(n, stream[n - (UNITS - GROUPS) * UNIT_CHUNKS])
            sp.wait_ge(*normed.at("final"))
            sp.dma_start(out, x[:, :, 0:SEQ]).then_inc(stored, 16)
            sp.wait_ge(stored, 16)

        SEQ_ONLY = [(0, SEQ)]
        BOTH = [(0, SEQ), (SEQ, CTX)]

        def norm_jobs(src, nk, pieces, mean_of, n, write, parts=P):
            return [dict(src=[src(k, c0, cn) for k in range(nk)], ones=mean_of, inv=1.0 / n, write=write,
                         piece=(c0, cn), parts=parts) for c0, cn in pieces]

        def slots(jobs):
            at, user, out_ = 0, {}, []
            for j, job in enumerate(jobs):
                own = []
                for k in range(len(job["src"])):
                    s = job.get("slots", range(8))[at % len(job.get("slots", range(8)))]
                    own.append((s, user.get(s)))
                    user[s] = j
                    at += 1
                out_.append(own)
            return out_

        def sums(pe, tag, jobs, j, bank=0):
            job = jobs[j]
            cn, parts = job["piece"][1], job["parts"]
            if j >= 2:
                pe.wait_ge(*rooted.at(tag, j - 2))
            for k, (s, _) in enumerate(slots(jobs)[j]):
                pe.wait_ge(*squared.at(tag, j, k))
                mm = pe.matmul(ps[0:parts, bank + j % 2, 0:cn], job["ones"][0:parts, 0:parts],
                               tmp[0:parts, s, 0:cn], start=(k == 0), stop=(k == len(job["src"]) - 1))
            mm.then_inc(*summed.on(tag, j))

        def norm_pe(pe, tag, jobs):
            for j in range(len(jobs)):
                sums(pe, tag, jobs, j)

        def x_ready(tag):
            return lambda j, k: normed.at(tag, j, "end" if k == KT - 1 else f"added{k}") if j < len(job_of[tag]) else None

        def moved_ready(tag, pieces):
            return lambda j, k: moved_at(tag, k * pieces + j)

        def squares(act, tag, jobs, j, ready=None):
            job = jobs[j]
            cn, parts = job["piece"][1], job["parts"]
            for k, (s, user) in enumerate(slots(jobs)[j]):
                if user is not None:
                    act.wait_ge(*summed.at(tag, user))
                if ready and ready(j, k):
                    act.wait_ge(*ready(j, k))
                nc.scalar.activation(tmp[0:parts, s, 0:cn], job["src"][k], ACT.Square).then_inc(*squared.on(tag, j, k))

        def roots(act, tag, jobs, j, bank=0):
            job = jobs[j]
            cn, parts = job["piece"][1], job["parts"]
            act.wait_ge(*summed.at(tag, j))
            if j >= 2:
                act.wait_ge(*inverted.at(tag, j - 2))
            nc.scalar.activation(std[0:parts, j % 2, 0:cn], ps[0:parts, bank + j % 2, 0:cn], ACT.Sqrt,
                                 bias=cols[0:parts, job.get("eps", 0):job.get("eps", 0) + 1],
                                 scale=job["inv"]).then_inc(*rooted.on(tag, j))

        def norm_act(act, tag, jobs, ready=None):
            for j in range(len(jobs) + 1):
                if j < len(jobs):
                    squares(act, tag, jobs, j, ready)
                if j >= 1:
                    roots(act, tag, jobs, j - 1)

        def scale_rows(dve, tag, jobs, j):
            job = jobs[j]
            cn, parts = job["piece"][1], job["parts"]
            dve.wait_ge(*rooted.at(tag, j))
            if j >= 2:
                dve.wait_ge(*normed.at(tag, j - 2, "end"))
            r = rstd[0:parts, j % 2, 0:cn]
            nc.vector.reciprocal(r, std[0:parts, j % 2, 0:cn]).then_inc(*inverted.on(tag, j))
            dve.wait_ge(*inverted.at(tag, j))
            job["write"](dve, tag, j, job["piece"], r)

        def norm_dve(dve, tag, jobs):
            for j in range(len(jobs)):
                scale_rows(dve, tag, jobs, j)

        def write_scaled(dst, gain, final=None):
            def write(dve, tag, j, piece, r):
                c0, cn = piece
                job = job_of[tag][j]
                nk = len(job["src"])
                for k in range(nk):
                    key = (tag, j, "end") if k == nk - 1 else (tag, j, k)
                    nc.vector.scalar_tensor_tensor(out=dst(k, c0, cn), in0=job["src"][k], scalar=gain(k, c0), in1=r,
                                                   op0=ALU.mult, op1=ALU.mult)\
                        .then_inc(*normed.on(*key, also=(final,) if final and k == nk - 1 else None))
            return write

        def write_residual(gain):
            def write(dve, tag, j, piece, r):
                c0, cn = piece
                job = job_of[tag][j]
                for k in range(KT):
                    nc.vector.scalar_tensor_tensor(out=job["src"][k], in0=job["src"][k], scalar=gain(k, c0), in1=r,
                                                   op0=ALU.mult, op1=ALU.mult).then_inc(*normed.on(tag, j, k))
                for k in range(KT):
                    dve.wait_ge(*normed.at(tag, j, k))
                    nc.vector.tensor_tensor(x[:, k, c0:c0 + cn], x[:, k, c0:c0 + cn], job["src"][k], ALU.add)\
                        .then_inc(*normed.on(tag, j, "end" if k == KT - 1 else f"added{k}"))
            return write

        job_of = {}

        def xs(k, c0, cn):
            return x[:, k, c0:c0 + cn]

        def hs(k, c0, cn):
            return h[:, k, c0:c0 + cn]

        job_of["norm_x"] = norm_jobs(xs, KT, SEQ_ONLY, ones, D, write_scaled(hs, lambda k, c0: pc("g_mix", k)))
        job_of["norm_x"] += norm_jobs(xs, KT, [(SEQ, CTX)], ones, D,
                                      write_scaled(hs, lambda k, c0: pc("g_mem", k), final="norm_mem done"))
        job_of["norm_moe"] = norm_jobs(xs, KT, SEQ_ONLY, ones, D, write_scaled(hs, lambda k, c0: pc("g_ffn", k)))
        job_of["norm_first"] = norm_jobs(xs, KT, SEQ_ONLY, ones, D, write_scaled(xs, lambda k, c0: pc("g_final", k)))
        job_of["ret_norm"] = [dict(src=[ret_y[:, 2 * hd + e, :] for e in range(2)], ones=ones, inv=1.0 / 256, eps=1,
                                   piece=(0, SEQ), parts=P,
                                   write=write_scaled(lambda k, c0, cn, hd=hd: ret_y[:, 2 * hd + k, :],
                                                      lambda k, c0, hd=hd: pc("ret_gain", 2 * hd + k)))
                              for hd in range(RET_HEADS)]

        def scal(kind, k, c0):
            a = 8 + (kind * 2 + (1 if c0 >= SEQ else 0)) * 8 + k
            return cols[:, a:a + 1]

        def mod(l, which, k, c0):
            return mods[:, l * 48 + which * 8 + k, (1 if c0 >= SEQ else 0):(2 if c0 >= SEQ else 1)]

        for l in range(LAYERS):
            own = BOTH if l < LAYERS - 1 else SEQ_ONLY
            job_of["attn_pre", l] = norm_jobs(xs, KT, BOTH, ones, D, write_scaled(
                hs, lambda k, c0: scal(0, k, c0)))
            job_of["attn_post", l] = norm_jobs(lambda k, c0, cn: attn_y[:, k, c0:c0 + cn], KT, own, ones, D,
                                               write_residual(lambda k, c0: scal(1, k, c0)))
            job_of["ffn_pre", l] = norm_jobs(xs, KT, own, ones, D, write_scaled(
                lambda k, c0, cn: h_rest[:, k, c0:c0 + cn], lambda k, c0: scal(0, k, c0)))
            job_of["ffn_post", l] = norm_jobs(lambda k, c0, cn: ffn_y[:, k, c0:c0 + cn], KT, own, ones, D,
                                              write_residual(lambda k, c0: scal(1, k, c0)))

            def low(k, c0, cn):
                return q_low[:, k, c0:c0 + cn]

            def kv(k, c0, cn):
                return kv_low[:, c0:c0 + cn]
            jobs = norm_jobs(kv, 1, BOTH, ones, 128, write_scaled(kv, lambda k, c0, l=l: pc(f"mla_kv{l}")))
            jobs += norm_jobs(low, 2, own, ones, 256, write_scaled(low, lambda k, c0, l=l: pc(f"mla_q{l}", k)))
            for t in range(4):
                def gq(k, c0, cn, t=t):
                    return gqa_q[:, t, c0:c0 + cn]
                jobs += norm_jobs(gq, 1, own, ones64, 64, write_scaled(gq, lambda k, c0, l=l: pc(f"gqa_q{l}")))

            def gk(k, c0, cn):
                return gqa_k[:, c0:c0 + cn]
            jobs += norm_jobs(gk, 1, BOTH, ones64, 64, write_scaled(gk, lambda k, c0, l=l: pc(f"gqa_k{l}")))
            job_of["low", l] = jobs
            jobs = []
            for t in range(2):
                def dd(k, c0, cn, t=t):
                    return out_1[:, t, c0:c0 + cn]
                jobs += norm_jobs(dd, 1, own, ones64, 64, write_scaled(
                    lambda k, c0, cn, t=t: h[:, 2 + t, c0:c0 + cn], lambda k, c0: cols[:, 6:7]))
            for job in jobs:
                job["slots"] = (6, 7)
            job_of["diff", l] = jobs

        chunks = Chunks()

        def take(pe, i=None, first=0, count=1):
            b = chunks.block
            n, o = b // BLOCKS, b % BLOCKS
            if o == 0:
                if i is None:
                    pe.wait_ge(loaded[n % RING], 16 * (n // RING + 1))
                else:
                    pe.wait_ge(loaded[n % RING], i * (16 * UNIT_CHUNKS // RING) + 16 * (n // RING + 1))
            chunks.block += count
            return ring[:, n % RING, o * P:(o + count) * P]

        def chunk_end():
            return ("chunk", chunks.block // BLOCKS - 1) if chunks.block % BLOCKS == 0 else None

        def group(pe, key, banks, rhs, K, pieces, out_cols=None, i=None):
            for k in range(K):
                w = take(pe, i)
                for pi, (c0, cn) in enumerate(pieces):
                    mm = pe.matmul(ps[:, banks[pi], 0:cn], w, rhs(k, c0, cn), start=(k == 0), stop=(k == K - 1))
                    last = pi == len(pieces) - 1
                    also = chunk_end() if last else None
                    if k == K - 1:
                        mm.then_inc(*streamed.on(*key, pi, also=also))
                    elif also:
                        mm.then_inc(*streamed.on(*also))

        def after_norm(pe, tag, shifted=False):
            for j in range(max(0, len(job_of[tag]) - 2), len(job_of[tag])):
                pe.wait_ge(*rooted.at(tag, j))

            def ready(k, pi):
                if shifted:
                    pe.wait_ge(*act_moved.at("shifted", tag, pi, k))
                else:
                    pe.wait_ge(*normed.at(tag, pi, "end" if k == KT - 1 else k))
            return ready

        def first_chunk(pe, keys, banks, rhs, pieces, ready):
            w = [[take(pe) for _ in range(KT)] for _ in keys]
            for pi, (c0, cn) in enumerate(pieces):
                for t, key in enumerate(keys):
                    for k in range(KT):
                        if t == 0:
                            ready(k, pi)
                        mm = pe.matmul(ps[:, banks[t][pi], 0:cn], w[t][k], rhs(k, c0, cn), start=(k == 0),
                                       stop=(k == KT - 1))
                    last = pi == len(pieces) - 1 and t == len(keys) - 1
                    mm.then_inc(*streamed.on(*key, pi, also=chunk_end() if last else None))

        def tiles(ms, pieces_of):
            g = 0
            for m in range(ms):
                for pi, (c0, cn) in enumerate(pieces_of(m)):
                    yield g, m, pi, c0, cn
                    g += 1

        def moved_at(tag, g):
            return (act_moved if g % 2 == 0 else dve_moved).at(tag, g)

        def project_pe(pe, tag, ms, K, rhs, pieces_of, ready=None):
            g = 0
            for m in range(ms):
                pieces = pieces_of(m)
                if ready and m < 2:
                    if m == 0:
                        n = len(pieces)
                        first_chunk(pe, [(tag, 0), (tag, 1)], [list(range(n)), list(range(n, 2 * n))], rhs, pieces, ready)
                    g += len(pieces)
                    continue
                for pi in range(len(pieces)):
                    if g + pi >= 8:
                        pe.wait_ge(*moved_at(tag, g + pi - 8))
                group(pe, (tag, m), [(g + pi) % 8 for pi in range(len(pieces))], rhs, K, pieces)
                g += len(pieces)

        def project_move(engine, which, tag, ms, pieces_of, dst):
            for g, m, pi, c0, cn in tiles(ms, pieces_of):
                if g % 2 != which:
                    continue
                engine.wait_ge(*streamed.at(tag, m, pi))
                d, s = dst(m, c0, cn, ps[:, g % 8, 0:cn])
                if which == 0:
                    nc.scalar.activation(d, s, ACT.Copy).then_inc(*act_moved.on(tag, g))
                else:
                    nc.vector.tensor_copy(d, s).then_inc(*dve_moved.on(tag, g))

        def values_pe(pe, tag, token_tiles, lhs, nb, g0=0):
            start = chunks.block
            taken = [take(pe, count=nb) for _ in range(KT)]
            for t in range(token_tiles):
                if g0 + t >= 8:
                    pe.wait_ge(*moved_at(tag, g0 + t - 8))
                for k in range(KT):
                    mm = pe.matmul(ps[:, (g0 + t) % 8, 0:nb * P], lhs(k, t), taken[k],
                                   start=(k == 0), stop=(k == KT - 1))
                    used = start + (k + 1) * nb
                    if t == token_tiles - 1 and k < KT - 1 and used % BLOCKS == 0:
                        mm.then_inc(*streamed.on("chunk", used // BLOCKS - 1))
                mm.then_inc(*streamed.on(tag, g0 + t, also=chunk_end() if t == token_tiles - 1 else None))

        def values_move(engine, which, tag, token_tiles, dst, width, g0=0):
            for t in range(token_tiles):
                if (g0 + t) % 2 != which:
                    continue
                engine.wait_ge(*streamed.at(tag, g0 + t))
                s = ps[:, (g0 + t) % 8, 0:width]
                if which == 0:
                    nc.scalar.activation(dst(t), s, ACT.Copy).then_inc(*act_moved.on(tag, g0 + t))
                else:
                    nc.vector.tensor_copy(dst(t), s).then_inc(*dve_moved.on(tag, g0 + t))

        def branch_pe(pe, tag, K, rhs):
            for m in range(KT):
                for b, (what, kk, r) in enumerate((("gate", KT, hs), ("y", K, rhs))):
                    if m >= 3:
                        pe.wait_ge(*(gated.at(tag, m - 3) if b == 0 else fused.at(tag, m - 3, "y")))
                    for half in range(2):
                        for k in range(half * kk // 2, (half + 1) * kk // 2):
                            w = take(pe)
                            mm = pe.matmul(ps[:, (2 * m + b) % 6, :], w, r(k, 0, SEQ), start=(k == 0), stop=(k == kk - 1))
                            if k == kk - 1:
                                mm.then_inc(*streamed.on(tag, what, m, 0, also=chunk_end()))
                            elif chunk_end():
                                mm.then_inc(*streamed.on(*chunk_end()))
                        a = 2 * b + half
                        if a == 0 and m >= 2:
                            pe.wait_ge(*dve_moved.at(tag, "ada", m - 2))
                        for k in range(KT):
                            w = take(pe)
                            mm = pe.matmul(ps[:, 6 + m % 2, 2 * a:2 * a + 2], w, silu_c[:, k, :],
                                           start=(k == 0), stop=(k == KT - 1))
                            if a == ADA_STEP - 1 and k == KT - 1:
                                mm.then_inc(*streamed.on(tag, "ada", m, also=chunk_end()))
                            elif chunk_end():
                                mm.then_inc(*streamed.on(*chunk_end()))

        def branch_act(act, tag):
            for m in range(KT):
                act.wait_ge(*streamed.at(tag, "gate", m, 0))
                if m >= 2:
                    act.wait_ge(*fused.at(tag, m - 2, "y"))
                nc.scalar.activation(tmp[:, m % 2, :], ps[:, (2 * m) % 6, :], ACT.Sigmoid).then_inc(*gated.on(tag, m))

        def branch_dve(dve, tag, number):
            for m in range(KT):
                dve.wait_ge(*gated.at(tag, m))
                dve.wait_ge(*streamed.at(tag, "y", m, 0))
                y = ps[:, (2 * m + 1) % 6, :]
                if number == 0:
                    nc.vector.tensor_tensor(mixed_sum[:, m, :], tmp[:, m % 2, :], y, ALU.mult)\
                        .then_inc(*fused.on(tag, m, "y"))
                else:
                    if m >= 2:
                        dve.wait_ge(*fused.at(tag, m - 2, "sum"))
                    nc.vector.tensor_tensor(tmp[:, 2 + m % 2, :], tmp[:, m % 2, :], y, ALU.mult)\
                        .then_inc(*fused.on(tag, m, "y"))
                    dve.wait_ge(*fused.at(tag, m, "y"))
                    nc.vector.tensor_tensor(mixed_sum[:, m, :], mixed_sum[:, m, :], tmp[:, 2 + m % 2, :], ALU.add)\
                        .then_inc(*fused.on(tag, m, "sum"))
                dve.wait_ge(*streamed.at(tag, "ada", m))
                n, a = 2 * ADA_STEP, (number * KT + m) * 2 * ADA_STEP
                nc.vector.tensor_tensor(mods[:].rearrange("p a b -> p (a b)")[:, a:a + n], ps[:, 6 + m % 2, 0:n],
                                        pc("b_ada", a, n), ALU.add).then_inc(*dve_moved.on(tag, "ada", m))

        class Attention:
            def __init__(self, tag, heads, per_head, keys, scale, score, mix, dest, p, pt, bias=None):
                self.tag, self.heads, self.per_head, self.keys, self.scale = tag, heads, per_head, keys, scale
                self.score, self.mix, self.dest, self.p, self.pt, self.bias = score, mix, dest, p, pt, bias
                self.units, self.kt = heads * per_head, keys // P

            def s(self, u):
                return ps[:, 2 * (u % 2):2 * (u % 2) + 2, :].rearrange("p a b -> p (a b)")[:, 0:self.keys]

            def copies(self, u):
                return [act_moved.at(self.tag, "pt", u)] + ([dve_moved.at(self.tag, "pt", u)] if self.kt > 4 else [])

        def attend_pe(pe, a):
            tag = a.tag
            for step in range(a.units + 3):
                u = step
                if u < a.units:
                    if u >= 2:
                        pe.wait_ge(*(fused.at(tag, "biased", u - 2) if a.bias else exped.at(tag, u - 2)))
                    for k0 in range(0, a.keys, 512):
                        kn = min(512, a.keys - k0)
                        lhs, rhs = a.score(u, k0, kn)
                        mm = pe.matmul(ps[:, 2 * (u % 2) + k0 // 512, 0:kn], lhs, rhs, start=True, stop=True)
                    mm.then_inc(*scored.on(tag, u))
                u = step - 2
                if 0 <= u < a.units:
                    pe.wait_ge(*scaled.at(tag, u))
                    if u >= 1:
                        for w in a.copies(u - 1):
                            pe.wait_ge(*w)
                    for t in range(a.kt):
                        mm = pe.matmul(ps[:, 4 + t // 4, (t % 4) * P:(t % 4 + 1) * P],
                                       a.p[:, u % 3, t * P:(t + 1) * P], inverse[:, u % 3, :], start=True, stop=True)
                        if t == min(3, a.kt - 1):
                            mm.then_inc(*turned.on(tag, u, 0))
                        elif t == a.kt - 1:
                            mm.then_inc(*turned.on(tag, u, 1))
                u = step - 3
                if u >= 0 and u % a.per_head == a.per_head - 1:
                    hd = u // a.per_head
                    for w in a.copies(u):
                        pe.wait_ge(*w)
                    if hd >= 2:
                        pe.wait_ge(*dve_moved.at(tag, "out", hd - 2))
                    products = a.mix(hd)
                    for o, lhs, rhs, start, stop in products:
                        mm = pe.matmul(o, lhs, rhs, start=start, stop=stop)
                    mm.then_inc(*attended.on(tag, hd))

        def attend_act(act, a):
            tag = a.tag
            for step in range(a.units + 2):
                u = step - 2
                if u >= 0:
                    act.wait_ge(*turned.at(tag, u, 0))
                    hd, q = u // a.per_head, u % a.per_head
                    if hd >= 2 and q == 0:
                        act.wait_ge(*attended.at(tag, hd - 2))
                    n = min(4, a.kt)
                    nc.scalar.activation(a.pt[:, hd % 2, 0:n, q * P:(q + 1) * P],
                                         ps[:, 4, 0:n * P].rearrange("p (t q) -> p t q", t=n), ACT.Copy)\
                        .then_inc(*act_moved.on(tag, "pt", u))
                u = step
                if u < a.units:
                    act.wait_ge(*maxed.at(tag, "negated", u))
                    if u >= 3:
                        act.wait_ge(*turned.at(tag, u - 3, 1 if a.kt > 4 else 0))
                    nc.scalar.activation(a.p[:, u % 3, 0:a.keys], a.p[:, u % 3, 0:a.keys] if a.bias else a.s(u),
                                         ACT.Exp, bias=stat[:, u % 8, 1:2], scale=1.0 if a.bias else a.scale(u),
                                         accum_out=stat[:, u % 8, 2:3]).then_inc(*exped.on(tag, u))

        def attend_dve(dve, a):
            tag = a.tag
            for step in range(a.units + 3):
                u = step
                if u < a.units:
                    s, st = a.s(u), stat[:, u % 8]
                    dve.wait_ge(*scored.at(tag, u))
                    if a.bias:
                        if u >= 3:
                            dve.wait_ge(*turned.at(tag, u - 3, 0))
                        buf = a.p[:, u % 3, 0:a.keys]
                        dve.wait_ge(near_masked, u + 1)
                        nc.vector.scalar_tensor_tensor(out=buf, in0=s, scalar=a.scale(u), in1=near_mask[:, u % 4, :],
                                                       op0=ALU.mult, op1=ALU.add)\
                            .then_inc(*fused.on(tag, "biased", u))
                        dve.wait_ge(*fused.at(tag, "biased", u))
                        s = buf
                    if u >= 8:
                        dve.wait_ge(*scaled.at(tag, u - 8))
                    nc.vector.reduce_max(st[:, 0:1], s, AX).then_inc(*maxed.on(tag, "max", u))
                    dve.wait_ge(*maxed.at(tag, "max", u))
                    nc.vector.tensor_scalar(st[:, 1:2], st[:, 0:1], -1.0 if a.bias else -a.scale(u), None, ALU.mult)\
                        .then_inc(*maxed.on(tag, "negated", u))
                u = step - 1
                if 0 <= u < a.units:
                    st = stat[:, u % 8]
                    dve.wait_ge(*exped.at(tag, u))
                    nc.vector.reciprocal(st[:, 3:4], st[:, 2:3]).then_inc(*inverted.on(tag, u))
                    dve.wait_ge(*inverted.at(tag, u))
                    if u >= 3:
                        dve.wait_ge(*turned.at(tag, u - 3, 1 if a.kt > 4 else 0))
                    nc.vector.tensor_scalar(inverse[:, u % 3, :], ident, st[:, 3:4], None,
                                            ALU.mult).then_inc(*scaled.on(tag, u))
                u = step - 2
                if 0 <= u < a.units and a.kt > 4:
                    dve.wait_ge(*turned.at(tag, u, 1))
                    hd, q = u // a.per_head, u % a.per_head
                    if hd >= 2 and q == 0:
                        dve.wait_ge(*attended.at(tag, hd - 2))
                    nc.vector.tensor_copy(a.pt[:, hd % 2, 4:6, q * P:(q + 1) * P],
                                          ps[:, 5, 0:2 * P].rearrange("p (t q) -> p t q", t=2))\
                        .then_inc(*dve_moved.on(tag, "pt", u))
                u = step - 3
                if u >= 0 and u % a.per_head == a.per_head - 1:
                    hd = u // a.per_head
                    dve.wait_ge(*attended.at(tag, hd))
                    d, s = a.dest(hd)
                    nc.vector.tensor_copy(d, s).then_inc(*dve_moved.on(tag, "out", hd))

        WIN_AT = [min(max(16 * t - 8, 0), GRID_W - WIN) for t in range(4)]

        def na_score(u, k0, kn):
            hd, t = u // 4, u % 4
            q0 = (hd % 2) * 64
            k0 = WIN_AT[t] * GRID_H
            return na_q[q0:q0 + 64, hd // 2, t * P:(t + 1) * P], na_k[q0:q0 + 64, hd // 2, k0:k0 + 256]

        def na_bias(u):
            hd, t = u // 4, u % 4
            shift = WIN_AT[t] - 16 * t + 15 + 1
            run = rpb[:, hd, shift:shift + 1]
            near = spread(run, (1, WIN), (31, GRID_H))
            kind = {0: 0, 1: 1, 2: 1, 3: 2}[t]
            return near, cc("mask")[:, kind * 256:(kind + 1) * 256]

        def na_mix(hd):
            q0 = (hd % 2) * 64
            return [(ps[q0:q0 + 64, 6 + hd % 2, t * P:(t + 1) * P], na_win[:, 2 * t + kt, hd * 64:(hd + 1) * 64],
                     b1_pt[:, hd % 2, kt, t * P:(t + 1) * P], kt == 0, kt == 1) for t in range(4) for kt in range(2)]

        def na_dest(hd):
            q0 = (hd % 2) * 64
            return (na_o[q0:q0 + 64, hd // 2, :].rearrange("p (r w) -> p r w", w=GRID_W),
                    ps[q0:q0 + 64, 6 + hd % 2, :].rearrange("p (w r) -> p r w", r=GRID_H))

        near_attention = Attention("na", NA_HEADS, 4, 256, lambda u: 64 ** -0.5, na_score, na_mix, na_dest, b1_p, b1_pt, na_bias)
        memory_attention = Attention(
            "xa", XA_HEADS, 4, 256, lambda u: 128 ** -0.5,
            lambda u, k0, kn: (xa_q[:, u // 4, (u % 4) * P:(u % 4 + 1) * P], xa_k[:, u // 4, :]),
            lambda hd: [(ps[:, 6 + hd % 2, :], xa_v[:, kt, hd * P:(hd + 1) * P], b1_pt[:, hd % 2, kt, :], kt == 0, kt == 1)
                        for kt in range(2)],
            lambda hd: (xa_o[:, hd, :], ps[:, 6 + hd % 2, :]), b1_p, b1_pt)

        def head_parts(kind, hd):
            if kind == "mla":
                return mla_q[0:96, hd, :], mla_k[0:96, hd, :], hd * 64, (h, hd // 2, hd % 2)
            if kind == "diff":
                a = (hd % 4) * 32
                return (diff_q[a:a + 32, hd // 4, :], diff_k[a:a + 32, hd // 4, :], 256 + (hd // 2) * 64,
                        ((out_1, out_2)[hd % 2], hd // 4, (hd // 2) % 2))
            a = (hd // 4) * 64
            return gqa_q[a:a + 64, hd % 4, :], gqa_k[a:a + 64, :], 512 + (hd // 4) * 64, (h, 4 + hd // 2, hd % 2)

        KINDS = [("mla", hd, 96 ** -0.5) for hd in range(MLA_H)] + [("gqa", hd, 64 ** -0.5) for hd in range(GQA_H)] + \
                [("diff", hd, 32 ** -0.5) for hd in range(2 * DIFF_H)]

        def block2_attention(l, on_context):
            q0, per_head = (SEQ, 2) if on_context else (0, 4)
            key0, keys = (SEQ, CTX) if on_context else (0, ALL)
            width = per_head * P

            def score(u, k0, kn):
                kind, hd, _ = KINDS[u // per_head]
                q, k, _, _ = head_parts(kind, hd)
                a = q0 + (u % per_head) * P
                return q[:, a:a + P], k[:, key0 + k0:key0 + k0 + kn]

            def mix(n):
                _, _, v0, (_, _, half) = head_parts(*KINDS[n][:2])
                o = ps[half * 64:half * 64 + 64, 6 + n % 2, 0:width]
                last = keys // P - 1
                return [(o, val[:, key0 // P + t, v0:v0 + 64], prob_t[:, n % 2, t, 0:width], t == 0, t == last)
                        for t in range(last + 1)]

            def dest(n):
                _, _, _, (buf, tile, half) = head_parts(*KINDS[n][:2])
                a = half * 64
                return buf[a:a + 64, tile, q0:q0 + width], ps[a:a + 64, 6 + n % 2, 0:width]
            return Attention(("heads", l, on_context), len(KINDS), per_head, keys, lambda u: KINDS[u // per_head][2],
                             score, mix, dest, prob, prob_t)

        attentions = {l: [block2_attention(l, c) for c in ([False, True] if l < LAYERS - 1 else [False])]
                      for l in range(LAYERS)}

        rope1 = [(ret_q[:, t, :], 0, P, "rot128", trig128[:, 0, :], trig128[:, 1, :]) for t in range(4)]
        rope1 += [(ret_k[:, t, :], 0, P, "rot128", trig128[:, 0, :], trig128[:, 1, :]) for t in range(4)]

        def full(kind, buf):
            return buf, 0, P, "rot64" if kind == "large" else "rot32", *(trig[:, (0 if kind == "large" else 2) + j, :]
                                                                         for j in range(2))

        rope2 = [(k_pe[:, 0:SEQ], 64, 32, "rot32", trig[:, 2, :], trig[:, 3, :])]
        rope2 += [full("large", gqa_q[:, t, 0:SEQ]) for t in range(4)] + [full("large", gqa_k[:, 0:SEQ])]
        rope2 += [full("small", b[:, t, 0:SEQ]) for b in (diff_q, diff_k) for t in range(2)]
        rope2 += [(b, 64, 32, "rot32", trig[:, 2, :], trig[:, 3, :])
                  for b in [mla_q[:, t, 0:SEQ] for t in range(4)]]

        def rope_pe(pe, tag, jobs):
            for j, (a, p0, n, m, c, s) in enumerate(jobs):
                if j >= 8:
                    pe.wait_ge(*roped.at(tag, "sine", j - 8))
                pe.matmul(ps[p0:p0 + n, j % 8, :], cc(m)[p0:p0 + n, p0:p0 + n], a[p0:p0 + n], start=True, stop=True)\
                    .then_inc(*multiplied.on(tag, j))

        def rope_pool(pool, tag, jobs, done):
            for j, (a, p0, n, m, c, s) in enumerate(jobs):
                a = a[p0:p0 + n]
                pool.wait_ge(*multiplied.at(tag, j))
                if done + j:
                    pool.wait_ge(cosines, done + j)
                nc.gpsimd.tensor_tensor(a, a, c[p0:p0 + n], ALU.mult).then_inc(cosines, 1)

        def rope_dve(dve, tag, jobs, done):
            for j, (a, p0, n, m, c, s) in enumerate(jobs):
                a = a[p0:p0 + n]
                t = tmp[p0:p0 + n, j % 4, :]
                dve.wait_ge(*multiplied.at(tag, j))
                if j >= 4:
                    dve.wait_ge(*roped.at(tag, "sum", j - 4))
                nc.vector.tensor_tensor(t, ps[p0:p0 + n, j % 8, :], s[p0:p0 + n], ALU.mult).then_inc(*roped.on(tag, "sine", j))
                dve.wait_ge(*roped.at(tag, "sine", j))
                dve.wait_ge(cosines, done + j + 1)
                nc.vector.tensor_tensor(a, a, t, ALU.add).then_inc(*roped.on(tag, "sum", j))

        def to_tiles(*bufs):
            flat = [b[:, t, :] for b in bufs for t in range(b.shape[1])]
            return lambda m, c0, cn, s: (flat[m][:, c0:c0 + cn], s)

        def na_store(m, c0, cn, s):
            d = (na_q, na_k, na_v)[m // 4][:, m % 4, :]
            return d.rearrange("p (w r) -> p r w", r=GRID_H), s.rearrange("p (r w) -> p r w", w=GRID_W)

        def in2_store(m, c0, cn, s):
            flat = [q_low[:, 0], q_low[:, 1], diff_q[:, 0], diff_q[:, 1]] + [gqa_q[:, t] for t in range(4)] + \
                   [kv_low, k_pe, diff_k[:, 0], diff_k[:, 1], gqa_k]
            return flat[m][:, c0:c0 + cn], s

        def seq_only(m):
            return SEQ_ONLY

        def in2_pieces(l):
            return lambda m: SEQ_ONLY if m < 8 and l == LAYERS - 1 else BOTH

        plain = {
            "ret_qk": (8, KT, hs, seq_only, to_tiles(ret_q, ret_k)),
            "na_in": (12, KT, hs, seq_only, na_store),
            "xa_k": (4, KT, lambda k, c0, cn: h[:, k, SEQ:ALL], lambda m: [(0, CTX)], to_tiles(xa_k)),
            "xa_q": (4, KT, hs, seq_only, to_tiles(xa_q)),
        }
        for l in range(LAYERS):
            own = (lambda m: BOTH) if l < LAYERS - 1 else seq_only
            plain["in2", l] = (13, KT, hs, in2_pieces(l), in2_store)
            plain["out2", l] = (KT, KT, hs, own, to_tiles(attn_y))

        def run_plain(e, which, tag, ready=None):
            ms, K, rhs, pieces_of, dst = plain[tag]
            if which == "pe":
                project_pe(e, tag, ms, K, rhs, pieces_of, ready)
            else:
                project_move(e, which, tag, ms, pieces_of, dst)

        def h_tokens(c):
            return lambda k, t: h[:, k, c + t * P:c + (t + 1) * P]

        value_stages = {
            "ret_v0": (4, h_tokens(0), 4, lambda t: ret_v[:, t, 0:512]),
            "ret_v1": (4, h_tokens(0), 4, lambda t: ret_v[:, t, 512:1024]),
            "xa_v": (2, h_tokens(SEQ), 4, lambda t: xa_v[:, t, :]),
        }
        for l in range(LAYERS):
            value_stages["diff_v", l] = (6, h_tokens(0), 2, lambda t: val[:, t, 256:512])
            value_stages["gqa_v", l] = (6, h_tokens(0), 1, lambda t: val[:, t, 512:640])

        def run_values(e, which, tag):
            n, lhs, nb, dst = value_stages[tag]
            if which == "pe":
                values_pe(e, tag, n, lhs, nb)
            else:
                values_move(e, which, tag, n, dst, nb * P)

        LOW_STEP = 2

        def value_tiles(l):
            return [(("diff_v", l), t, t, None) for t in range(6)] + \
                   [(("gqa_v", l), t, t, (("diff_v", l), t)) for t in range(6)]

        def low_steps(l, step):
            return range(LOW_STEP * step, min(LOW_STEP * (step + 1), len(job_of["low", l]))) if step >= 0 else range(0)

        def value_low_pe(pe, l):
            taken = None
            for step, (tag, t, bank, before) in enumerate(value_tiles(l)):
                n, lhs, nb, _ = value_stages[tag]
                if t == 0:
                    start = chunks.block
                    taken = [take(pe, count=nb) for _ in range(KT)]
                if before:
                    pe.wait_ge(*moved_at(*before))
                for k in range(KT):
                    mm = pe.matmul(ps[:, bank, 0:nb * P], lhs(k, t), taken[k], start=(k == 0), stop=(k == KT - 1))
                    used = start + (k + 1) * nb
                    if t == n - 1 and k < KT - 1 and used % BLOCKS == 0:
                        mm.then_inc(*streamed.on("chunk", used // BLOCKS - 1))
                mm.then_inc(*streamed.on(tag, t, also=chunk_end() if t == n - 1 else None))
                for j in low_steps(l, step):
                    sums(pe, ("low", l), job_of["low", l], j, 6)

        def value_low_act(act, l):
            tiles_ = value_tiles(l)
            for step in range(len(tiles_) + 1):
                for j in low_steps(l, step):
                    squares(act, ("low", l), job_of["low", l], j)
                if step >= 1 and tiles_[step - 1][1] % 2 == 0:
                    tag, t, bank, _ = tiles_[step - 1]
                    _, _, nb, dst = value_stages[tag]
                    act.wait_ge(*streamed.at(tag, t))
                    nc.scalar.activation(dst(t), ps[:, bank, 0:nb * P], ACT.Copy).then_inc(*act_moved.on(tag, t))
                for j in low_steps(l, step - 1):
                    roots(act, ("low", l), job_of["low", l], j, 6)

        def value_low_dve(dve, l):
            tiles_ = value_tiles(l)
            for step in range(1, len(tiles_) + 1):
                if tiles_[step - 1][1] % 2 == 1:
                    tag, t, bank, _ = tiles_[step - 1]
                    _, _, nb, dst = value_stages[tag]
                    dve.wait_ge(*streamed.at(tag, t))
                    nc.vector.tensor_copy(dst(t), ps[:, bank, 0:nb * P]).then_inc(*dve_moved.on(tag, t))
                for j in low_steps(l, step - 1):
                    scale_rows(dve, ("low", l), job_of["low", l], j)

        qb = w_small[:, 0:768].rearrange("p (k n) -> p k n", k=2)
        kvb = w_small[:, 768:1280]

        def lifts(l):
            own = BOTH if l < LAYERS - 1 else SEQ_ONLY
            jobs = []
            for hd in range(MLA_H):
                for c0, cn in own:
                    jobs.append((96, cn, [(qb[:, k, hd * 96:hd * 96 + 96], q_low[:, k, c0:c0 + cn]) for k in range(2)],
                                 mla_q[0:96, hd, c0:c0 + cn]))
                for c0, cn in BOTH:
                    jobs.append((64, cn, [(kvb[:, hd * P:hd * P + 64], kv_low[:, c0:c0 + cn])], mla_k[0:64, hd, c0:c0 + cn]))
            v = kvb.rearrange("p (h n) -> p h n", h=MLA_H)[:, :, 64:128]
            for t in range(6):
                jobs.append((P, 256, [(kv_low[:, t * P:(t + 1) * P], v)], val[:, t, 0:256]))
            return jobs

        def lift_pe(pe, l):
            jobs = lifts(l)
            for g, (n, cn, products, _) in enumerate(jobs):
                if g >= 8:
                    pe.wait_ge(*moved_at(("lift", l), g - 8))
                for k, (lhs, rhs) in enumerate(products):
                    mm = pe.matmul(ps[0:n, g % 8, 0:cn], lhs, rhs, start=(k == 0), stop=(k == len(products) - 1))
                mm.then_inc(*multiplied.on("lift", l, g))

        def lift_move(e, which, l):
            jobs = lifts(l)
            for g, (n, cn, _, d) in enumerate(jobs):
                if g % 2 != which:
                    continue
                e.wait_ge(*multiplied.at("lift", l, g))
                also = ("lift done", l) if g >= len(jobs) - 2 else None
                s = ps[0:n, g % 8, 0:cn]
                if which == 0:
                    nc.scalar.activation(d, s, ACT.Copy).then_inc(*act_moved.on(("lift", l), g, also=also))
                else:
                    nc.vector.tensor_copy(d, s).then_inc(*dve_moved.on(("lift", l), g, also=also))

        def half_end(l, part, q, i):
            if q >= 0:
                return streamed.at("half", l, part, q, i=i) if part == "loop" else streamed.at("half", l, part, q)
            return streamed.at("half", l, "loop", 3 * PART - 1, i=i - 1) if part == "loop" else \
                streamed.at("half", l, "loop", 3 * PART - 1)

        def when(signal_, i, *key):
            return signal_.at(*key, i=i) if i is not None else signal_.at(*key)

        def split_products(pe, banks, q, b, high, low, pieces, start, stop):
            wh, wl = (w[:, q % SPLITS, b * P:(b + 1) * P] for w in (w_high, w_low))
            for pi, (c0, cn) in enumerate(pieces):
                pe.matmul(ps[:, banks[pi], 0:cn], wh, high[:, c0:c0 + cn], start=start, stop=False)
                pe.matmul(ps[:, banks[pi], 0:cn], wh, low[:, c0:c0 + cn], start=False, stop=False)
            return [pe.matmul(ps[:, banks[pi], 0:cn], wl, high[:, c0:c0 + cn], start=False, stop=stop)
                    for pi, (c0, cn) in enumerate(pieces)]

        def ffn_part_pe(pe, l, part, n, i, own):
            base = SPLIT_HALVES * l + OUT2_HALVES + (0 if part == "loop" else 12 * FFN_LOOPS)

            def wait_split(q):
                value = base + q + 1
                pe.wait_ge(low_split, i * 12 + value if i is not None else value)

            def wait_down(m, at_part, at_i):
                for pi in range(len(own)):
                    pe.wait_ge(*when(dve_moved, at_i, "ffn", l, at_part, m, pi))

            for t in range(n):
                for b, what in enumerate(("gate", "up")):
                    q = 2 * t + b
                    wait_split(q)
                    if t >= 2:
                        for pi in range(len(own)):
                            pe.wait_ge(*when(fused if b else gated, i, "ffn", l, part, t - 2, pi))
                    else:
                        wait_down(4 + 2 * t + b, "loop", i - 1 if i is not None else None)
                    for k in range(KT):
                        if q == 0 and part == "loop":
                            for pi in range(len(own)):
                                pe.wait_ge(*fused.at("h_low", l, pi, k))
                        ends_ = split_products(pe, [4 * (t % 2) + 2 * b + pi for pi in range(len(own))], q, k,
                                               h_round[:, k, :], h_low[:, k, :], own, k == 0, k == KT - 1)
                    for pi, mm in enumerate(ends_):
                        last = pi == len(ends_) - 1
                        mm.then_inc(*streamed.on("ffn", l, part, what, t, pi, also=("half", l, part, q) if last else None))
            for m in range(KT):
                if m >= 4:
                    wait_down(m - 4, part, i)
                for k in range(n):
                    block_ = m * n + k
                    q = 2 * n + block_ // HALF
                    if block_ % HALF == 0:
                        wait_split(q)
                    if m == 0:
                        for pi in range(len(own)):
                            pe.wait_ge(*when(fused, i, "ffn", l, part, "low", k, pi))
                    ends_ = split_products(pe, [2 * (m % 4) + pi for pi in range(len(own))], q, block_ % HALF,
                                           hid_high[:, k, :], hid_low[:, k, :], own, k == 0, k == n - 1)
                for pi, mm in enumerate(ends_):
                    last = pi == len(ends_) - 1 and block_ % HALF == HALF - 1
                    mm.then_inc(*streamed.on("ffn", l, part, "down", m, pi, also=("half", l, part, q) if last else None))

        def out2_tiles(l, ks):
            own = BOTH if l < LAYERS - 1 else SEQ_ONLY
            return [(k, pi, c0, cn) for k in ks for pi, (c0, cn) in enumerate(own)]

        def out2_high_act(l, ks):
            for k, pi, c0, cn in out2_tiles(l, ks):
                nc.scalar.activation(heads_high[:, k, c0:c0 + cn], h[:, k, c0:c0 + cn], ACT.Copy)\
                    .then_inc(*act_moved.on("heads high", l, k, pi))

        def out2_low_dve(dve, l, ks):
            for k, pi, c0, cn in out2_tiles(l, ks):
                dve.wait_ge(*act_moved.at("heads high", l, k, pi))
                nc.vector.tensor_tensor(h_round[:, k, c0:c0 + cn], h[:, k, c0:c0 + cn],
                                        heads_high[:, k, c0:c0 + cn].bitcast(F32), ALU.subtract)\
                    .then_inc(*fused.on("heads low", l, k, pi))

        def out2_pe(pe, l, own):
            for m in range(OUT2_HALVES):
                pe.wait_ge(low_split, SPLIT_HALVES * l + m + 1)
                banks = [(m * len(own) + pi) % 8 for pi in range(len(own))]
                for pi in range(len(own)):
                    if m * len(own) + pi >= 8:
                        pe.wait_ge(*moved_at(("out2", l), m * len(own) + pi - 8))
                for k in range(KT):
                    if m == 0:
                        for pi in range(len(own)):
                            pe.wait_ge(*fused.at("heads low", l, k, pi))
                    ends_ = split_products(pe, banks, m, k, heads_high[:, k, :], h_round[:, k, :], own,
                                           k == 0, k == KT - 1)
                for pi, mm in enumerate(ends_):
                    mm.then_inc(*streamed.on(("out2", l), m, pi))
            chunks.block += OUT2_HALVES * HALF

        def out2_act(act, l):
            _, _, _, pieces_of, dst = plain["out2", l]
            own = pieces_of(0)
            for m in range(OUT2_HALVES):
                if m + 2 < OUT2_HALVES:
                    free = streamed.at(("out2", l), m - 1, len(own) - 1) if m else None
                    high_part(act, OUT2_FIRST[l], m + 2, None, free)
                for g, m_, pi, c0, cn in tiles(OUT2_HALVES, pieces_of):
                    if m_ == m and g % 2 == 0:
                        act.wait_ge(*streamed.at(("out2", l), m, pi))
                        d, src = dst(m, c0, cn, ps[:, g % 8, 0:cn])
                        nc.scalar.activation(d, src, ACT.Copy).then_inc(*act_moved.on(("out2", l), g))

        def high_part(act, first, q, i, free):
            c = first + q // 2
            value = 16 * (c // RING + 1)
            act.wait_ge(loaded[c % RING], i * (16 * 3 * PART // 2 // RING) + value if i is not None else value)
            if free is not None:
                act.wait_ge(*free)
            a = (q % 2) * HALF * P
            nc.scalar.activation(w_high[:, q % SPLITS, :], ring[:, c % RING, a:a + HALF * P], ACT.Copy)\
                .then_inc(high_split, 1)

        def ffn_part_act(act, l, part, n, i, own):
            first = 0 if part == "loop" else 12 * FFN_LOOPS
            for q in range(3 * n):
                if part == "loop" or q + 2 < 3 * n:
                    high_part(act, FFN_FIRST[l], first + q + 2, i, half_end(l, part, q - 1, i))
                t = q // 2
                if t < n:
                    for pi, (c0, cn) in enumerate(own):
                        if q % 2 == 0:
                            act.wait_ge(*when(streamed, i, "ffn", l, part, "gate", t, pi))
                            if t >= 2:
                                act.wait_ge(*when(fused, i, "ffn", l, part, t - 2, pi))
                            nc.scalar.activation(tmp[:, 2 * (t % 2) + pi, 0:cn], ps[:, 4 * (t % 2) + pi, 0:cn], ACT.Silu)\
                                .then_inc(*gated.on("ffn", l, part, t, pi))
                        else:
                            act.wait_ge(*when(fused, i, "ffn", l, part, t, pi))
                            nc.scalar.activation(hid_high[:, t, c0:c0 + cn], hid_rest[:, t, c0:c0 + cn], ACT.Copy)\
                                .then_inc(*act_moved.on("ffn", l, part, "high", t, pi))

        def ffn_part_dve(dve, l, part, n, i, own):
            for t in range(n):
                for pi, (c0, cn) in enumerate(own):
                    dve.wait_ge(*when(gated, i, "ffn", l, part, t, pi))
                    dve.wait_ge(*when(streamed, i, "ffn", l, part, "up", t, pi))
                    nc.vector.tensor_tensor(hid_rest[:, t, c0:c0 + cn], tmp[:, 2 * (t % 2) + pi, 0:cn],
                                            ps[:, 4 * (t % 2) + 2 + pi, 0:cn], ALU.mult)\
                        .then_inc(*fused.on("ffn", l, part, t, pi))
                for pi, (c0, cn) in enumerate(own):
                    dve.wait_ge(*when(act_moved, i, "ffn", l, part, "high", t, pi))
                    nc.vector.tensor_tensor(hid_low[:, t, c0:c0 + cn], hid_rest[:, t, c0:c0 + cn],
                                            hid_high[:, t, c0:c0 + cn].bitcast(F32), ALU.subtract)\
                        .then_inc(*fused.on("ffn", l, part, "low", t, pi))
            for m in range(KT):
                for pi, (c0, cn) in enumerate(own):
                    dve.wait_ge(*when(streamed, i, "ffn", l, part, "down", m, pi))
                    nc.vector.tensor_tensor(ffn_y[:, m, c0:c0 + cn], ffn_y[:, m, c0:c0 + cn],
                                            ps[:, 2 * (m % 4) + pi, 0:cn], ALU.add)\
                        .then_inc(*dve_moved.on("ffn", l, part, m, pi))

        @block.gpsimd
        def _(pool):
            pool.wait_ge(*normed.at("norm_mem done"))
            nc.gpsimd.dma_start(x[:, :, SEQ:ALL], ins["ctxT"]).then_inc(context_loaded, 16)
            rope_pool(pool, "rope1", rope1, 0)
            pool.wait_ge(*streamed.at("na_in", 0, 0))
            for u in range(near_attention.units):
                if u >= 4:
                    pool.wait_ge(*fused.at("na", "biased", u - 4))
                near, mask = near_attention.bias(u)
                nc.gpsimd.tensor_tensor(near_mask[:, u % 4, :].rearrange("p (w r) -> p w r", w=WIN), near,
                                        mask.rearrange("p (w r) -> p w r", w=WIN), ALU.add).then_inc(near_masked, 1)
            pool.wait_ge(*normed.at("norm_moe", 0, "end"))
            nc.gpsimd.dma_start(slot_row, ins["slot_row"]).then_inc(slots_loaded, 16)
            pool.wait_ge(*dve_moved.at("moe done"))
            nc.gpsimd.dma_start(trig, ins["trig"]).then_inc(late_loaded, 16)
            nc.gpsimd.dma_start(w_small, ins["w_small"][0]).then_inc(late_loaded, 16)

            def low_parts(first, done, i, count):
                for q in range(count):
                    c = first + q // 2
                    pool.wait_ge(high_split, i * 12 + (done + q + 1) if i is not None else done + q + 1)
                    a = (q % 2) * HALF * P
                    nc.gpsimd.tensor_tensor(w_low[:, q % SPLITS, :], ring[:, c % RING, a:a + HALF * P],
                                            w_high[:, q % SPLITS, :].bitcast(F32), ALU.subtract).then_inc(low_split, 1)

            for l in range(LAYERS):
                pool.wait_ge(late_loaded, 16 * (2 + 2 * l))
                rope_pool(pool, ("rope2", l), rope2, len(rope1) + l * len(rope2))
                pool.wait_ge(cosines, len(rope1) + (l + 1) * len(rope2))
                low_parts(OUT2_FIRST[l], SPLIT_HALVES * l, None, OUT2_HALVES)
                nc.gpsimd.memset(ffn_y, 0.0).then_inc(cleared, 1)
                done = SPLIT_HALVES * l + OUT2_HALVES
                with pool.Fori(0, FFN_LOOPS) as i:
                    low_parts(FFN_FIRST[l], done, i, 3 * PART)
                low_parts(FFN_FIRST[l], done + 12 * FFN_LOOPS, None, 3 * LAST_PART)
                if l < LAYERS - 1:
                    pool.wait_ge(*normed.at(("ffn_post", l), 1, "end"))
                    nc.gpsimd.dma_start(w_small, ins["w_small"][l + 1]).then_inc(late_loaded, 16)
                    nc.gpsimd.dma_start(trig, ins["trig"]).then_inc(late_loaded, 16)

        @block.tensor
        def _(pe):
            def begin(wait=True):
                stage("pe", pe, wait)

            pe.wait_ge(inputs_loaded, 16 * 8)
            norm_pe(pe, "norm_x", job_of["norm_x"])
            begin(wait=False)
            run_plain(pe, "pe", "ret_qk", after_norm(pe, "norm_x"))
            begin()
            run_values(pe, "pe", "ret_v0")
            begin()
            run_values(pe, "pe", "ret_v1")
            begin()
            rope_pe(pe, "rope1", rope1)
            begin()
            for hd in range(RET_HEADS):
                for jt in range(4):
                    if hd:
                        pe.wait_ge(*fused.at("decayed", hd - 1, jt))
                    pe.matmul(ps[:, jt, :], ret_k[:, hd, jt * P:(jt + 1) * P], ret_q[:, hd, :], start=True, stop=True)\
                        .then_inc(*scored.on("ret", hd, jt))
                for e in range(2):
                    if hd:
                        pe.wait_ge(*act_moved.at("ret_y", hd - 1, e))
                    for jt in range(4):
                        pe.wait_ge(*fused.at("decayed", hd, jt))
                        mm = pe.matmul(ps[:, 4 + e, :], ret_v[:, jt, hd * 256 + e * P:hd * 256 + (e + 1) * P],
                                       ret_s[:, jt, :], start=(jt == 0), stop=(jt == 3))
                    mm.then_inc(*attended.on("ret", hd, e))
            begin()
            for hd in range(RET_HEADS):
                for e in range(2):
                    mm = pe.matmul(ps[:, hd, :], ones, ret_y[:, 2 * hd + e, :], start=(e == 0), stop=(e == 1))
                mm.then_inc(*summed.on("ret_mean", hd))
            begin()
            norm_pe(pe, "ret_norm", job_of["ret_norm"])
            begin(wait=False)
            for m in range(8):
                if m >= 6:
                    pe.wait_ge(*rooted.at("ret_norm", m - 4))
                group(pe, ("ret_gate", m), [(m + 2) % 8], hs, KT, SEQ_ONLY)
            begin()
            branch_pe(pe, "ret_out", 8, lambda k, c0, cn: ret_y[:, k, :])
            begin()
            run_plain(pe, "pe", "na_in")
            begin()
            for w in range(8):
                k0 = WIN_AT[w // 2] * GRID_H + (w % 2) * P
                for c in range(4):
                    mm = pe.transpose(ps[:, w, c * P:(c + 1) * P], na_v[:, c, k0:k0 + P], ident)
                mm.then_inc(*turned.on("windows", w))
            begin()
            attend_pe(pe, near_attention)
            begin()
            branch_pe(pe, "na_out", 4, lambda k, c0, cn: na_o[:, k, :])
            begin()
            run_plain(pe, "pe", "xa_k")
            begin()
            run_values(pe, "pe", "xa_v")
            begin()
            run_plain(pe, "pe", "xa_q")
            begin()
            attend_pe(pe, memory_attention)
            begin()
            branch_pe(pe, "xa_out", 4, lambda k, c0, cn: xa_o[:, k, :])
            begin()
            for m in range(KT):
                group(pe, ("mix_out", m), [m], lambda k, c0, cn: mixed_sum[:, k, :], KT, SEQ_ONLY)
            begin()
            norm_pe(pe, "norm_moe", job_of["norm_moe"])
            begin(wait=False)
            ready = after_norm(pe, "norm_moe")
            for t in range(4):
                for k in range(KT):
                    if t == 0:
                        ready(k, 0)
                    mm = pe.matmul(ps[:, 0, t * 20:(t + 1) * 20], h[:, k, t * P:(t + 1) * P], w_router[:, k, :],
                                   start=(k == 0), stop=(k == KT - 1))
            mm.then_inc(*multiplied.on("logits"))
            for t in range(4):
                for half in range(2):
                    g = 2 * t + half
                    bank = 4 + g % 4
                    if g >= 4:
                        pe.wait_ge(*act_moved.at("h_tok", g - 4))
                    for k in range(4):
                        mm = pe.transpose(ps[:, bank, k * P:(k + 1) * P], h[:, 4 * half + k, t * P:(t + 1) * P], ident)
                    mm.then_inc(*turned.on("h_tok", g))
            pe.wait_ge(*small.at("group", "hit"))
            for t in range(4):
                for t2 in range(t + 1):
                    pe.matmul(ps[:, 1, t * 4:t * 4 + 4], ones if t2 < t else cc("before"), R["g1"][:, t2, :],
                              start=(t2 == 0), stop=(t2 == t))
            for t in range(4):
                mm = pe.matmul(ps[:, 1, 16:20], ones, R["g1"][:, t, :], start=(t == 0), stop=(t == 3))
            mm.then_inc(*multiplied.on("places"))
            pe.wait_ge(*small.at("slot diagonal", 3))
            pe.matmul(ps[:, 2, :], ones, tmp[:, 0, :], start=True, stop=True).then_inc(*multiplied.on("slot row"))
            pe.wait_ge(*small.at("picked", 3))
            pe.wait_ge(*small.at("expert weights"))
            for u in range(UNITS):
                for t in range(4):
                    mm = pe.matmul(ps[:, 3, 4 * u:4 * u + 4], pick[:, t, u * P:(u + 1) * P], R["ee"][:, t, :],
                                   start=(t == 0), stop=(t == 3))
            mm.then_inc(*multiplied.on("slot weights"))

            def gather(slots_of, bank, half, key):
                for k in range(4):
                    for t in range(4):
                        mm = pe.matmul(ps[:, bank, k * P:(k + 1) * P],
                                       h_tok[:, t, (4 * half + k) * P:(4 * half + k + 1) * P], slots_of(t),
                                       start=(t == 0), stop=(t == 3))
                mm.then_inc(*attended.on("gather", key, half))

            for half in range(2):
                pe.wait_ge(*act_moved.at("h_tok", 7))
                gather(lambda t: pick[:, t, 0:P], (7, 0)[half], half, "first")
            begin()
            assert chunks.block == MOE_FIRST * BLOCKS
            with repeated(pe, UNITS, signals["pe"]) as i:
                before = chunks.block

                def gate_or_up(e, what, bank):
                    for k in range(KT):
                        w = take(pe, i, count=4)
                        mm = pe.matmul(ps[:, bank, :], unit_h[:, k, :], w, start=(k == 0), stop=(k == KT - 1))
                        if k == KT - 1:
                            mm.then_inc(*streamed.on("moe", what, e, also=chunk_end()))
                        elif chunk_end():
                            mm.then_inc(*streamed.on(*chunk_end()))

                def turn(e):
                    pe.wait_ge(*fused.at("moe", "hid", e, i=i))
                    if e == IN_GROUP - 1:
                        pe.wait_ge(*act_moved.at("moe", "hid_t", e - 1, i=i))
                    for f in range(4):
                        mm = pe.transpose(ps[:, 4, f * P:(f + 1) * P], hid[:, e % 2, f * P:(f + 1) * P], ident)
                    mm.then_inc(*turned.on("moe", e))

                def down(e):
                    pe.wait_ge(*act_moved.at("moe", "hid_t", e, i=i))
                    for k in range(4):
                        for half in range(2):
                            w = take(pe, i, count=4)
                            mm = pe.matmul(ps[:, 5 + half, :], hid_t[:, e % 2, k, :], w, start=(e == 0 and k == 0),
                                           stop=(e == IN_GROUP - 1 and k == 3))
                            if e == IN_GROUP - 1 and k == 3:
                                mm.then_inc(*streamed.on("moe", "down", half, also=chunk_end()))
                            elif chunk_end():
                                mm.then_inc(*streamed.on(*chunk_end()))

                pe.wait_ge(*act_moved.at("gather", "next", i=i - 1))
                pe.wait_ge(*dve_moved.at("gather", "next", i=i - 1))
                for e in range(IN_GROUP):
                    if e >= 2:
                        pe.wait_ge(*gated.at("moe", e - 2, i=i))
                    gate_or_up(e, "gate", 2 * (e % 2))
                    if e >= 1:
                        turn(e - 1)
                    if e >= 2:
                        pe.wait_ge(*fused.at("moe", "hid", e - 2, i=i))
                    gate_or_up(e, "up", 2 * (e % 2) + 1)
                    if e == 1:
                        pe.wait_ge(*act_moved.at("moe", "y", i=i - 1))
                        pe.wait_ge(*dve_moved.at("moe", "y", i=i - 1))
                    if 1 <= e < IN_GROUP - 1:
                        down(e - 1)
                for half in range(2):
                    gather(lambda t: pick[:, t, bass.ds(i * P + P, P)], (7, 0)[half], half, "next")
                turn(IN_GROUP - 1)
                down(IN_GROUP - 2)
                down(IN_GROUP - 1)
                assert chunks.block - before == UNIT_CHUNKS * BLOCKS
            chunks.block += UNIT_CHUNKS * BLOCKS * (UNITS - 1)
            begin()
            for m in range(KT):
                for u in range(UNITS):
                    pe.wait_ge(*small.at("put", u))
                    mm = pe.matmul(ps[:, m, :], unit_y[:, u * D + m * P:u * D + (m + 1) * P], put[:, u, :],
                                   start=(u == 0), stop=(u == UNITS - 1))
                mm.then_inc(*attended.on("put", m))
            begin()
            norm_pe(pe, "norm_first", job_of["norm_first"])
            begin()
            for l in range(LAYERS):
                own = BOTH if l < LAYERS - 1 else SEQ_ONLY
                norm_pe(pe, ("attn_pre", l), job_of["attn_pre", l])
                pe.wait_ge(*small.at("lambda products", l))
                pe.matmul(ps[:, 7, 0:2], ones[0:32, :], cols[0:32, 2:4], start=True, stop=True)\
                    .then_inc(*multiplied.on("lambda", l))
                begin(wait=False)
                ready = after_norm(pe, ("attn_pre", l), shifted=True)
                pe.wait_ge(*exped.at("lambda", l))
                if l == LAYERS - 1:
                    for k in range(KT):
                        ready(k, 1)
                run_plain(pe, "pe", ("in2", l), ready)
                begin()
                value_low_pe(pe, l)
                begin()
                pe.wait_ge(late_loaded, 16 * (2 + 2 * l))
                lift_pe(pe, l)
                begin()
                rope_pe(pe, ("rope2", l), rope2)
                begin()
                for a in attentions[l]:
                    attend_pe(pe, a)
                    begin()
                begin()
                norm_pe(pe, ("diff", l), job_of["diff", l])
                begin()
                out2_pe(pe, l, own)
                begin()
                norm_pe(pe, ("attn_post", l), job_of["attn_post", l])
                begin()
                norm_pe(pe, ("ffn_pre", l), job_of["ffn_pre", l])
                begin(wait=False)
                for j in range(len(own)):
                    pe.wait_ge(*rooted.at(("ffn_pre", l), j))
                assert chunks.block == FFN_FIRST[l] * BLOCKS
                with repeated(pe, FFN_LOOPS, signals["pe"]) as i:
                    ffn_part_pe(pe, l, "loop", PART, i, own)
                ffn_part_pe(pe, l, "last", LAST_PART, None, own)
                chunks.block += FFN_HALVES * HALF
                begin()
                norm_pe(pe, ("ffn_post", l), job_of["ffn_post", l])
                begin()
            assert chunks.block == (n_chunks + (UNITS - GROUPS) * UNIT_CHUNKS) * BLOCKS

        @block.scalar
        def _(act):
            def begin(wait=True):
                stage("act", act, wait)

            act.wait_ge(inputs_loaded, 16 * 8)
            act.wait_ge(*small.at("epsilons"))
            norm_act(act, "norm_x", job_of["norm_x"])
            begin()
            nc.scalar.activation(silu_c[:].rearrange("p a b -> p (a b)"), pc("c", 0, 16), ACT.Silu).then_inc(*act_moved.on("silu_c"))
            nc.scalar.activation(route[:, 0:8], pc("decay", 0, 8), ACT.Abs).then_inc(*act_moved.on("abs"))
            act.wait_ge(*act_moved.at("abs"))
            nc.scalar.activation(route[:, 8:16], route[:, 0:8], ACT.Exp, scale=-1.0).then_inc(*exped.on("decay"))
            act.wait_ge(*small.at("one plus"))
            nc.scalar.activation(route[:, 24:32], route[:, 16:24], ACT.Ln).then_inc(*exped.on("decay log"))
            run_plain(act, 0, "ret_qk")
            begin()
            run_values(act, 0, "ret_v0")
            begin()
            run_values(act, 0, "ret_v1")
            begin()
            begin()
            for hd in range(RET_HEADS):
                act.wait_ge(*fused.at("exponent", hd))
                if hd >= 2:
                    act.wait_ge(*fused.at("decayed", hd - 2, 3))
                nc.scalar.activation(ret_e[:, hd % 2, :], ret_t, ACT.Exp).then_inc(*exped.on("ret", hd))
                for e in range(2):
                    act.wait_ge(*attended.at("ret", hd, e))
                    nc.scalar.activation(ret_y[:, 2 * hd + e, :], ps[:, 4 + e, :], ACT.Copy).then_inc(*act_moved.on("ret_y", hd, e))
            begin()
            begin()
            norm_act(act, "ret_norm", job_of["ret_norm"])
            begin()
            for m in range(8):
                act.wait_ge(*streamed.at("ret_gate", m, 0))
                nc.scalar.activation(tmp[:, m, :], ps[:, (m + 2) % 8, :], ACT.Silu).then_inc(*gated.on("ret_gate", m))
            begin()
            branch_act(act, "ret_out")
            begin()
            run_plain(act, 0, "na_in")
            begin()
            for w in range(0, 8, 2):
                act.wait_ge(*turned.at("windows", w))
                nc.scalar.activation(na_win[:, w, :], ps[:, w, :], ACT.Copy).then_inc(*act_moved.on("windows", w))
            begin()
            attend_act(act, near_attention)
            begin()
            branch_act(act, "na_out")
            begin()
            run_plain(act, 0, "xa_k")
            begin()
            run_values(act, 0, "xa_v")
            begin()
            run_plain(act, 0, "xa_q")
            begin()
            attend_act(act, memory_attention)
            begin()
            branch_act(act, "xa_out")
            begin()
            begin()
            norm_act(act, "norm_moe", job_of["norm_moe"])
            begin()
            act.wait_ge(*small.at("group distance"))
            nc.scalar.activation(R["ge"], R["gd"], ACT.Exp).then_inc(*exped.on("groups"))
            act.wait_ge(*small.at("expert distance"))
            nc.scalar.activation(R["ee"], R["ed"], ACT.Exp).then_inc(*exped.on("experts"))
            for g in range(8):
                act.wait_ge(*turned.at("h_tok", g))
                nc.scalar.activation(h_tok[:, g // 2, (g % 2) * 512:(g % 2) * 512 + 512], ps[:, 4 + g % 4, :], ACT.Copy)\
                    .then_inc(*act_moved.on("h_tok", g))
            act.wait_ge(*attended.at("gather", "first", 0))
            nc.scalar.activation(unit_h[:, 0:4, :].rearrange("p a b -> p (a b)"), ps[:, 7, :], ACT.Copy)\
                .then_inc(*act_moved.on("gather", "first"))
            begin()
            with repeated(act, UNITS, signals["act"]) as i:
                for e in range(IN_GROUP):
                    act.wait_ge(*streamed.at("moe", "gate", e, i=i))
                    if e >= 2:
                        act.wait_ge(*fused.at("moe", "hid", e - 2, i=i))
                    nc.scalar.activation(tmp[:, e % 2, :], ps[:, 2 * (e % 2), :], ACT.Silu).then_inc(*gated.on("moe", e))
                    if e >= 1:
                        act.wait_ge(*turned.at("moe", e - 1, i=i))
                        nc.scalar.activation(hid_t[:, (e - 1) % 2].rearrange("p a b -> p (a b)"), ps[:, 4, :], ACT.Copy)\
                            .then_inc(*act_moved.on("moe", "hid_t", e - 1))
                act.wait_ge(*attended.at("gather", "next", 0, i=i))
                nc.scalar.activation(unit_h[:, 0:4, :].rearrange("p a b -> p (a b)"), ps[:, 7, :], ACT.Copy)\
                    .then_inc(*act_moved.on("gather", "next"))
                e = IN_GROUP - 1
                act.wait_ge(*turned.at("moe", e, i=i))
                nc.scalar.activation(hid_t[:, e % 2].rearrange("p a b -> p (a b)"), ps[:, 4, :], ACT.Copy)\
                    .then_inc(*act_moved.on("moe", "hid_t", e))
                act.wait_ge(*streamed.at("moe", "down", 0, i=i))
                nc.scalar.activation(unit_y[:, bass.ds(i * D, 512)], ps[:, 5, :], ACT.Copy).then_inc(*act_moved.on("moe", "y"))
            begin()
            begin()
            norm_act(act, "norm_first", job_of["norm_first"])
            begin()
            for l in range(LAYERS):
                own = BOTH if l < LAYERS - 1 else SEQ_ONLY
                if l == 0:
                    act.wait_ge(context_loaded, 16)
                norm_act(act, ("attn_pre", l), job_of["attn_pre", l], x_ready(("ffn_post", l - 1)) if l else None)
                act.wait_ge(*multiplied.at("lambda", l))
                nc.scalar.activation(cols[:, 4:6], ps[:, 7, 0:2], ACT.Exp).then_inc(*exped.on("lambda", l))
                for j, (c0, cn) in enumerate(BOTH):
                    for k in range(KT):
                        act.wait_ge(*normed.at(("attn_pre", l), j, "end" if k == KT - 1 else k))
                        nc.scalar.activation(hs(k, c0, cn), hs(k, c0, cn), ACT.Identity, bias=mod(l, 0, k, c0))\
                            .then_inc(*act_moved.on("shifted", ("attn_pre", l), j, k))
                begin()
                run_plain(act, 0, ("in2", l))
                begin()
                value_low_act(act, l)
                begin()
                lift_move(act, 0, l)
                begin()
                act.wait_ge(*roped.at(("rope2", l), "sum", 0))
                for hd in range(MLA_H):
                    nc.scalar.activation(mla_k[64:96, hd, :], k_pe[64:96, :], ACT.Copy).then_inc(*act_moved.on("k_pe", l, hd))
                begin()
                for a in attentions[l]:
                    attend_act(act, a)
                    begin()
                high_part(act, OUT2_FIRST[l], 0, None, None)
                out2_high_act(l, range(2))
                begin()
                norm_act(act, ("diff", l), job_of["diff", l])
                high_part(act, OUT2_FIRST[l], 1, None, None)
                begin()
                out2_high_act(l, range(2, 4))
                out2_high_act(l, range(4, KT))
                out2_act(act, l)
                begin(wait=False)
                norm_act(act, ("attn_post", l), job_of["attn_post", l], moved_ready(("out2", l), len(own)))
                begin(wait=False)
                for q in range(2):
                    high_part(act, FFN_FIRST[l], q, None, streamed.at(("out2", l), OUT2_HALVES - 1, len(own) - 1))
                norm_act(act, ("ffn_pre", l), job_of["ffn_pre", l], x_ready(("attn_post", l)))
                for j, (c0, cn) in enumerate(own):
                    for k in range(KT):
                        act.wait_ge(*normed.at(("ffn_pre", l), j, "end" if k == KT - 1 else k))
                        nc.scalar.activation(h_round[:, k, c0:c0 + cn], h_rest[:, k, c0:c0 + cn], ACT.Identity,
                                             bias=mod(l, 3, k, c0)).then_inc(*act_moved.on("h_high", l, j, k))
                begin()
                with repeated(act, FFN_LOOPS, signals["act"]) as i:
                    ffn_part_act(act, l, "loop", PART, i, own)
                ffn_part_act(act, l, "last", LAST_PART, None, own)
                begin(wait=False)
                norm_act(act, ("ffn_post", l), job_of["ffn_post", l], lambda j, k: dve_moved.at("ffn", l, "last", k, j))
                begin(wait=False)

        @block.vector
        def _(dve):
            def begin(wait=True):
                stage("dve", dve, wait)

            def then(instruction, *key):
                instruction.then_inc(*small.on(*key))
                dve.wait_ge(*small.at(*key))

            nc.vector.memset(cols[:, 0:1], 1e-6).then_inc(*small.on("epsilon norm"))
            nc.vector.memset(cols[:, 1:2], 1e-5).then_inc(*small.on("epsilons"))
            dve.wait_ge(inputs_loaded, 16 * 8)
            norm_dve(dve, "norm_x", job_of["norm_x"])
            begin()
            e_, one_e, ln_e, d_, eq_, t_ = (route[:, a:a + 8] for a in (8, 16, 24, 32, 40, 48))
            dve.wait_ge(*exped.at("decay"))
            nc.vector.tensor_scalar(one_e, e_, 1.0, None, ALU.add).then_inc(*small.on("one plus"))
            dve.wait_ge(*small.at("one plus"))
            then(nc.vector.tensor_scalar(d_, one_e, -1.0, None, ALU.add), "lg", 0)
            then(nc.vector.tensor_scalar(eq_, d_, 0.0, None, ALU.is_equal), "lg", 1)
            then(nc.vector.tensor_tensor(d_, d_, eq_, ALU.add), "lg", 2)
            then(nc.vector.reciprocal(d_, d_), "lg", 3)
            dve.wait_ge(*exped.at("decay log"))
            then(nc.vector.tensor_tensor(ln_e, ln_e, eq_, ALU.add), "lg", 4)
            then(nc.vector.tensor_tensor(d_, d_, e_, ALU.mult), "lg", 5)
            then(nc.vector.tensor_tensor(d_, d_, ln_e, ALU.mult), "lg", 6)
            then(nc.vector.tensor_scalar(t_, pc("decay", 0, 8), 0.0, None, ALU.min), "lg", 7)
            then(nc.vector.tensor_tensor(route[:, 56:64], t_, d_, ALU.subtract), "lg", 8)
            lg = route[:, 56:64]
            run_plain(dve, 1, "ret_qk")
            begin()
            run_values(dve, 1, "ret_v0")
            begin()
            run_values(dve, 1, "ret_v1")
            begin()
            rope_dve(dve, "rope1", rope1, 0)
            begin()
            for hd in range(RET_HEADS):
                if hd:
                    dve.wait_ge(*exped.at("ret", hd - 1))
                nc.vector.tensor_scalar(ret_t, dist[:, 1, :], lg[:, 4 + hd:5 + hd], None, ALU.mult)\
                    .then_inc(*fused.on("backward", hd))
                dve.wait_ge(*fused.at("backward", hd))
                nc.vector.scalar_tensor_tensor(out=ret_t, in0=dist[:, 0, :], scalar=lg[:, hd:hd + 1], in1=ret_t,
                                               op0=ALU.mult, op1=ALU.add).then_inc(*fused.on("exponent", hd))
                dve.wait_ge(*exped.at("ret", hd))
                for jt in range(4):
                    dve.wait_ge(*scored.at("ret", hd, jt))
                    if hd:
                        dve.wait_ge(*attended.at("ret", hd - 1, 1))
                    a = 3 * P - jt * P
                    nc.vector.scalar_tensor_tensor(out=ret_s[:, jt, :], in0=ps[:, jt, :], scalar=128 ** -0.5,
                                                   in1=ret_e[:, hd % 2, a:a + SEQ], op0=ALU.mult, op1=ALU.mult)\
                        .then_inc(*fused.on("decayed", hd, jt))
            begin()
            for hd in range(RET_HEADS):
                dve.wait_ge(*summed.at("ret_mean", hd))
                for e in range(2):
                    nc.vector.scalar_tensor_tensor(out=ret_y[:, 2 * hd + e, :], in0=ps[:, hd, :], scalar=-1.0 / 256,
                                                   in1=ret_y[:, 2 * hd + e, :], op0=ALU.mult, op1=ALU.add)\
                        .then_inc(*fused.on("centred", hd, e))
            begin()
            norm_dve(dve, "ret_norm", job_of["ret_norm"])
            begin()
            for m in range(8):
                dve.wait_ge(*gated.at("ret_gate", m))
                nc.vector.tensor_tensor(ret_y[:, m, :], ret_y[:, m, :], tmp[:, m, :], ALU.mult).then_inc(*fused.on("ret_gated", m))
            begin()
            branch_dve(dve, "ret_out", 0)
            begin()
            run_plain(dve, 1, "na_in")
            begin()
            for w in range(1, 8, 2):
                dve.wait_ge(*turned.at("windows", w))
                nc.vector.tensor_copy(na_win[:, w, :], ps[:, w, :]).then_inc(*dve_moved.on("windows", w))
            begin()
            attend_dve(dve, near_attention)
            begin()
            branch_dve(dve, "na_out", 1)
            begin()
            run_plain(dve, 1, "xa_k")
            begin()
            run_values(dve, 1, "xa_v")
            begin()
            run_plain(dve, 1, "xa_q")
            begin()
            attend_dve(dve, memory_attention)
            begin()
            branch_dve(dve, "xa_out", 2)
            begin()
            for m in range(KT):
                dve.wait_ge(*streamed.at("mix_out", m, 0))
                nc.vector.tensor_tensor(x[:, m, 0:SEQ], x[:, m, 0:SEQ], ps[:, m, :], ALU.add).then_inc(*dve_moved.on("mix_out", m))
            begin()
            norm_dve(dve, "norm_moe", job_of["norm_moe"])
            begin()
            def wide(ap):
                return spread(ap, (1, 4), (0, 4))

            def first_best(hit, out_, *key):
                then(nc.vector.tensor_tensor(R["cand"], hit, R["rank"], ALU.mult), *key, "rank")
                then(nc.vector.reduce_max(R["best"], R["cand"], AX), *key, "best")
                then(nc.vector.tensor_tensor(out_, R["cand"], wide(R["best"]), ALU.is_equal), *key, "hit")

            dve.wait_ge(*multiplied.at("logits"))
            then(nc.vector.tensor_tensor(R["lg"], ps[:, 0, 0:80].rearrange("p (t n) -> p t n", t=4),
                                         pc("router_bias", 0, 80).rearrange("p (t n) -> p t n", t=4), ALU.add), "logits")
            gl, el = R["lg"][:, :, 0:4], R["lg"][:, :, 4:20]
            then(nc.vector.reduce_max(R["gm"], gl, AX), "group max")
            then(nc.vector.tensor_tensor(R["gd"], gl, wide(R["gm"]), ALU.subtract), "group distance")
            then(nc.vector.tensor_scalar(R["eq"], R["gd"], 0.0, None, ALU.is_ge), "group hits")
            first_best(R["eq"], R["g1"], "group")
            dve.wait_ge(*exped.at("groups"))
            then(nc.vector.reduce_sum(R["gw"], R["ge"], axis=AX), "group sum")
            then(nc.vector.reciprocal(R["gw"], R["gw"]), "group weight")
            g1_wide = spread(R["g1"], (4, 4), (1, 4), (0, 4))
            then(nc.vector.tensor_tensor(R["sel"], el.rearrange("p t (g e) -> p t g e", g=4), g1_wide, ALU.mult), "chosen")
            sel_a = R["sel"]
            then(nc.vector.reduce_sum(R["ig"], sel_a.rearrange("p t g e -> p t e g"), axis=AX), "in group")
            then(nc.vector.reduce_max(R["em"], R["ig"], AX), "expert max")
            then(nc.vector.tensor_tensor(R["ed"], R["ig"], wide(R["em"]), ALU.subtract), "expert distance")
            then(nc.vector.tensor_scalar(R["eq"], R["ed"], 0.0, None, ALU.is_ge), "expert hits")
            first_best(R["eq"], R["o1"], "first")
            then(nc.vector.scalar_tensor_tensor(out=R["e2"], in0=R["o1"], scalar=-BIG, in1=R["ed"], op0=ALU.mult,
                                                op1=ALU.add), "without the first")
            then(nc.vector.reduce_max(R["em"], R["e2"], AX), "second max")
            then(nc.vector.tensor_tensor(R["eq"], R["e2"], wide(R["em"]), ALU.is_equal), "second hits")
            first_best(R["eq"], R["o2"], "second")
            then(nc.vector.tensor_tensor(R["o1"], R["o1"], R["o2"], ALU.add), "both")
            dve.wait_ge(*exped.at("experts"))
            then(nc.vector.tensor_tensor(R["ee"], R["ee"], R["o1"], ALU.mult), "two weights")
            then(nc.vector.reduce_sum(R["em"], R["ee"], axis=AX), "their sum")
            then(nc.vector.reciprocal(R["em"], R["em"]), "its reciprocal")
            then(nc.vector.tensor_tensor(R["em"], R["em"], R["gw"], ALU.mult), "with the group's weight")
            then(nc.vector.tensor_tensor(R["ee"], R["ee"], wide(R["em"]), ALU.mult), "expert weights")
            dve.wait_ge(*multiplied.at("places"))
            then(nc.vector.tensor_copy(R["rk"].rearrange("p a b -> p (a b)"), ps[:, 1, 0:16]), "ranks")
            then(nc.vector.tensor_copy(R["n"], ps[:, 1, 16:20]), "sizes")
            steps = cc("steps").rearrange("p (t n) -> p t n", t=4)
            then(nc.vector.tensor_tensor(R["cmp"], wide(R["n"]), steps, ALU.is_gt), "size steps")
            then(nc.vector.reduce_sum(R["units"], R["cmp"], axis=AX), "units of each group")
            then(nc.vector.memset(R["from"][:, 0:1], 0.0), "first unit", 0)
            for g in range(GROUPS):
                then(nc.vector.tensor_tensor(R["from"][:, g + 1:g + 2], R["from"][:, g:g + 1], R["units"][:, g:g + 1],
                                             ALU.add), "first unit", g + 1)
            no = cc("unit_no").rearrange("p (u g) -> p u g", g=4)
            over = R["over"].rearrange("p (u g) -> p u g", g=4)
            then(nc.vector.tensor_tensor(over, spread(R["from"][:, 1:5], (0, UNITS), (1, 4)), no, ALU.is_le), "groups before")
            then(nc.vector.reduce_sum(R["ug"], over, axis=AX), "group of each unit")
            then(nc.vector.tensor_scalar(unit_group[:, 0:UNITS], R["ug"], float(GROUPS - 1), None, ALU.min), "unit groups")
            then(nc.vector.scalar_tensor_tensor(out=R["rk"], in0=spread(R["from"], (0, 4), (1, 4)), scalar=float(P),
                                                in1=R["rk"], op0=ALU.mult, op1=ALU.add), "slots if in group")
            then(nc.vector.tensor_tensor(R["rk"], R["rk"], R["g1"], ALU.mult), "slot of its group")
            then(nc.vector.reduce_sum(R["slot"], R["rk"], axis=AX), "slots")
            for t in range(4):
                nc.vector.tensor_scalar(tmp[:, 0, t * P:(t + 1) * P], ident, R["slot"][:, t:t + 1], None, ALU.mult)\
                    .then_inc(*small.on("slot diagonal", t))
            dve.wait_ge(slots_loaded, 16)
            for t in range(4):
                nc.vector.tensor_scalar(pick[:, t, :], slot_row, R["slot"][:, t:t + 1], None, ALU.is_equal)\
                    .then_inc(*small.on("picked", t))
            dve.wait_ge(*multiplied.at("slot weights"))
            nc.vector.tensor_copy(R["w"], ps[:, 3, 0:4 * UNITS]).then_inc(*small.on("slot weights"))
            dve.wait_ge(*attended.at("gather", "first", 1))
            nc.vector.tensor_copy(unit_h[:, 4:8, :].rearrange("p a b -> p (a b)"), ps[:, 0, :])\
                .then_inc(*dve_moved.on("gather", "first"))
            for u in range(UNITS):
                nc.vector.tensor_scalar(put[:, u, :], ps[:, 2, :], cc("slot_no")[:, u:u + 1], None, ALU.is_equal)\
                    .then_inc(*small.on("put", u))
            begin()
            with repeated(dve, UNITS, signals["dve"]) as i:
                for e in range(IN_GROUP):
                    dve.wait_ge(*gated.at("moe", e, i=i))
                    dve.wait_ge(*streamed.at("moe", "up", e, i=i))
                    nc.vector.scalar_tensor_tensor(out=hid[:, e % 2, :], in0=tmp[:, e % 2, :],
                                                   scalar=R["w"][:, bass.ds(i * 4 + e, 1)],
                                                   in1=ps[:, 2 * (e % 2) + 1, :], op0=ALU.mult, op1=ALU.mult)\
                        .then_inc(*fused.on("moe", "hid", e))
                dve.wait_ge(*attended.at("gather", "next", 1, i=i))
                nc.vector.tensor_copy(unit_h[:, 4:8, :].rearrange("p a b -> p (a b)"), ps[:, 0, :])\
                    .then_inc(*dve_moved.on("gather", "next"))
                dve.wait_ge(*streamed.at("moe", "down", 1, i=i))
                nc.vector.tensor_copy(unit_y[:, bass.ds(i * D + 512, 512)], ps[:, 6, :]).then_inc(*dve_moved.on("moe", "y"))
            begin()
            for m in range(KT):
                dve.wait_ge(*attended.at("put", m))
                nc.vector.tensor_tensor(x[:, m, 0:SEQ], x[:, m, 0:SEQ], ps[:, m, :], ALU.add)\
                    .then_inc(*dve_moved.on("moe result", m, also=("moe done",) if m == KT - 1 else None))
            begin()
            norm_dve(dve, "norm_first", job_of["norm_first"])
            begin()
            for l in range(LAYERS):
                own = BOTH if l < LAYERS - 1 else SEQ_ONLY
                lam = pc(f"lambda{l}", 0, 4)
                nc.vector.tensor_tensor(cols[:, 2:4], spread(lam, (2, 2)), spread(lam[:, 1:2], (2, 2)), ALU.mult)\
                    .then_inc(*small.on("lambda products", l))

                def gains(kind, name, which, plus, *key):
                    for s in range(2):
                        a = 8 + (kind * 2 + s) * 8
                        m = spread(mods[:, l * 48 + which * 8, s:s + 1], (2, 8))
                        then(nc.vector.scalar_tensor_tensor(out=cols[:, a:a + 8], in0=m, scalar=plus, in1=pc(name, 0, 8),
                                                            op0=ALU.add, op1=ALU.mult), *key, s)
                gains(0, f"attn_pre{l}", 1, 1.0, "attn_pre", l)
                gains(1, f"attn_post{l}", 2, 0.0, "attn_post", l)
                if l == 0:
                    dve.wait_ge(context_loaded, 16)
                norm_dve(dve, ("attn_pre", l), job_of["attn_pre", l])
                dve.wait_ge(*exped.at("lambda", l))
                then(nc.vector.tensor_tensor(cols[:, 7:8], cols[:, 5:6], cols[:, 4:5], ALU.subtract), "lambda", l, 0)
                then(nc.vector.tensor_scalar(cols[:, 7:8], cols[:, 7:8], -LAM_INIT[l], None, ALU.add), "lambda", l, 1)
                then(nc.vector.tensor_scalar(cols[:, 6:7], pc(f"diff_sub{l}"), 1.0 - LAM_INIT[l], None, ALU.mult),
                     "lambda", l, 2)
                begin()
                run_plain(dve, 1, ("in2", l))
                begin()
                value_low_dve(dve, l)
                begin()
                lift_move(dve, 1, l)
                begin()
                dve.wait_ge(late_loaded, 16 * (2 + 2 * l))
                rope_dve(dve, ("rope2", l), rope2, len(rope1) + l * len(rope2))
                begin()
                for a in attentions[l]:
                    attend_dve(dve, a)
                    begin()
                for t in range(2):
                    w = ALL if l < LAYERS - 1 else SEQ
                    nc.vector.scalar_tensor_tensor(out=out_1[:, t, 0:w], in0=out_2[:, t, 0:w], scalar=cols[:, 7:8],
                                                   in1=out_1[:, t, 0:w], op0=ALU.mult, op1=ALU.add)\
                        .then_inc(*fused.on("difference", l, t))
                begin()
                out2_low_dve(dve, l, range(2))
                norm_dve(dve, ("diff", l), job_of["diff", l])
                begin()
                out2_low_dve(dve, l, range(2, KT))
                run_plain(dve, 1, ("out2", l))
                begin()
                norm_dve(dve, ("attn_post", l), job_of["attn_post", l])
                begin()
                gains(0, f"ffn_pre{l}", 4, 1.0, "ffn_pre", l)
                gains(1, f"ffn_post{l}", 5, 0.0, "ffn_post", l)
                norm_dve(dve, ("ffn_pre", l), job_of["ffn_pre", l])
                for k in range(KT):
                    for j, (c0, cn) in enumerate(own):
                        dve.wait_ge(*act_moved.at("h_high", l, j, k))
                        nc.vector.scalar_tensor_tensor(
                            out=h_low[:, k, c0:c0 + cn], in0=h_rest[:, k, c0:c0 + cn], scalar=mod(l, 3, k, c0),
                            in1=h_round[:, k, c0:c0 + cn].bitcast(F32), op0=ALU.add, op1=ALU.subtract)\
                            .then_inc(*fused.on("h_low", l, j, k))
                begin()
                dve.wait_ge(cleared, l + 1)
                with repeated(dve, FFN_LOOPS, signals["dve"]) as i:
                    ffn_part_dve(dve, l, "loop", PART, i, own)
                ffn_part_dve(dve, l, "last", LAST_PART, None, own)
                begin()
                norm_dve(dve, ("ffn_post", l), job_of["ffn_post", l])
                begin()
            normed.points[("final",)] = (normed.n, 0, 1)
    return {**{s.name: s.points for v in signals.values() for s in v}, "ends": ends}


def _blocks(w):
    k, m = w.shape
    return w.reshape(k // P, P, m // P, P).transpose(2, 0, 1, 3).reshape(-1, P, P)


def _side_by_side(w):
    k, m = w.shape
    return w.reshape(k // P, P, m // P, P).transpose(0, 2, 1, 3).reshape(-1, P, P)


def _interleaved(*ws):
    tiles = [_blocks(w).reshape(w.shape[1] // P, w.shape[0] // P, P, P) for w in ws]
    return np.concatenate([t[m] for m in range(tiles[0].shape[0]) for t in tiles])


def _stream(a):
    w, kvw = a["w_in"][0], a["w_mem_kv"][0]
    gates = [w[:, 5120 + b * D:5120 + (b + 1) * D] for b in range(3)]
    ada = _blocks(np.concatenate([a["w_ada_2"][l] for l in range(LAYERS)], axis=1)).reshape(3, KT, ADA_STEP, KT, P, P)

    def branch(b, y):
        out = []
        for m in range(KT):
            for j, v in enumerate((gates[b], y)):
                v = _blocks(v[:, m * P:(m + 1) * P])
                half = v.shape[0] // 2
                out += [v[:half], ada[b, m, 2 * j], v[half:], ada[b, m, 2 * j + 1]]
        return np.concatenate(out)

    out = [_blocks(w[:, 0:1024]), _side_by_side(w[:, 1024:1536]), _side_by_side(w[:, 1536:2048]),
           _blocks(w[:, 2048:3072]), branch(0, a["w_ret_o"][0]), _blocks(w[:, 3072:4608]),
           branch(1, a["w_na_o"][0]), _blocks(kvw[:, 0:512]), _side_by_side(kvw[:, 512:1024]),
           _blocks(w[:, 4608:5120]), branch(2, a["w_xa_o"][0]), _blocks(a["w_out"][0])]
    for g in range(GROUPS):
        gate, up, down = (a[f"w_exp_{n}"][0, g] for n in ("gate", "up", "down"))
        for e in range(IN_GROUP):
            out += [_side_by_side(gate[e]), _side_by_side(up[e])]
            if 1 <= e < IN_GROUP - 1:
                out.append(_side_by_side(down[e - 1]))
        out += [_side_by_side(down[IN_GROUP - 2]), _side_by_side(down[IN_GROUP - 1])]
    for l in range(LAYERS):
        v = a["w_in_2"][l]
        k_pe = np.zeros((D, P), v.dtype)
        k_pe[:, 64:96] = v[:, 384:416]
        gq = v[:, 1184:1696].reshape(D, 2, 4, 64).transpose(0, 2, 1, 3).reshape(D, 512)
        out += [_blocks(np.concatenate([v[:, 0:256], v[:, 416:672], gq, v[:, 256:384], k_pe, v[:, 672:928],
                                        v[:, 1696:1824]], axis=1)),
                _side_by_side(v[:, 928:1184]), _side_by_side(v[:, 1824:1952]), _blocks(a["w_out_2"][l]),
                ]
        for t in range(0, HT, PART):
            part = slice(t * P, min(t + PART, HT) * P)
            out += [_interleaved(a["w_ffn_gate_2"][l][:, part], a["w_ffn_up_2"][l][:, part]),
                    _blocks(a["w_ffn_down_2"][l][part])]
    out = np.concatenate(out)
    n = out.shape[0] // BLOCKS
    return np.ascontiguousarray(out.reshape(n, BLOCKS, P, P).transpose(0, 2, 1, 3).reshape(n, P, CHUNK))


def _columns(v):
    return v.reshape(-1, P).T


def _params(a):
    lay, n = param_layout()
    out = np.zeros((P, n), np.float32)

    def put(name, v):
        first, w = lay[name]
        out[:v.shape[0], first:first + w] = v

    put("g_mix", _columns(a["g_mix"][0]))
    put("ret_gain", _columns(a["ret_norm_gain"][0]))
    put("g_mem", _columns(a["g_mem"][0]))
    put("g_ffn", _columns(a["g_ffn"][0]))
    put("g_final", _columns(a["g_final"]))
    put("decay", np.broadcast_to(np.concatenate([a["ret_decay_fwd"][0], a["ret_decay_bwd"][0]]), (P, 8)))
    put("router_bias", np.broadcast_to(np.tile(np.concatenate([a["b_router_group"][0], a["b_router_expert"][0]]), 4),
                                       (P, 80)))
    put("c", np.stack([_columns(a["c_2"][0]), _columns(a["c_ctx_2"])], axis=2).reshape(P, 16))
    put("b_ada", np.repeat(_columns(a["b_ada_2"].reshape(-1)), 2, axis=1))
    for l in range(LAYERS):
        for name, source in (("attn_pre", "g_attn_pre_2"), ("attn_post", "g_attn_post_2"), ("mla_q", "g_mla_q_2"),
                             ("mla_kv", "g_mla_kv_2"), ("ffn_pre", "g_ffn_pre_2"), ("ffn_post", "g_ffn_post_2")):
            put(f"{name}{l}", _columns(a[source][l]))
        for name, source in (("diff_sub", "g_diff_sub_2"), ("gqa_q", "g_gqa_q_2"), ("gqa_k", "g_gqa_k_2")):
            put(f"{name}{l}", _columns(np.tile(a[source][l], 2)))
        put(f"lambda{l}", np.stack([a[f"lambda_{n}_2"][l] for n in ("q1", "k1", "q2", "k2")], axis=1))
    return out


def _rotation(half):
    out = np.zeros((P, P), np.float32)
    for m in range(P):
        first = m % (2 * half) < half
        out[m + half if first else m - half, m] = -1.0 if first else 1.0
    return out


def _constants():
    f = np.float32
    lay, n = const_layout()
    con = np.zeros((P, n), f)

    def put(name, v):
        first, w = lay[name]
        con[:, first:first + w] = v

    put("ident", np.eye(P))
    put("ones", 1.0)
    put("ones64", np.kron(np.eye(2), np.ones((64, 64))))
    for half in (64, 32, 16):
        put(f"rot{2 * half}", _rotation(half))
    mask = np.zeros((P, 3, 256), f)
    for kind, (t, start) in enumerate(((0, 0), (1, 8), (3, 32))):
        q = 16 * t + np.arange(P) // 8
        off = (start + np.arange(256) // GRID_H)[None, :] - np.clip(q - 8, 0, 48)[:, None]
        mask[:, kind] = np.where((off >= 0) & (off < 16), 0.0, -BIG)
    put("mask", mask.reshape(P, -1))
    put("rank", np.tile([4.0, 3.0, 2.0, 1.0], 4))
    put("before", np.triu(np.ones((P, P)), 1))
    put("steps", np.tile(np.arange(4.0) * P, 4))
    put("unit_no", np.repeat(np.arange(UNITS), 4))
    put("slot_no", np.arange(P)[:, None] + P * np.arange(UNITS)[None, :])
    delta = np.arange(DIFFS)[None, :] - 3 * P - np.arange(P)[:, None]
    dist = np.stack([np.maximum(delta, 0), np.maximum(-delta, 0)], axis=1).astype(f)

    def trig(ang):
        return [np.cos(ang).T.astype(f), np.sin(ang).T.astype(f)]

    s = np.arange(SEQ, dtype=f)
    inv = (f(10000.0) ** (-np.arange(64, dtype=f) / f(64))).astype(f)
    trig128 = np.stack(trig((s[:, None] * inv[None, :])[:, np.arange(P) % 64]), axis=1)
    both = []
    for quarter in (16, 8):
        inv = (f(10000.0) ** (-np.arange(quarter, dtype=f) / f(quarter))).astype(f)
        row, col = np.floor(s / GRID_W).astype(f), (s % GRID_W).astype(f)
        ang = np.concatenate([row[:, None] * inv, col[:, None] * inv], axis=1)
        both += trig(ang[:, np.arange(P) % (2 * quarter)])
    return {"con": con, "slot_row": np.tile(np.arange(SLOTS, dtype=f), (P, 1)), "dist": dist, "trig128": trig128, "trig": np.stack(both, axis=1)}


def _near_bias(rpb):
    flat = np.pad(rpb.reshape(-1), (16, 32))
    q = np.arange(P)
    first = 16 + (7 - q % 8) * 31 - q // 8 - 1
    at = first[:, None, None] + 465 * np.arange(NA_HEADS)[None, :, None] + np.arange(RPB_RUN)[None, None, :]
    return flat[at]


def _feature_major(v):
    return np.ascontiguousarray(v.reshape(-1, KT, P).transpose(2, 1, 0))


def kernel(**inputs):
    import concourse.bacc as bacc
    from concourse.bass_utils import run_bass_kernel_spmd

    a = {k: np.asarray(v) for k, v in inputs.items()}
    small = [np.concatenate([a["w_mla_qb_2"][l].reshape(2, P, 384).transpose(1, 0, 2).reshape(P, 768),
                             a["w_mla_kvb_2"][l]], axis=1) for l in range(LAYERS)]
    arrays = {"stream": _stream(a), "xT": _feature_major(a["x"][0]), "memT": _feature_major(a["mem"][0]),
              "ctxT": _feature_major(a["ctx_2"][0]), "par": _params(a), "rpb": _near_bias(a["na_rpb"][0]),
              "w_router": np.concatenate([a["w_router_group"][0], a["w_router_expert"][0]], axis=1)
              .reshape(KT, P, 20).transpose(1, 0, 2), "w_small": np.stack(small), **_constants()}
    arrays = {k: np.ascontiguousarray(v) for k, v in arrays.items()}

    def build(known):
        nc = bacc.Bacc("TRN2", target_bir_lowering=False, num_devices=1)
        ins = {n: nc.dram_tensor(f"in_{n}", v.shape, mybir.dt.from_np(v.dtype), kind="ExternalInput").ap()
               for n, v in arrays.items()}
        out = nc.dram_tensor("out_0", (P, KT, SEQ), F32, kind="ExternalOutput").ap()
        return nc, program(nc, ins, out, known)

    _, counted = build({})
    nc, again = build(counted)
    assert again == counted or all(again[k] == counted[k] for k in counted if k != "ends")
    r = run_bass_kernel_spmd(nc, [{f"in_{n}": v for n, v in arrays.items()}], core_ids=[0])
    y = r.results[0]["out_0"]
    return np.ascontiguousarray(y.transpose(2, 1, 0)).reshape(1, SEQ, D)
```
